# Optimizing a Trainium2 kernel written in Bass

```python
import math
import jax, jax.numpy as jnp
from jax import lax
import numpy as np
import jax
import jax.numpy as jnp

D_MODEL = 1024
BATCH = 1
SEQ = 512
DEPTH = 1

MEM_LEN = 256
SSD_HEADS = 16
SSD_HEAD_DIM = 64
SSD_INNER = SSD_HEADS * SSD_HEAD_DIM
SSD_GROUPS = 2
SSD_HEADS_PER_GROUP = SSD_HEADS // SSD_GROUPS
SSD_STATE = 128
SSD_CONV = 4
SSD_CONV_DIM = SSD_INNER + 2 * SSD_GROUPS * SSD_STATE
SSD_CHUNK = 128
RET_HEADS = 8
RET_QK_DIM = 64
RET_V_DIM = 128
RET_QK = RET_HEADS * RET_QK_DIM
RET_INNER = RET_HEADS * RET_V_DIM
RET_CHUNK = 128
ROPE_BASE = 10000.0
MIX_WIDTH = SSD_INNER + RET_INNER
IN_SIZES = (SSD_INNER, SSD_CONV_DIM, SSD_HEADS, RET_QK, RET_QK, RET_INNER, RET_INNER)
IN_COLS = SSD_INNER + SSD_CONV_DIM + SSD_HEADS + 2 * RET_QK + 2 * RET_INNER
XATTN_HEADS = 4
XATTN_HEAD_DIM = D_MODEL // XATTN_HEADS
D_FF = 2752
FFN_CONV = 3
ALPHA = (2.0 * DEPTH) ** 0.25
BETA = (8.0 * DEPTH) ** -0.25
EPS = 1e-5


def _layer_norm(x, g, b):
    xf = x.astype(jnp.float32)
    mu = jnp.mean(xf, axis=-1, keepdims=True)
    var = jnp.mean(jnp.square(xf - mu), axis=-1, keepdims=True)
    return ((xf - mu) * lax.rsqrt(var + EPS) * g.astype(jnp.float32) + b.astype(jnp.float32)).astype(x.dtype)

def _split_cols(u, sizes):
    offs, acc = [], 0
    for s in sizes[:-1]:
        acc += s
        offs.append(acc)
    return jnp.split(u, offs, axis=-1)

def _causal_dwconv(u, w, b):
    k, ch = w.shape
    y = lax.conv_general_dilated(
        u, w[:, None, :].astype(u.dtype), window_strides=(1,), padding=[(k - 1, 0)],
        dimension_numbers=("NWC", "WIO", "NWC"), feature_group_count=ch)
    return y + b.astype(u.dtype)

def _ssd_chunked(xh, dt, a_head, b_in, c_in):
    bsz, seqlen, ng, nr, hp = xh.shape
    ns = b_in.shape[-1]
    q = SSD_CHUNK
    nc = seqlen // q
    f32 = jnp.float32
    xdt = (xh.astype(f32) * dt[..., None]).reshape(bsz, nc, q, ng, nr, hp)
    a = jnp.moveaxis((dt * a_head).reshape(bsz, nc, q, ng, nr), 2, -1)
    a_cs = jnp.cumsum(a, axis=-1)
    bc = b_in.astype(f32).reshape(bsz, nc, q, ng, ns)
    cc = c_in.astype(f32).reshape(bsz, nc, q, ng, ns)
    causal = jnp.tril(jnp.ones((q, q), dtype=bool))
    seg = jnp.exp(jnp.where(causal, a_cs[..., :, None] - a_cs[..., None, :], -jnp.inf))
    cb = jnp.einsum("bclgn,bcsgn->bcgls", cc, bc)
    att = cb[:, :, :, None] * seg
    y_diag = jnp.einsum("bcgrls,bcsgrp->bclgrp", att, xdt)
    decay_to_end = jnp.moveaxis(jnp.exp(a_cs[..., -1:] - a_cs), -1, 2)
    states = jnp.einsum("bcsgn,bcsgrp->bcgrpn", bc, xdt * decay_to_end[..., None])
    chunk_decay = jnp.exp(a_cs[..., -1])

    def step(h, inp):
        st, dec = inp
        return h * dec[..., None, None] + st, h

    h0 = jnp.zeros((bsz, ng, nr, hp, ns), f32)
    _, h_prev = lax.scan(step, h0, (jnp.moveaxis(states, 1, 0), jnp.moveaxis(chunk_decay, 1, 0)))
    h_prev = jnp.moveaxis(h_prev, 0, 1)
    decay_from_start = jnp.moveaxis(jnp.exp(a_cs), -1, 2)
    y_off = jnp.einsum("bclgn,bcgrpn->bclgrp", cc, h_prev) * decay_from_start[..., None]
    return (y_diag + y_off).reshape(bsz, seqlen, ng, nr, hp)

def _rotary(u, cos, sin):
    u = u.astype(jnp.float32)
    u1, u2 = jnp.split(u, 2, axis=-1)
    c = cos[None, :, None, :]
    s = sin[None, :, None, :]
    return jnp.concatenate([u1 * c - u2 * s, u1 * s + u2 * c], axis=-1)

def _retention_chunkwise(q, k, v, log_gamma):
    bsz, seqlen, nh, dk = q.shape
    dv = v.shape[-1]
    n = RET_CHUNK
    nc = seqlen // n
    f32 = jnp.float32
    qc = q.reshape(bsz, nc, n, nh, dk)
    kc = k.reshape(bsz, nc, n, nh, dk)
    vc = v.astype(f32).reshape(bsz, nc, n, nh, dv)
    pos = jnp.arange(n, dtype=f32)
    dist = pos[:, None] - pos[None, :]
    decay = jnp.exp(jnp.where(dist >= 0, dist * log_gamma[:, None, None], -jnp.inf))
    s = jnp.einsum("bcnhd,bcmhd->bchnm", qc, kc) * decay
    y_in = jnp.einsum("bchnm,bcmhe->bcnhe", s, vc)
    k_dec = jnp.exp((n - 1 - pos)[:, None] * log_gamma)
    states = jnp.einsum("bcmhd,bcmhe->bchde", kc * k_dec[:, :, None], vc)
    chunk_decay = jnp.exp(n * log_gamma)

    def step(r, st):
        return r * chunk_decay[:, None, None] + st, r

    r0 = jnp.zeros((bsz, nh, dk, dv), f32)
    _, r_prev = lax.scan(step, r0, jnp.moveaxis(states, 1, 0))
    r_prev = jnp.moveaxis(r_prev, 0, 1)
    q_dec = jnp.exp((pos + 1.0)[:, None] * log_gamma)
    y_cross = jnp.einsum("bcnhd,bchde->bcnhe", qc * q_dec[:, :, None], r_prev)
    return (y_in + y_cross).reshape(bsz, seqlen, nh, dv)

def _mixer(x, w_in, conv_w, conv_b, dt_bias, a_log, d_skip, norm_w, gn_w, gn_b, w_out, cos, sin):
    f32 = jnp.float32
    bsz, seqlen, _ = x.shape
    proj = x @ w_in
    z, xbc, dt_raw, q, k, v, g = _split_cols(proj, IN_SIZES)
    xbc = jax.nn.silu(_causal_dwconv(xbc, conv_w, conv_b))
    xs, b_in, c_in = _split_cols(xbc, (SSD_INNER, SSD_GROUPS * SSD_STATE, SSD_GROUPS * SSD_STATE))
    dt = jax.nn.softplus(dt_raw.astype(f32) + dt_bias.astype(f32))
    a_head = -jnp.exp(a_log.astype(f32))
    xh = xs.reshape(bsz, seqlen, SSD_GROUPS, SSD_HEADS_PER_GROUP, SSD_HEAD_DIM)
    y = _ssd_chunked(
        xh, dt.reshape(bsz, seqlen, SSD_GROUPS, SSD_HEADS_PER_GROUP),
        a_head.reshape(SSD_GROUPS, SSD_HEADS_PER_GROUP),
        b_in.reshape(bsz, seqlen, SSD_GROUPS, SSD_STATE),
        c_in.reshape(bsz, seqlen, SSD_GROUPS, SSD_STATE))
    y = y + d_skip.astype(f32).reshape(SSD_GROUPS, SSD_HEADS_PER_GROUP)[:, :, None] * xh.astype(f32)
    u = (y.reshape(bsz, seqlen, SSD_INNER) * jax.nn.silu(z.astype(f32))).reshape(bsz, seqlen, SSD_GROUPS, -1)
    u = u * lax.rsqrt(jnp.mean(jnp.square(u), axis=-1, keepdims=True) + EPS)
    y_ssd = u.reshape(bsz, seqlen, SSD_INNER) * norm_w.astype(f32)
    log_gamma = jnp.log1p(-jnp.exp2(-5.0 - jnp.arange(RET_HEADS, dtype=f32)))
    qh = _rotary(q.reshape(bsz, seqlen, RET_HEADS, RET_QK_DIM), cos, sin)
    kh = _rotary(k.reshape(bsz, seqlen, RET_HEADS, RET_QK_DIM), cos, sin) * (RET_QK_DIM ** -0.5)
    yr = _retention_chunkwise(qh, kh, v.reshape(bsz, seqlen, RET_HEADS, RET_V_DIM), log_gamma)
    mu = jnp.mean(yr, axis=-1, keepdims=True)
    var = jnp.mean(jnp.square(yr - mu), axis=-1, keepdims=True)
    yr = ((yr - mu) * lax.rsqrt(var + EPS)).reshape(bsz, seqlen, RET_INNER)
    yr = yr * gn_w.astype(f32) + gn_b.astype(f32)
    y_ret = jax.nn.silu(g.astype(f32)) * yr
    y_mix = jnp.concatenate([y_ssd, y_ret], axis=-1).astype(x.dtype)
    return y_mix @ w_out

def _memory_cross_attention(x, mem, w_q, w_k, w_v, w_o):
    bsz, seqlen, _ = x.shape
    m = mem.shape[1]
    qx = (x @ w_q).reshape(bsz, seqlen, XATTN_HEADS, XATTN_HEAD_DIM)
    km = (mem @ w_k).reshape(bsz, m, XATTN_HEADS, XATTN_HEAD_DIM)
    vm = (mem @ w_v).reshape(bsz, m, XATTN_HEADS, XATTN_HEAD_DIM)
    s = jnp.einsum("blhd,bmhd->bhlm", qx, km).astype(jnp.float32) * (XATTN_HEAD_DIM ** -0.5)
    p = jax.nn.softmax(s, axis=-1).astype(vm.dtype)
    o = jnp.einsum("bhlm,bmhd->blhd", p, vm).reshape(bsz, seqlen, D_MODEL)
    return o @ w_o

def _conv_glu_ffn(x, w_up, b_up, conv_w, conv_b, w_down):
    h = x @ w_up + b_up
    h = _causal_dwconv(h, conv_w, conv_b)
    a, u = jnp.split(h, 2, axis=-1)
    return (jax.nn.silu(a) * u) @ w_down

def first_inputs(seed: int = 0) -> dict:
    key = jax.random.key(seed)
    ks = jax.random.split(key, 32)
    f32 = jnp.float32

    def nrm(k, shape, scale):
        return jax.random.normal(k, shape, f32) * scale

    nl = DEPTH
    dt0 = jnp.exp(jax.random.uniform(ks[5], (nl, SSD_HEADS), f32, math.log(1e-3), math.log(1e-1)))
    return {
        "x": nrm(ks[0], (BATCH, SEQ, D_MODEL), 1.0),
        "mem": nrm(ks[1], (BATCH, MEM_LEN, D_MODEL), 1.0),
        "w_in": nrm(ks[2], (nl, D_MODEL, IN_COLS), D_MODEL ** -0.5),
        "ssd_conv_w": nrm(ks[3], (nl, SSD_CONV, SSD_CONV_DIM), SSD_CONV ** -0.5),
        "ssd_conv_b": nrm(ks[4], (nl, SSD_CONV_DIM), 0.02),
        "ssd_dt_bias": dt0 + jnp.log(-jnp.expm1(-dt0)),
        "ssd_a_log": jnp.log(jax.random.uniform(ks[6], (nl, SSD_HEADS), f32, 1.0, 16.0)),
        "ssd_d": 1.0 + nrm(ks[7], (nl, SSD_HEADS), 0.02),
        "ssd_norm_w": 1.0 + nrm(ks[8], (nl, SSD_INNER), 0.02),
        "ret_gn_w": 1.0 + nrm(ks[9], (nl, RET_INNER), 0.02),
        "ret_gn_b": nrm(ks[10], (nl, RET_INNER), 0.02),
        "w_mix_out": nrm(ks[11], (nl, MIX_WIDTH, D_MODEL), BETA * MIX_WIDTH ** -0.5),
        "ln1_g": 1.0 + nrm(ks[12], (nl, D_MODEL), 0.02),
        "ln1_b": nrm(ks[13], (nl, D_MODEL), 0.02),
        "w_xq": nrm(ks[14], (nl, D_MODEL, D_MODEL), D_MODEL ** -0.5),
        "w_xk": nrm(ks[15], (nl, D_MODEL, D_MODEL), D_MODEL ** -0.5),
        "w_xv": nrm(ks[16], (nl, D_MODEL, D_MODEL), D_MODEL ** -0.5),
        "w_xo": nrm(ks[17], (nl, D_MODEL, D_MODEL), BETA * D_MODEL ** -0.5),
        "ln2_g": 1.0 + nrm(ks[18], (nl, D_MODEL), 0.02),
        "ln2_b": nrm(ks[19], (nl, D_MODEL), 0.02),
        "w_ffn_up": nrm(ks[20], (nl, D_MODEL, 2 * D_FF), D_MODEL ** -0.5),
        "b_ffn_up": nrm(ks[21], (nl, 2 * D_FF), 0.02),
        "ffn_conv_w": nrm(ks[22], (nl, FFN_CONV, 2 * D_FF), FFN_CONV ** -0.5),
        "ffn_conv_b": nrm(ks[23], (nl, 2 * D_FF), 0.02),
        "w_ffn_down": nrm(ks[24], (nl, D_FF, D_MODEL), BETA * D_FF ** -0.5),
        "ln3_g": 1.0 + nrm(ks[25], (nl, D_MODEL), 0.02),
        "ln3_b": nrm(ks[26], (nl, D_MODEL), 0.02),
    }

def first_block(x, mem, w_in, ssd_conv_w, ssd_conv_b, ssd_dt_bias, ssd_a_log, ssd_d, ssd_norm_w,
              ret_gn_w, ret_gn_b, w_mix_out, ln1_g, ln1_b, w_xq, w_xk, w_xv, w_xo, ln2_g, ln2_b,
              w_ffn_up, b_ffn_up, ffn_conv_w, ffn_conv_b, w_ffn_down, ln3_g, ln3_b):
    seqlen = x.shape[1]
    pos = jnp.arange(seqlen, dtype=jnp.float32)
    freqs = 1.0 / (ROPE_BASE ** jnp.linspace(0.0, 1.0, RET_QK_DIM // 2, dtype=jnp.float32))
    ang = pos[:, None] * freqs[None, :]
    cos, sin = jnp.cos(ang), jnp.sin(ang)
    for l in range(DEPTH):
        mix = _mixer(x, w_in[l], ssd_conv_w[l], ssd_conv_b[l], ssd_dt_bias[l], ssd_a_log[l], ssd_d[l],
                     ssd_norm_w[l], ret_gn_w[l], ret_gn_b[l], w_mix_out[l], cos, sin)
        x = _layer_norm(ALPHA * x + mix, ln1_g[l], ln1_b[l])
        xa = _memory_cross_attention(x, mem, w_xq[l], w_xk[l], w_xv[l], w_xo[l])
        x = _layer_norm(ALPHA * x + xa, ln2_g[l], ln2_b[l])
        ff = _conv_glu_ffn(x, w_ffn_up[l], b_ffn_up[l], ffn_conv_w[l], ffn_conv_b[l], w_ffn_down[l])
        x = _layer_norm(ALPHA * x + ff, ln3_g[l], ln3_b[l])
    return x


_first_inputs = first_inputs


def first_inputs(seed=0):
    import zlib

    import numpy as np

    out = dict(_first_inputs(seed))
    spreads = {}
    factors = {'ssd_conv_b': 6.16,
     'ssd_d': 8.0,
     'ssd_norm_w': 8.0,
     'ret_gn_w': 8.0,
     'ret_gn_b': 8.0,
     'ln1_g': 2.777,
     'ln2_g': 2.793,
     'ln2_b': 2.718,
     'b_ffn_up': 7.057,
     'ffn_conv_b': 6.825,
     'ln3_g': 2.8,
     'ln3_b': 2.803}
    for name, (base, spread) in spreads.items():
        noise = np.random.default_rng([zlib.crc32(name.encode()), seed]).standard_normal(out[name].shape)
        drawn = base * np.exp(spread * noise) if base else spread * noise
        out[name] = __import__('jax').numpy.asarray(drawn.astype(out[name].dtype))
    for name, factor in factors.items():
        out[name] = (out[name] * factor).astype(out[name].dtype)
    return out


_narrow_inputs = first_inputs


def first_inputs(seed=0):

    out = dict(_narrow_inputs(seed))
    wider = {'ssd_d': 3.89,
     'ssd_norm_w': 3.48,
     'ret_gn_w': 5.31,
     'ret_gn_b': 5.45,
     'ln1_b': 6.86,
     'ln3_g': 3.15,
     'ln3_b': 3.15}
    for name, times in wider.items():
        mean = out[name].mean()
        out[name] = (mean + times * (out[name] - mean)).astype(out[name].dtype)
    return out


D_CONV = D_MODEL
CONV_GROUPS = 8
CONV_WIDTH = 3
D_RNN = (5 * D_MODEL) // 4
RNN_BLOCKS = 10
RNN_BLOCK = D_RNN // RNN_BLOCKS
RNN_CONV_WIDTH = 4
LRU_C = 8.0
W_IN_COLS = 3 * D_CONV + 2 * D_RNN + 2 * D_MODEL
SPLITS = (D_CONV, 2 * D_CONV, 3 * D_CONV, 3 * D_CONV + D_RNN,
          3 * D_CONV + 2 * D_RNN, 3 * D_CONV + 2 * D_RNN + D_MODEL)
PEER_HEADS = 8
PEER_NKEYS = 128
PEER_NEXPERTS = PEER_NKEYS * PEER_NKEYS
PEER_QDIM = 256
PEER_HALF = PEER_QDIM // 2
PEER_TOPK = 16
PEER_CHUNK = 128
EPS_2 = 1e-6


def rms_norm(x, g):
    xf = x.astype(jnp.float32)
    y = xf * lax.rsqrt(jnp.mean(xf * xf, axis=-1, keepdims=True) + EPS_2)
    return (y * g.astype(jnp.float32)).astype(x.dtype)

def causal_depthwise_conv(x, w):
    k = w.shape[0]
    s = x.shape[1]
    xp = jnp.pad(x, ((0, 0), (k - 1, 0), (0, 0)))
    out = xp[:, 0:s] * w[0]
    for j in range(1, k):
        out = out + xp[:, j:j + s] * w[j]
    return out

def block_diag_linear(x, w, b):
    bsz, s, _ = x.shape
    xb = x.reshape(bsz, s, RNN_BLOCKS, RNN_BLOCK)
    return jnp.einsum('bsni,nij->bsnj', xb, w).reshape(bsz, s, D_RNN) + b

def rg_lru(x, w_rg, b_rg, w_ig, b_ig, lam):
    r = jax.nn.sigmoid(block_diag_linear(x, w_rg, b_rg).astype(jnp.float32))
    i = jax.nn.sigmoid(block_diag_linear(x, w_ig, b_ig).astype(jnp.float32))
    log_a = -LRU_C * r * jax.nn.softplus(-lam.astype(jnp.float32))
    a = jnp.exp(log_a)
    mult = jnp.sqrt(jnp.maximum(-jnp.expm1(2.0 * log_a), 0.0))
    b = mult * i * x.astype(jnp.float32)

    def combine(c1, c2):
        a1, b1 = c1
        a2, b2 = c2
        return a1 * a2, a2 * b1 + b2

    _, h = lax.associative_scan(combine, (a, b), axis=1)
    return h.astype(x.dtype)

def hybrid_mixer(n, w_in, conv_a_w, w_out_a, rnn_conv_w, rnn_conv_b,
                 w_rg, b_rg, w_ig, b_ig, lru_lambda, w_out_b, w_o):
    proj = n @ w_in
    a_x, a_b, a_c, r_x, r_y, g_a, g_b = jnp.split(proj, SPLITS, axis=-1)
    y_a = (a_b * causal_depthwise_conv(a_c * a_x, conv_a_w)) @ w_out_a
    r_c = causal_depthwise_conv(r_x, rnn_conv_w) + rnn_conv_b
    r_h = rg_lru(r_c, w_rg, b_rg, w_ig, b_ig, lru_lambda)
    y_b = (jax.nn.gelu(r_y, approximate=True) * r_h) @ w_out_b
    merged = jax.nn.sigmoid(g_a) * y_a + jax.nn.sigmoid(g_b) * y_b
    return merged @ w_o

def peer(n, w_q, sub_keys_1, sub_keys_2, expert_u, expert_v):
    bsz, s, d = n.shape
    xt = n.reshape(-1, PEER_CHUNK, d)

    def chunk(xc):
        q = (xc @ w_q).reshape(PEER_CHUNK, PEER_HEADS, 2, PEER_HALF)
        s1 = jnp.einsum('thd,hnd->thn', q[:, :, 0], sub_keys_1).astype(jnp.float32)
        s2 = jnp.einsum('thd,hnd->thn', q[:, :, 1], sub_keys_2).astype(jnp.float32)
        v1, i1 = lax.top_k(s1, PEER_TOPK)
        v2, i2 = lax.top_k(s2, PEER_TOPK)
        cand_s = (v1[..., :, None] + v2[..., None, :]).reshape(PEER_CHUNK, PEER_HEADS, PEER_TOPK * PEER_TOPK)
        cand_i = (i1[..., :, None] * PEER_NKEYS + i2[..., None, :]).reshape(PEER_CHUNK, PEER_HEADS, PEER_TOPK * PEER_TOPK)
        top_s, pos = lax.top_k(cand_s, PEER_TOPK)
        idx = jnp.take_along_axis(cand_i, pos, axis=-1)
        g = jax.nn.softmax(top_s, axis=-1)
        u_sel = jnp.take(expert_u, idx, axis=0)
        act = jax.nn.gelu(jnp.einsum('thkd,td->thk', u_sel, xc).astype(jnp.float32))
        v_sel = jnp.take(expert_v, idx, axis=0)
        return jnp.einsum('thk,thkd->td', (g * act).astype(xc.dtype), v_sel)

    return lax.map(chunk, xt).reshape(bsz, s, d)

def second_inputs(seed: int = 0) -> dict:
    key = jax.random.key(seed)
    ks = jax.random.split(key, 24)
    f = jnp.float32
    L = DEPTH

    def nrm(k, shape, scale):
        return jax.random.normal(k, shape, f) * scale

    u = jax.random.uniform(ks[10], (L, D_RNN), f, 0.9, 0.999)
    a0 = u ** (1.0 / LRU_C)
    lru_lambda = jnp.log(a0) - jnp.log1p(-a0)
    return {
        "x": nrm(ks[0], (BATCH, SEQ, D_MODEL), 1.0),
        "norm_mix": 1.0 + nrm(ks[1], (L, D_MODEL), 0.01),
        "w_in": nrm(ks[2], (L, D_MODEL, W_IN_COLS), D_MODEL ** -0.5),
        "conv_a_w": nrm(ks[3], (L, CONV_WIDTH, D_CONV), CONV_WIDTH ** -0.5),
        "w_out_a": nrm(ks[4], (L, D_CONV, D_MODEL), D_CONV ** -0.5),
        "rnn_conv_w": nrm(ks[5], (L, RNN_CONV_WIDTH, D_RNN), RNN_CONV_WIDTH ** -0.5),
        "rnn_conv_b": nrm(ks[6], (L, D_RNN), 0.01),
        "w_rg": nrm(ks[7], (L, RNN_BLOCKS, RNN_BLOCK, RNN_BLOCK), RNN_BLOCK ** -0.5),
        "b_rg": nrm(ks[8], (L, D_RNN), 0.01),
        "w_ig": nrm(ks[9], (L, RNN_BLOCKS, RNN_BLOCK, RNN_BLOCK), RNN_BLOCK ** -0.5),
        "b_ig": nrm(ks[11], (L, D_RNN), 0.01),
        "lru_lambda": lru_lambda,
        "w_out_b": nrm(ks[12], (L, D_RNN, D_MODEL), D_RNN ** -0.5),
        "w_o": nrm(ks[13], (L, D_MODEL, D_MODEL), D_MODEL ** -0.5),
        "norm_ffn": 1.0 + nrm(ks[14], (L, D_MODEL), 0.01),
        "w_q": nrm(ks[15], (L, D_MODEL, PEER_HEADS * PEER_QDIM), D_MODEL ** -0.5),
        "sub_keys_1": nrm(ks[16], (L, PEER_HEADS, PEER_NKEYS, PEER_HALF), PEER_HALF ** -0.5),
        "sub_keys_2": nrm(ks[17], (L, PEER_HEADS, PEER_NKEYS, PEER_HALF), PEER_HALF ** -0.5),
        "expert_u": nrm(ks[18], (L, PEER_NEXPERTS, D_MODEL), D_MODEL ** -0.5),
        "expert_v": nrm(ks[19], (L, PEER_NEXPERTS, D_MODEL), PEER_HEADS ** -0.5),
        "norm_final": 1.0 + nrm(ks[20], (D_MODEL,), 0.01),
    }

def second_block(x, norm_mix, w_in, conv_a_w, w_out_a, rnn_conv_w, rnn_conv_b,
              w_rg, b_rg, w_ig, b_ig, lru_lambda, w_out_b, w_o, norm_ffn,
              w_q, sub_keys_1, sub_keys_2, expert_u, expert_v, norm_final):
    h = x
    for l in range(DEPTH):
        n = rms_norm(h, norm_mix[l])
        h = h + hybrid_mixer(n, w_in[l], conv_a_w[l], w_out_a[l], rnn_conv_w[l],
                             rnn_conv_b[l], w_rg[l], b_rg[l], w_ig[l], b_ig[l],
                             lru_lambda[l], w_out_b[l], w_o[l])
        n = rms_norm(h, norm_ffn[l])
        h = h + peer(n, w_q[l], sub_keys_1[l], sub_keys_2[l], expert_u[l], expert_v[l])
    return rms_norm(h, norm_final)


_first_inputs_2 = second_inputs


def second_inputs(seed=0):
    import zlib

    import numpy as np

    out = dict(_first_inputs_2(seed))
    spreads = {}
    factors = {}
    for name, (base, spread) in spreads.items():
        noise = np.random.default_rng([zlib.crc32(name.encode()), seed]).standard_normal(out[name].shape)
        drawn = base * np.exp(spread * noise) if base else spread * noise
        out[name] = __import__('jax').numpy.asarray(drawn.astype(out[name].dtype))
    for name, factor in factors.items():
        out[name] = (out[name] * factor).astype(out[name].dtype)
    return out


_narrow_inputs_2 = second_inputs


def second_inputs(seed=0):

    out = dict(_narrow_inputs_2(seed))
    wider = {'norm_mix': 3.59, 'b_rg': 12.0, 'b_ig': 12.0, 'norm_ffn': 3.96, 'norm_final': 6.63}
    for name, times in wider.items():
        mean = out[name].mean()
        out[name] = (mean + times * (out[name] - mean)).astype(out[name].dtype)
    return out


GM_W = 512
GM_GROUPS = 4
GM_CHUNK = 128
ML_H = 4
ML_DH = 128
ML_W = ML_H * ML_DH
ML_CHUNK = 64
CONV_K = 4
NSA_H = 8
NSA_G = 2
NSA_R = NSA_H // NSA_G
NSA_DH = 64
NSA_W = NSA_H * NSA_DH
NSA_KV = NSA_G * NSA_DH
NSA_NB = 3
CMP_BLOCK = 32
CMP_STRIDE = 16
SEL_BLOCK = 64
TOP_N = 8
WINDOW = 512
NSA_QC = 32
N_BRANCH = 3
D_FF_3 = 4 * D_MODEL
EPS_3 = 1e-6
NEG = -1e30
BIG = 1e4
F32 = jnp.float32
SPLIT_SIZES = (GM_W, GM_W, ML_W, ML_W, ML_W, ML_W, ML_H, ML_H, NSA_W, NSA_KV, NSA_KV, NSA_KV, NSA_KV, NSA_KV, NSA_KV, NSA_H * NSA_NB, D_MODEL, D_MODEL, D_MODEL)
P_TOTAL = sum(SPLIT_SIZES)


def rms_norm_3(x, g):
    x32 = x.astype(F32)
    y = x32 * lax.rsqrt(jnp.mean(x32 * x32, axis=-1, keepdims=True) + EPS_3)
    return (y * g.astype(F32)).astype(x.dtype)

def layer_norm(x, g, b):
    x32 = x.astype(F32)
    mu = jnp.mean(x32, axis=-1, keepdims=True)
    var = jnp.mean(jnp.square(x32 - mu), axis=-1, keepdims=True)
    return ((x32 - mu) * lax.rsqrt(var + EPS_3) * g.astype(F32) + b.astype(F32)).astype(x.dtype)

def causal_conv(x, w, b):
    S = x.shape[1]
    xp = jnp.pad(x, ((0, 0), (CONV_K - 1, 0), (0, 0)))
    y = b
    for j in range(CONV_K):
        y = y + xp[:, j:j + S] * w[j]
    return y

def gmlp_mixer(u_pre, v_pre, ln_g, ln_b, ws, bs):
    B, S, _ = u_pre.shape
    u = jax.nn.gelu(u_pre)
    v = layer_norm(jax.nn.gelu(v_pre), ln_g, ln_b)
    dg = GM_W // GM_GROUPS
    v = v.reshape(B, S // GM_CHUNK, GM_CHUNK, GM_GROUPS, dg)
    w = ws * jnp.tril(jnp.ones((GM_CHUNK, GM_CHUNK), ws.dtype))
    mixed = jnp.einsum('gts,bcsgd->bctgd', w, v) + bs.T[:, :, None]
    return u * mixed.reshape(B, S, GM_W)

def mlstm_chunk_step(carry, xs):
    c_mat, n_vec, m_prev = carry
    q, k, v, ig, lf = xs
    L = q.shape[2]
    tril = jnp.tril(jnp.ones((L, L), dtype=bool))
    b = jnp.cumsum(lf, axis=-1)
    a = b + m_prev[..., None]
    d = jnp.where(tril, b[..., :, None] - b[..., None, :] + ig[..., None, :], -jnp.inf)
    m = jnp.maximum(a, jnp.max(d, axis=-1))
    w_inter = jnp.exp(a - m)
    s = jnp.einsum('bhtd,bhsd->bhts', q, k) * jnp.exp(d - m[..., None])
    num = jnp.einsum('bhts,bhse->bhte', s, v) + w_inter[..., None] * jnp.einsum('bhed,bhtd->bhte', c_mat, q)
    den = jnp.sum(s, axis=-1) + w_inter * jnp.einsum('bhd,bhtd->bht', n_vec, q)
    h = num / jnp.maximum(jnp.abs(den), jnp.exp(-m))[..., None]
    m_last = m[..., -1]
    w_prev = jnp.exp(a[..., -1] - m_last)
    w_s = jnp.exp(b[..., -1:] - b + ig - m_last[..., None])
    c_new = w_prev[..., None, None] * c_mat + jnp.einsum('bhs,bhse,bhsd->bhed', w_s, v, k)
    n_new = w_prev[..., None] * n_vec + jnp.einsum('bhs,bhsd->bhd', w_s, k)
    return (c_new, n_new, m_last), h

def mlstm_mixer(q, k, v, o_pre, i_pre, f_pre, conv_w, conv_b, gate_b, norm_g):
    B, S, _ = v.shape
    dtype = v.dtype
    qk = jax.nn.silu(causal_conv(jnp.concatenate([q, k], axis=-1), conv_w, conv_b))
    q, k = jnp.split(qk, 2, axis=-1)
    nc = S // ML_CHUNK

    def heads(t):
        return t.astype(F32).reshape(B, nc, ML_CHUNK, ML_H, ML_DH).transpose(1, 0, 3, 2, 4)

    def gate_heads(t):
        return t.reshape(B, nc, ML_CHUNK, ML_H).transpose(1, 0, 3, 2)

    qh = heads(q)
    kh = heads(k) * (ML_DH ** -0.5)
    vh = heads(v)
    ig = gate_heads((i_pre + gate_b[:ML_H]).astype(F32))
    lf = gate_heads(jax.nn.log_sigmoid((f_pre + gate_b[ML_H:]).astype(F32)))
    init = (jnp.zeros((B, ML_H, ML_DH, ML_DH), F32), jnp.zeros((B, ML_H, ML_DH), F32), jnp.zeros((B, ML_H), F32))
    _, h = lax.scan(mlstm_chunk_step, init, (qh, kh, vh, ig, lf))
    h = h.transpose(1, 0, 3, 2, 4).reshape(B, S, ML_H, ML_DH)
    mu = jnp.mean(h, axis=-1, keepdims=True)
    var = jnp.mean(jnp.square(h - mu), axis=-1, keepdims=True)
    hn = (h - mu) * lax.rsqrt(var + EPS_3) * norm_g.astype(F32).reshape(ML_H, ML_DH)
    return (jax.nn.sigmoid(o_pre.astype(F32)) * hn.reshape(B, S, ML_W)).astype(dtype)

def compress_blocks(kv, pe, w1, w2):
    B, S, G, dh = kv.shape
    n_cmp = (S - CMP_BLOCK) // CMP_STRIDE + 1
    idx = jnp.arange(n_cmp)[:, None] * CMP_STRIDE + jnp.arange(CMP_BLOCK)[None, :]
    blocks = kv[:, idx] + pe[:, None, :]
    blocks = blocks.transpose(0, 3, 1, 2, 4).reshape(B, G, n_cmp, CMP_BLOCK * dh)
    return jax.nn.gelu(blocks @ w1) @ w2

def masked_softmax(s, valid, axis=-1):
    p = jax.nn.softmax(jnp.where(valid, s, NEG), axis=axis)
    return jnp.where(valid, p, 0.0)

def nsa_mixer(q, kc, vc, ks, vs, kw, vw, gates, pe_k, pe_v, phi_k1, phi_k2, phi_v1, phi_v2):
    B, S, _ = q.shape
    dtype = q.dtype
    qh = q.reshape(B, S, NSA_G, NSA_R, NSA_DH).transpose(0, 2, 3, 1, 4)

    def kv_heads(t):
        return t.reshape(B, S, NSA_G, NSA_DH)

    k_cmp = compress_blocks(kv_heads(kc), pe_k, phi_k1, phi_k2)
    v_cmp = compress_blocks(kv_heads(vc), pe_v, phi_v1, phi_v2).astype(F32)
    n_cmp = k_cmp.shape[2]
    cmp_start = jnp.arange(n_cmp) * CMP_STRIDE
    cmp_end = cmp_start + CMP_BLOCK - 1
    cmp_center = cmp_start.astype(F32) + (CMP_BLOCK - 1) * 0.5
    n_sel = S // SEL_BLOCK
    top_n = min(TOP_N, n_sel)
    sel = jnp.arange(n_sel)
    overlap = ((cmp_start[:, None] <= sel[None, :] * SEL_BLOCK + SEL_BLOCK - 1) & (cmp_end[:, None] >= sel[None, :] * SEL_BLOCK)).astype(F32)
    k_sel = kv_heads(ks).transpose(0, 2, 1, 3).reshape(B, NSA_G, n_sel, SEL_BLOCK, NSA_DH)
    v_sel = kv_heads(vs).transpose(0, 2, 1, 3).reshape(B, NSA_G, n_sel, SEL_BLOCK, NSA_DH)
    pad = ((0, 0), (0, 0), (WINDOW, 0), (0, 0))
    k_win = jnp.pad(kv_heads(kw).transpose(0, 2, 1, 3), pad)
    v_win = jnp.pad(kv_heads(vw).transpose(0, 2, 1, 3), pad)
    g = jax.nn.sigmoid(gates.astype(F32)).reshape(B, S, NSA_G, NSA_R, NSA_NB).transpose(0, 2, 3, 1, 4)
    slopes = (2.0 ** (-8.0 * (jnp.arange(NSA_H, dtype=F32) + 1.0) / NSA_H)).reshape(NSA_G, NSA_R)
    scale = NSA_DH ** -0.5
    bi = jnp.arange(B)[:, None, None, None]
    gi = jnp.arange(NSA_G)[None, :, None, None]

    def query_chunk(qi):
        t0 = qi * NSA_QC
        qb = lax.dynamic_slice_in_dim(qh, t0, NSA_QC, axis=3)
        t = t0 + jnp.arange(NSA_QC)
        tf = t.astype(F32)
        sc = jnp.einsum('bgrqd,bgcd->bgrqc', qb, k_cmp).astype(F32) * scale - slopes[:, :, None, None] * (tf[:, None] - cmp_center[None, :])
        p_c = masked_softmax(sc, cmp_end[None, :] <= t[:, None])
        o_cmp = jnp.einsum('bgrqc,bgcd->bgrqd', p_c, v_cmp)
        imp = jnp.einsum('bgrqc,cj->bgqj', p_c, overlap)
        jt = (t // SEL_BLOCK)[:, None]
        forced = (sel == 0) | (sel == jt) | (sel == jt - 1)
        imp = jnp.where(sel > jt, NEG, jnp.where(forced, BIG, imp))
        _, idx = lax.top_k(imp, top_n)
        kg = k_sel[bi, gi, idx]
        vg = v_sel[bi, gi, idx].astype(F32)
        s_pos = idx[..., None] * SEL_BLOCK + jnp.arange(SEL_BLOCK)
        dist_s = (tf[:, None, None] - s_pos.astype(F32))[:, :, None]
        ss = jnp.einsum('bgrqd,bgqnld->bgrqnl', qb, kg).astype(F32) * scale - slopes[:, :, None, None, None] * dist_s
        p_s = masked_softmax(ss, (s_pos <= t[:, None, None])[:, :, None], axis=(-2, -1))
        o_sel = jnp.einsum('bgrqnl,bgqnld->bgrqd', p_s, vg)
        kwb = lax.dynamic_slice_in_dim(k_win, t0, WINDOW + NSA_QC, axis=2)
        vwb = lax.dynamic_slice_in_dim(v_win, t0, WINDOW + NSA_QC, axis=2).astype(F32)
        pos = t0 - WINDOW + jnp.arange(WINDOW + NSA_QC)
        sw = jnp.einsum('bgrqd,bgkd->bgrqk', qb, kwb).astype(F32) * scale - slopes[:, :, None, None] * (tf[:, None] - pos.astype(F32)[None, :])
        valid_w = (pos[None, :] >= 0) & (pos[None, :] <= t[:, None]) & (t[:, None] - pos[None, :] < WINDOW)
        o_win = jnp.einsum('bgrqk,bgkd->bgrqd', masked_softmax(sw, valid_w), vwb)
        gb = lax.dynamic_slice_in_dim(g, t0, NSA_QC, axis=3)
        return gb[..., 0:1] * o_cmp + gb[..., 1:2] * o_sel + gb[..., 2:3] * o_win

    out = lax.map(query_chunk, jnp.arange(S // NSA_QC))
    return out.transpose(1, 0, 4, 2, 3, 5).reshape(B, S, NSA_W).astype(dtype)

def hybrid_mixer_3(h, w_in, gm_ln_g, gm_ln_b, gm_ws, gm_bs, ml_conv_w, ml_conv_b, ml_gate_b, ml_norm_g,
                 nsa_pe_k, nsa_pe_v, nsa_phi_k1, nsa_phi_k2, nsa_phi_v1, nsa_phi_v2, w_up_a, w_up_b, w_up_c, w_out):
    z = h @ w_in
    (gu, gv, mq, mk, mv, mo, mi, mf, nq, nkc, nvc, nks, nvs, nkw, nvw, ngate, ga, gbr, gc) = jnp.split(
        z, np.cumsum(SPLIT_SIZES)[:-1].tolist(), axis=-1)
    y_a = gmlp_mixer(gu, gv, gm_ln_g, gm_ln_b, gm_ws, gm_bs) @ w_up_a
    y_b = mlstm_mixer(mq, mk, mv, mo, mi, mf, ml_conv_w, ml_conv_b, ml_gate_b, ml_norm_g) @ w_up_b
    y_c = nsa_mixer(nq, nkc, nvc, nks, nvs, nkw, nvw, ngate, nsa_pe_k, nsa_pe_v,
                    nsa_phi_k1, nsa_phi_k2, nsa_phi_v1, nsa_phi_v2) @ w_up_c
    merged = jax.nn.sigmoid(ga) * y_a + jax.nn.sigmoid(gbr) * y_b + jax.nn.sigmoid(gc) * y_c
    return merged @ w_out

def third_inputs(seed: int = 0) -> dict:
    key = jax.random.key(seed)
    ks = jax.random.split(key, 40)
    L = DEPTH

    def nrm(k, shape, scale):
        return scale * jax.random.normal(k, shape, F32)

    ml_gate_b = jnp.concatenate([nrm(ks[12], (L, ML_H), 0.1),
                                 jnp.linspace(3.0, 6.0, ML_H, dtype=F32)[None, :] + nrm(ks[13], (L, ML_H), 0.1)], axis=-1)
    return {
        'x': nrm(ks[0], (BATCH, SEQ, D_MODEL), 1.0),
        'c': nrm(ks[1], (BATCH, D_MODEL), 1.0),
        'g_norm1': 1.0 + nrm(ks[2], (L, D_MODEL), 0.02),
        'g_norm2': 1.0 + nrm(ks[3], (L, D_MODEL), 0.02),
        'w_ada': nrm(ks[4], (L, D_MODEL, 6 * D_MODEL), 0.3 * D_MODEL ** -0.5),
        'b_ada': nrm(ks[5], (L, 6 * D_MODEL), 0.02),
        'w_in': nrm(ks[6], (L, D_MODEL, P_TOTAL), D_MODEL ** -0.5),
        'gm_ln_g': 1.0 + nrm(ks[7], (L, GM_W), 0.02),
        'gm_ln_b': nrm(ks[8], (L, GM_W), 0.02),
        'gm_ws': nrm(ks[9], (L, GM_GROUPS, GM_CHUNK, GM_CHUNK), GM_CHUNK ** -0.5),
        'gm_bs': 1.0 + nrm(ks[10], (L, GM_GROUPS, GM_CHUNK), 0.1),
        'ml_conv_w': nrm(ks[11], (L, CONV_K, 2 * ML_W), CONV_K ** -0.5),
        'ml_conv_b': nrm(ks[14], (L, 2 * ML_W), 0.02),
        'ml_gate_b': ml_gate_b,
        'ml_norm_g': 1.0 + nrm(ks[15], (L, ML_W), 0.02),
        'nsa_pe_k': nrm(ks[16], (L, CMP_BLOCK, NSA_DH), 0.1),
        'nsa_pe_v': nrm(ks[17], (L, CMP_BLOCK, NSA_DH), 0.1),
        'nsa_phi_k1': nrm(ks[18], (L, CMP_BLOCK * NSA_DH, NSA_DH), (CMP_BLOCK * NSA_DH) ** -0.5),
        'nsa_phi_k2': nrm(ks[19], (L, NSA_DH, NSA_DH), NSA_DH ** -0.5),
        'nsa_phi_v1': nrm(ks[20], (L, CMP_BLOCK * NSA_DH, NSA_DH), (CMP_BLOCK * NSA_DH) ** -0.5),
        'nsa_phi_v2': nrm(ks[21], (L, NSA_DH, NSA_DH), NSA_DH ** -0.5),
        'w_up_a': nrm(ks[22], (L, GM_W, D_MODEL), GM_W ** -0.5),
        'w_up_b': nrm(ks[23], (L, ML_W, D_MODEL), ML_W ** -0.5),
        'w_up_c': nrm(ks[24], (L, NSA_W, D_MODEL), NSA_W ** -0.5),
        'w_out': nrm(ks[25], (L, D_MODEL, D_MODEL), D_MODEL ** -0.5),
        'w_mlp1': nrm(ks[26], (L, D_MODEL, D_FF_3), D_MODEL ** -0.5),
        'w_mlp2': nrm(ks[27], (L, D_FF_3, D_MODEL), D_FF_3 ** -0.5),
        'g_final': 1.0 + nrm(ks[28], (D_MODEL,), 0.02),
    }

def third_block(x, c, g_norm1, g_norm2, w_ada, b_ada, w_in, gm_ln_g, gm_ln_b, gm_ws, gm_bs,
              ml_conv_w, ml_conv_b, ml_gate_b, ml_norm_g, nsa_pe_k, nsa_pe_v, nsa_phi_k1, nsa_phi_k2,
              nsa_phi_v1, nsa_phi_v2, w_up_a, w_up_b, w_up_c, w_out, w_mlp1, w_mlp2, g_final):
    cond = jax.nn.silu(c)
    for l in range(DEPTH):
        mod = (cond @ w_ada[l] + b_ada[l])[:, None, :]
        sh1, sc1, gt1, sh2, sc2, gt2 = jnp.split(mod, 6, axis=-1)
        h = rms_norm_3(x, g_norm1[l]) * (1.0 + sc1) + sh1
        x = x + gt1 * hybrid_mixer_3(h, w_in[l], gm_ln_g[l], gm_ln_b[l], gm_ws[l], gm_bs[l],
                                   ml_conv_w[l], ml_conv_b[l], ml_gate_b[l], ml_norm_g[l],
                                   nsa_pe_k[l], nsa_pe_v[l], nsa_phi_k1[l], nsa_phi_k2[l],
                                   nsa_phi_v1[l], nsa_phi_v2[l], w_up_a[l], w_up_b[l], w_up_c[l], w_out[l])
        h = rms_norm_3(x, g_norm2[l]) * (1.0 + sc2) + sh2
        x = x + gt2 * (jnp.square(jax.nn.relu(h @ w_mlp1[l])) @ w_mlp2[l])
    return rms_norm_3(x, g_final)


_first_inputs_3 = third_inputs


def third_inputs(seed=0):
    import zlib

    import numpy as np

    out = dict(_first_inputs_3(seed))
    spreads = {}
    factors = {'g_norm1': 8.0,
     'g_norm2': 24.037,
     'gm_ln_g': 38.318,
     'gm_ln_b': 39.729,
     'gm_bs': 7.936,
     'ml_conv_b': 64.0,
     'ml_norm_g': 64.0,
     'nsa_pe_k': 24.976,
     'nsa_pe_v': 53.439,
     'nsa_phi_k1': 8.0,
     'nsa_phi_k2': 8.0,
     'g_final': 7.547,
     'ml_conv_w': 6.663}
    for name, (base, spread) in spreads.items():
        noise = np.random.default_rng([zlib.crc32(name.encode()), seed]).standard_normal(out[name].shape)
        drawn = base * np.exp(spread * noise) if base else spread * noise
        out[name] = jnp.asarray(drawn.astype(out[name].dtype))
    for name, factor in factors.items():
        out[name] = (out[name] * factor).astype(out[name].dtype)
    return out


_narrow_inputs_3 = third_inputs


def third_inputs(seed=0):

    out = dict(_narrow_inputs_3(seed))
    wider = {'g_norm2': 3.05,
     'gm_ln_g': 3.23,
     'gm_ln_b': 3.2,
     'ml_conv_b': 12.0,
     'ml_norm_g': 8.74,
     'nsa_pe_k': 4.58,
     'nsa_pe_v': 3.14,
     'g_final': 3.14}
    for name, times in wider.items():
        mean = out[name].mean()
        out[name] = (mean + times * (out[name] - mean)).astype(out[name].dtype)
    return out


def setup_inputs(seed=0):
    out = dict(first_inputs(seed))
    for name, value in second_inputs(seed + 1).items():
        if name != "x":
            out[name + "_2"] = value
    for name, value in third_inputs(seed + 2).items():
        if name != "x":
            out[name + "_3"] = value
    return out


def reference(
    x, mem, w_in, ssd_conv_w, ssd_conv_b, ssd_dt_bias, ssd_a_log, ssd_d, ssd_norm_w, ret_gn_w,
    ret_gn_b, w_mix_out, ln1_g, ln1_b, w_xq, w_xk, w_xv, w_xo, ln2_g, ln2_b, w_ffn_up, b_ffn_up,
    ffn_conv_w, ffn_conv_b, w_ffn_down, ln3_g, ln3_b, norm_mix_2, w_in_2, conv_a_w_2, w_out_a_2,
    rnn_conv_w_2, rnn_conv_b_2, w_rg_2, b_rg_2, w_ig_2, b_ig_2, lru_lambda_2, w_out_b_2, w_o_2,
    norm_ffn_2, w_q_2, sub_keys_1_2, sub_keys_2_2, expert_u_2, expert_v_2, norm_final_2, c_3,
    g_norm1_3, g_norm2_3, w_ada_3, b_ada_3, w_in_3, gm_ln_g_3, gm_ln_b_3, gm_ws_3, gm_bs_3,
    ml_conv_w_3, ml_conv_b_3, ml_gate_b_3, ml_norm_g_3, nsa_pe_k_3, nsa_pe_v_3, nsa_phi_k1_3,
    nsa_phi_k2_3, nsa_phi_v1_3, nsa_phi_v2_3, w_up_a_3, w_up_b_3, w_up_c_3, w_out_3, w_mlp1_3,
    w_mlp2_3, g_final_3,
):
    x = first_block(
        x, mem, w_in, ssd_conv_w, ssd_conv_b, ssd_dt_bias, ssd_a_log, ssd_d, ssd_norm_w,
        ret_gn_w, ret_gn_b, w_mix_out, ln1_g, ln1_b, w_xq, w_xk, w_xv, w_xo, ln2_g, ln2_b,
        w_ffn_up, b_ffn_up, ffn_conv_w, ffn_conv_b, w_ffn_down, ln3_g, ln3_b,
    )
    x = second_block(
        x, norm_mix_2, w_in_2, conv_a_w_2, w_out_a_2, rnn_conv_w_2, rnn_conv_b_2, w_rg_2,
        b_rg_2, w_ig_2, b_ig_2, lru_lambda_2, w_out_b_2, w_o_2, norm_ffn_2, w_q_2, sub_keys_1_2,
        sub_keys_2_2, expert_u_2, expert_v_2, norm_final_2,
    )
    return third_block(
        x, c_3, g_norm1_3, g_norm2_3, w_ada_3, b_ada_3, w_in_3, gm_ln_g_3, gm_ln_b_3, gm_ws_3,
        gm_bs_3, ml_conv_w_3, ml_conv_b_3, ml_gate_b_3, ml_norm_g_3, nsa_pe_k_3, nsa_pe_v_3,
        nsa_phi_k1_3, nsa_phi_k2_3, nsa_phi_v1_3, nsa_phi_v2_3, w_up_a_3, w_up_b_3, w_up_c_3,
        w_out_3, w_mlp1_3, w_mlp2_3, g_final_3,
    )


_drawn_inputs = setup_inputs


def setup_inputs(seed=0):
    import zlib

    import numpy as np

    out = dict(_drawn_inputs(seed))
    spreads = {}
    factors = {'rnn_conv_b_2': 3.107, 'b_rg_2': 5.971, 'b_ig_2': 3.321, 'ml_conv_b_3': 5.966}
    for name, (base, spread) in spreads.items():
        noise = np.random.default_rng([zlib.crc32(name.encode()), seed]).standard_normal(out[name].shape)
        drawn = base * np.exp(spread * noise) if base else spread * noise
        out[name] = jnp.asarray(drawn.astype(out[name].dtype))
    for name, factor in factors.items():
        out[name] = (out[name] * factor).astype(out[name].dtype)
    return out
```

```python
from contextlib import contextmanager

import numpy as np

import concourse.bass as bass
import concourse.mybir as mybir

F32 = mybir.dt.float32
U32 = mybir.dt.uint32
ACT = mybir.ActivationFunctionType
ALU = mybir.AluOpType
AX = mybir.AxisListType

P = 128
T = 512
TT = T // P
D = 1024
DT = D // P
MEM = 256
SLAB = 4096
BANKS = 4

SSD_INNER, SSD_HEADS, SSD_HD, SSD_CONV = 1024, 16, 64, 4
XBC = 1536
RET_HEADS, RET_QK, RET_DV = 8, 64, 128
D_FF, FF_TILES = 2752, 22
ALPHA = 2.0 ** 0.25
XH, XHD = 4, 256
D_RNN, RT = 1280, 10
PEER_H, PEER_K = 8, 16
NKEYS = 128
SLOTS = PEER_H * PEER_K
GATHER = 8
NSA_H, NSA_DH, N_CMP, CMP_BLOCK, CMP_STRIDE = 8, 64, 31, 32, 16
FF3_TILES = 32
NEG = -1e30

SEG = [0, 512, 896, 1152]
SEG_LEN = 1280


def seg_width(s):
    return T - s * P


def cols(v, tiles):
    v = np.asarray(v).reshape(-1)
    out = np.zeros((tiles * P,), np.float32)
    out[: v.size] = v
    return out.reshape(tiles, P).T


def rows(v):
    out = np.zeros((P, 1), np.float32)
    out[: np.size(v), 0] = np.asarray(v).reshape(-1)
    return out


def slabs(w, width):
    k, n = w.shape
    kt, ns = -(-k // P), -(-n // width)
    if (kt * P, ns * width) != (k, n):
        w = np.pad(w, ((0, kt * P - k), (0, ns * width - n)))
    return np.ascontiguousarray(w.reshape(kt, P, ns, width).transpose(2, 1, 0, 3).reshape(ns, P, kt * width))


def channel_major(x):
    t, c = x.shape
    return np.ascontiguousarray(x.T.reshape(c // P, P, t).transpose(1, 0, 2).reshape(P, -1))


def lay_out(i):
    a, par, at = {}, [], {}

    def param(name, v):
        at[name] = (sum(p.shape[1] for p in par), v.shape[1])
        par.append(np.asarray(v, np.float32))

    w = i["w_in"][0]
    o = np.cumsum([0, 1024, 1536, 16, 512, 512, 1024, 1024])
    a["x"] = channel_major(i["x"][0])
    a["mem"] = channel_major(i["mem"][0])
    a["w_z"] = slabs(w[:, o[0]:o[1]], 512)
    a["w_xbc"] = slabs(w[:, o[1]:o[2]], 512)
    a["w_dt"] = slabs(w[:, o[2]:o[3]], 16)
    a["w_qk"] = slabs(w[:, o[3]:o[5]], 512)
    a["w_v"] = slabs(w[:, o[5]:o[6]], 512)
    a["w_g"] = slabs(w[:, o[6]:o[7]], 512)
    a["w_mix"] = slabs(i["w_mix_out"][0], 256)
    a["w_xk"], a["w_xv"] = slabs(i["w_xk"][0], 512), slabs(i["w_xv"][0], 512)
    a["w_xq"], a["w_xo"] = slabs(i["w_xq"][0], 512), slabs(i["w_xo"][0], 512)
    up, pad = i["w_ffn_up"][0], FF_TILES * P - D_FF

    def pairs(v):
        v = np.pad(v.reshape(-1, 2, D_FF), ((0, 0), (0, 0), (0, pad)))
        return v.reshape(-1, 2, FF_TILES, P).transpose(0, 2, 1, 3).reshape(v.shape[0], -1)

    a["w_up"] = slabs(pairs(up), 256)
    a["w_down"] = slabs(i["w_ffn_down"][0], 128)
    for k in range(SSD_CONV):
        param(f"ssd_conv{k}", cols(i["ssd_conv_w"][0, k], 12))
    param("ssd_conv_b", cols(i["ssd_conv_b"][0], 12))
    param("dt_bias", rows(i["ssd_dt_bias"]))
    param("a_log", rows(i["ssd_a_log"]))
    param("ssd_d", cols(np.repeat(np.asarray(i["ssd_d"][0]), SSD_HD), 8))
    param("ssd_norm", cols(i["ssd_norm_w"], 8))
    param("gn_w", cols(i["ret_gn_w"], 8))
    param("gn_b", cols(i["ret_gn_b"], 8))
    for n in (1, 2, 3):
        param(f"ln{n}_g", cols(i[f"ln{n}_g"], 8))
        param(f"ln{n}_b", cols(i[f"ln{n}_b"], 8))
    param("b_up", cols(pairs(np.asarray(i["b_ffn_up"])), 2 * FF_TILES))
    for k in range(3):
        param(f"ffn_conv{k}", cols(pairs(np.asarray(i["ffn_conv_w"][0, k:k + 1])), 2 * FF_TILES))
    param("ffn_conv_b", cols(pairs(np.asarray(i["ffn_conv_b"])), 2 * FF_TILES))

    w = i["w_in_2"][0]
    o = np.cumsum([0, 1024, 1024, 1024, 1280, 1280, 1024, 1024])
    for n, name in enumerate(("ax", "ab", "ac", "rx", "ry", "ga", "gb")):
        a["w2_" + name] = slabs(w[:, o[n]:o[n + 1]], 256 if name in ("rx", "ry") else 512)
    a["w2_out_a"], a["w2_o"] = slabs(i["w_out_a_2"][0], 512), slabs(i["w_o_2"][0], 512)
    a["w2_out_b"] = slabs(i["w_out_b_2"][0], 256)
    a["w2_q"] = slabs(i["w_q_2"][0], 512)
    a["w2_rg"] = np.ascontiguousarray(np.asarray(i["w_rg_2"][0]).transpose(1, 0, 2).reshape(1, P, -1))
    a["w2_ig"] = np.ascontiguousarray(np.asarray(i["w_ig_2"][0]).transpose(1, 0, 2).reshape(1, P, -1))
    k1, k2 = np.asarray(i["sub_keys_1_2"][0]), np.asarray(i["sub_keys_2_2"][0])
    a["keys"] = np.ascontiguousarray(np.stack([k1, k2], 1).transpose(3, 0, 1, 2).reshape(P, -1))
    a["expert_u"], a["expert_v"] = i["expert_u_2"][0], i["expert_v_2"][0]
    param("norm_mix", cols(i["norm_mix_2"], 8))
    for k in range(3):
        param(f"conv_a{k}", cols(i["conv_a_w_2"][0, k], 8))
    for k in range(4):
        param(f"rnn_conv{k}", cols(i["rnn_conv_w_2"][0, k], RT))
    for name in ("rnn_conv_b", "b_rg", "b_ig", "lru_lambda"):
        param(name, cols(i[name + "_2"], RT))
    param("norm_ffn", cols(i["norm_ffn_2"], 8))
    param("norm_final", cols(i["norm_final_2"], 8))

    w = np.asarray(i["w_in_3"][0])
    o = np.cumsum([0, 512, 512, 512, 512, 512, 512, 4, 4, 512] + [128] * 6 + [24, 1024, 1024, 1024])
    a["w3_ada"] = slabs(i["w_ada_3"][0], 512)
    a["c"] = channel_major(np.asarray(i["c_3"]))
    a["w3_gu"], a["w3_gv"] = slabs(w[:, o[0]:o[1]], 512), slabs(w[:, o[1]:o[2]], 512)
    a["w3_mqk"] = slabs(w[:, o[2]:o[4]], 512)
    a["w3_mv"], a["w3_mo"] = slabs(w[:, o[4]:o[5]], 512), slabs(w[:, o[5]:o[6]], 512)
    a["w3_mi"], a["w3_mf"] = slabs(w[:, o[6]:o[7]], 4), slabs(w[:, o[7]:o[8]], 4)
    a["w3_nq"] = slabs(w[:, o[8]:o[9]], 512)
    kc, vc, ks, vs, kw, vw = (w[:, o[9 + n]:o[10 + n]] for n in range(6))
    a["w3_kvc"] = slabs(np.concatenate([kc, vc], 1), 256)
    a["w3_ksw"] = slabs(np.concatenate([k[:, g * 64:g * 64 + 64] for k in (ks, kw) for g in (0, 0, 1, 1)], 1), 512)
    a["w3_vsw"] = slabs(np.concatenate([vs, vw], 1), 256)
    a["w3_ng"] = slabs(w[:, o[15]:o[16]], 24)
    for n, name in enumerate(("ga", "gb", "gc")):
        a["w3_" + name] = slabs(w[:, o[16 + n]:o[17 + n]], 512)
        a["w3_up_" + name[1]] = slabs(i[f"w_up_{name[1]}_3"][0], 1024)
    a["w3_out"] = slabs(i["w_out_3"][0], 512)
    a["w3_mlp1"], a["w3_mlp2"] = slabs(i["w_mlp1_3"][0], 512), slabs(i["w_mlp2_3"][0], 128)
    param("b_ada", cols(i["b_ada_3"], 48))
    for name in ("g_norm1", "g_norm2", "g_final"):
        param(name, cols(i[name + "_3"], 8))
    param("gm_ln_g", cols(i["gm_ln_g_3"], 4))
    param("gm_ln_b", cols(i["gm_ln_b_3"], 4))
    a["gm_w"] = np.ascontiguousarray(np.asarray(i["gm_ws_3"][0]).transpose(2, 0, 1).reshape(P, -1))
    a["gm_b"] = np.ascontiguousarray(np.broadcast_to(np.asarray(i["gm_bs_3"][0]).reshape(1, -1), (P, 512)))
    for k in range(4):
        param(f"ml_conv{k}", cols(i["ml_conv_w_3"][0, k], 8))
    param("ml_conv_b", cols(i["ml_conv_b_3"], 8))
    param("ml_bi", rows(np.asarray(i["ml_gate_b_3"])[0, :4]))
    param("ml_bf", rows(np.asarray(i["ml_gate_b_3"])[0, 4:]))
    param("ml_norm", cols(i["ml_norm_g_3"], 4))
    for n in "kv":
        pe = np.asarray(i[f"nsa_pe_{n}_3"][0]).T
        param(f"pe_{n}", np.concatenate([pe, pe], 0))
        phi = np.asarray(i[f"nsa_phi_{n}1_3"][0]).reshape(CMP_BLOCK, 64, 64).transpose(1, 0, 2).reshape(64, -1)
        a[f"phi_{n}1"] = np.ascontiguousarray(np.concatenate([phi, phi], 0))
        a[f"phi_{n}2"] = np.ascontiguousarray(i[f"nsa_phi_{n}2_3"][0])
    a["phi_k2"] = np.concatenate([a["phi_k2"], a["phi_k2"]], 1)
    a["params"] = np.ascontiguousarray(np.concatenate(par, 1))
    a.update(constants())
    return {k: np.ascontiguousarray(v) for k, v in a.items()}, at


def constants():
    c = {}
    p, j = np.arange(P)[:, None], np.arange(T)[None, :]
    eye = np.eye(P)
    turn = np.zeros((P, P))
    for m in range(P):
        d = m % RET_QK
        if d < 32:
            turn[m + 32, m] = -1.0
        else:
            turn[m - 32, m] = 1.0
    causal = (p <= np.arange(P)[None, :]).astype(float)
    eps = np.tile(np.array([[1e-5, 1e-6]]), (P, 1))
    c["base"] = np.concatenate([eye, turn, causal, np.ones((P, P)), eps], 1)
    freqs = (1.0 / (np.float32(10000.0) ** np.linspace(0.0, 1.0, 32, dtype=np.float32))).astype(np.float32)
    ang = (np.arange(T, dtype=np.float32)[None, :] * freqs[:, None]).astype(np.float32)
    ang = np.tile(ang.astype(np.float64), (4, 1))
    c["rope"] = np.concatenate([np.cos(ang), np.sin(ang)], 1)
    gamma = np.log1p(-np.exp2(-5.0 - np.arange(RET_HEADS)))
    dist = j - p
    c["decay"] = np.concatenate(
        [np.where(dist >= 0, np.exp(np.maximum(dist, 0) * g), 0.0) * RET_QK ** -0.5 for g in gamma], 1)
    alibi = j - p - 384.0
    c["alibi"] = np.where(alibi > 0, NEG, alibi)
    t = np.arange(T)
    n = np.arange(N_CMP)
    ok = (n * CMP_STRIDE + CMP_BLOCK - 1)[None, :] <= t[:, None]
    center = n * CMP_STRIDE + (CMP_BLOCK - 1) * 0.5
    cd = np.where(ok, center[None, :] - t[:, None], NEG)
    for name, v in (("cmp_dist", cd), ("cmp_ok", ok.astype(float))):
        c[name] = v.reshape(TT, P, N_CMP).transpose(1, 0, 2).reshape(P, -1)
    sel = np.zeros((24, 12, P))
    for b in range(3):
        for tile in range(4):
            for q in range(P):
                sel[(2 * tile + q // 64) * 3 + b, b * 4 + tile, q] = 1.0
    c["gate_sel"] = sel.reshape(24, -1)
    c["iota"] = np.tile(np.arange(256.0)[None, :], (P, 1))
    return {k: np.ascontiguousarray(v, dtype=np.float32) for k, v in c.items()}


class Names:
    pass


class Counter:

    def __init__(self, nc, name):
        self.sem, self.base = nc.alloc_semaphore(name), 0

    def at(self, n):
        return self.base + n

    def passed(self, n):
        self.base += n


class Chain:

    def __init__(self, eng, counter):
        self.eng, self.counter, self.turn = eng, counter, 0

    def __call__(self, ins):
        self.counter.base += 1
        ins.then_inc(self.counter.sem, 1)
        self.eng.wait_ge(self.counter.sem, self.counter.base + self.turn)

    @contextmanager
    def loop(self, count, steps):
        start, outer = self.counter.base, self.turn
        with self.eng.Fori(0, count) as i:
            self.turn = outer + i * steps
            yield i
        assert self.counter.base == start + steps, (self.counter.base - start, steps)
        self.turn = outer
        self.counter.base = start + steps * count


PLAN = [
    ("w_z", 8, 512), ("w_xbc", 8, 512), ("w_dt", 8, 16), ("w_qk", 8, 512), ("w_g", 8, 512), ("w_v", 8, 512),
    ("w_mix", 16, 256), ("w_xk", 8, 512), ("w_xv", 8, 512), ("w_xq", 8, 512), ("w_xo", 8, 512),
    ("w_up", 8, 256), ("w_down", 22, 128),
    ("w2_ax", 8, 512), ("w2_ac", 8, 512), ("w2_ab", 8, 512), ("w2_rx", 8, 256), ("w2_ry", 8, 256),
    ("w2_rg", 1, 1280), ("w2_ig", 1, 1280), ("w2_ga", 8, 512), ("w2_gb", 8, 512), ("w2_out_a", 8, 512),
    ("w2_out_b", 10, 256), ("w2_o", 8, 512), ("w2_q", 8, 512),
    ("w3_ada", 8, 512), ("w3_gu", 8, 512), ("w3_gv", 8, 512), ("w3_mqk", 8, 512), ("w3_mv", 8, 512),
    ("w3_mo", 8, 512), ("w3_mi", 8, 4), ("w3_mf", 8, 4), ("w3_nq", 8, 512), ("w3_kvc", 8, 256),
    ("w3_ksw", 8, 512), ("w3_vsw", 8, 256), ("w3_ng", 8, 24),
    ("w3_ga", 8, 512), ("w3_gb", 8, 512), ("w3_gc", 8, 512),
    ("w3_up_a", 4, 1024), ("w3_up_b", 4, 1024), ("w3_up_c", 4, 1024), ("w3_out", 8, 512),
    ("w3_mlp1", 8, 512), ("w3_mlp2", 32, 128),
]
RING = 2


def part(name, act, evac, tile=P, n=T, tokens=0, by="act", steps=0, block_diag=False):
    p = Names()
    p.name, p.act, p.evac, p.tile, p.n, p.tokens, p.by, p.steps, p.block_diag = name, act, evac, tile, n, tokens, by, steps, block_diag
    return p


def linears(s, parts):
    nc = s.nc
    for p in parts:
        p.index = [w[0] for w in PLAN].index(p.name)
        assert p.index == s.next_part, p.name
        s.next_part += 1
        _, p.kt, p.width = PLAN[p.index]
        p.first = s.first_slab[p.index]
        p.slabs = s.first_slab[p.index + 1] - p.first
        p.per_slab = p.tokens or p.width // p.tile
        p.tile0 = s.tiles
        s.tiles += p.slabs * p.per_slab
        p.body = 4 if p.per_slab == 1 else 2
        p.bodies = p.slabs // p.body if p.slabs >= 2 * p.body else 0
        for k in range(p.slabs):
            s.slab_end.append(p.tile0 + (k + 1) * p.per_slab)

    def load(sync, slab, consumed, index, k, slot):
        if consumed is not None:
            sync.wait_ge(s.tiles_done.sem, consumed)
        _, kt, width = PLAN[index]
        sync.dma_start(s.ring[:, slot, 0:kt * width], s.I[PLAN[index][0]][k]).then_inc(s.slab_ready[slot], 16)

    def load_static(sync, slab):
        if slab < s.first_slab[-1]:
            index = max(j for j in range(len(PLAN)) if s.first_slab[j] <= slab)
            consumed = s.slab_end[slab - RING] if slab >= RING else None
            load(sync, slab, consumed, index, slab - s.first_slab[index], slab % RING)

    with nc.Block() as block:
        @block.sync
        def _(sync):
            for p in parts:
                if p.first == 0:
                    for slab in range(RING):
                        load_static(sync, slab)
                inside = max(p.slabs - RING, 0)
                pairs = inside // RING if inside >= 2 * RING else 0
                if pairs:
                    with sync.Fori(0, pairs) as i:
                        for j in range(RING):
                            load(sync, None, p.tile0 + (i * RING + j + 1) * p.per_slab, p.index,
                                 i * RING + j + RING, (p.first + j) % RING)
                for k in range(pairs * RING, p.slabs):
                    load_static(sync, p.first + k + RING)

        @block.tensor
        def _(pe):
            def slab_products(p, i, j):
                slab = p.first + j
                slot, t0 = slab % RING, j * p.per_slab
                pe.wait_ge(s.slab_ready[slot], (slab // RING + 1) * 16 + i * (p.body // RING) * 16)
                w = s.ring[:, slot, 0:p.kt * p.width].rearrange("p (k n) -> p k n", k=p.kt)
                for u in range(p.per_slab):
                    t = t0 + u
                    bank = s.ps[(p.tile0 + t) % BANKS]
                    if not (isinstance(i, int) and t < BANKS):
                        pe.wait_ge(s.evac_done.sem, p.tile0 + t - BANKS + 1 + i * (p.body * p.per_slab))
                    for k in range(p.kt):
                        first, last = k == 0, k == p.kt - 1
                        if p.tokens:
                            mm = pe.matmul(bank[:, 0:p.width], p.act(k)[:, u * P:(u + 1) * P], w[:, k, :],
                                           start=first, stop=last)
                        else:
                            mm = pe.matmul(bank[0:p.tile, 0:p.n], w[:, k, u * p.tile:(u + 1) * p.tile],
                                           p.act(u if p.block_diag else k), start=first, stop=last)
                    mm.then_inc(s.tiles_done.sem, 1)

            for p in parts:
                if p.tile0:
                    pe.wait_ge(s.evac_done.sem, p.tile0)
                if p.bodies:
                    with pe.Fori(0, p.bodies) as i:
                        for j in range(p.body):
                            slab_products(p, i, j)
                for j in range(p.bodies * p.body, p.slabs):
                    slab_products(p, 0, j)

        def evacuate(eng, chain, by):
            for p in parts:
                if p.by != by:
                    continue
                tiles = p.body * p.per_slab

                def one(t, bank):
                    eng.wait_ge(s.tiles_done.sem, p.tile0 + t + 1)
                    if not isinstance(t, int) and by == "act":
                        eng.sem_inc(s.held, 1)
                    ps = s.ps[bank]
                    ps = ps[:, 0:p.width] if p.tokens else ps[0:p.tile, 0:p.n]
                    p.evac(eng, chain, t, ps).then_inc(s.evac_done.sem, 1)

                if p.bodies:
                    with chain.loop(p.bodies, p.steps * tiles) as i:
                        for u in range(tiles):
                            one(i * tiles + u, (p.tile0 + u) % BANKS)
                for t in range(p.bodies * tiles, p.slabs * p.per_slab):
                    one(t, (p.tile0 + t) % BANKS)

        @block.scalar
        def _(act):
            evacuate(act, Chain(act, s.act_chain), "act")

        @block.vector
        def _(dve):
            evacuate(dve, Chain(dve, s.dve_chain), "dve")


def residual(s, scale=1.0):
    def evac(dve, step, t, ps):
        return dve.scalar_tensor_tensor(s.x[:, t, :], s.x[:, t, :], scale, ps, ALU.mult, ALU.add)
    return evac


def store(dst, func=ACT.Copy, bias=None, scale=1.0):
    def evac(act, step, t, ps):
        if bias is None:
            return act.activation(dst(t), ps, func, scale=scale)
        return act.activation(dst(t), ps, func, bias=bias(t), scale=scale)
    return evac


def norm(s, src, tiles, group, dst, scratch, center, eps, gain, bias=None, post=None):
    n, groups = group * P, tiles // group
    sq, std = scratch[:, 0:group, :], scratch[:, group:group + 2, :]
    mean_ready, cen_ready, sq_ready, var_ready, std_ready, out_ready = s.norm_sems
    with s.nc.Block() as block:
        @block.tensor
        def _(pe):
            for g in range(groups):
                if center:
                    for u in range(group):
                        mm = pe.matmul(s.ps[4 + g % 2][:], s.ones, src[:, g * group + u, :], start=u == 0, stop=u == group - 1)
                    mm.then_inc(mean_ready.sem, 1)
                pe.wait_ge(sq_ready.sem, sq_ready.at(g + 1))
                for u in range(group):
                    mm = pe.matmul(s.ps[6 + g % 2][:], s.ones, sq[:, u, :], start=u == 0, stop=u == group - 1)
                mm.then_inc(var_ready.sem, 1)

        @block.scalar
        def _(act):
            for g in range(groups):
                if center:
                    act.wait_ge(cen_ready.sem, cen_ready.at(g + 1))
                if g >= 1:
                    act.wait_ge(var_ready.sem, var_ready.at(g))
                act.activation(sq, src[:, g * group:(g + 1) * group, :], ACT.Square).then_inc(sq_ready.sem, 1)
                act.wait_ge(var_ready.sem, var_ready.at(g + 1))
                if g >= 2:
                    act.wait_ge(out_ready.sem, out_ready.at(g - 1))
                act.activation(std[:, g % 2, :], s.ps[6 + g % 2][:], ACT.Sqrt, bias=s.eps[eps], scale=1.0 / n).then_inc(std_ready.sem, 1)

        @block.vector
        def _(dve):
            step = Chain(dve, s.dve_chain)

            def centre(g):
                dve.wait_ge(mean_ready.sem, mean_ready.at(g + 1))
                for u in range(group):
                    t = src[:, g * group + u, :]
                    ins = dve.scalar_tensor_tensor(t, s.ps[4 + g % 2][:], -1.0 / n, t, ALU.mult, ALU.add)
                ins.then_inc(cen_ready.sem, 1)

            for g in range(groups):
                if center:
                    centre(g)
                dve.wait_ge(std_ready.sem, std_ready.at(g + 1))
                r = std[:, g % 2, :]
                step(dve.reciprocal(r, r))
                for u in range(group):
                    t = g * group + u
                    ins = dve.scalar_tensor_tensor(dst[:, t, :], src[:, t, :], gain[:, t:t + 1], r, ALU.mult, ALU.mult)
                    if bias is not None or post is not None:
                        step(ins)
                    if bias is not None and post is not None:
                        ins = dve.scalar_tensor_tensor(dst[:, t, :], dst[:, t, :], bias[:, t:t + 1], post[:, t, :], ALU.add, ALU.mult)
                    elif bias is not None:
                        ins = dve.tensor_scalar(dst[:, t, :], dst[:, t, :], bias[:, t:t + 1], None, ALU.add)
                    elif post is not None:
                        ins = dve.tensor_tensor(dst[:, t, :], dst[:, t, :], post[:, t, :], ALU.mult)
                ins.then_inc(out_ready.sem, 1)
    for c in (sq_ready, var_ready, std_ready, out_ready) + ((mean_ready, cen_ready) if center else ()):
        c.passed(groups)


def softplus_rows(s, jobs):
    ready, taken = s.pair_sems
    with s.nc.Block() as block:
        @block.scalar
        def _(act):
            step = Chain(act, s.act_chain)
            for n, (x, out, e, w, d, sigmoid) in enumerate(jobs):
                step(act.activation(e, x, ACT.Abs))
                act.activation(e, e, ACT.Exp, scale=-1.0).then_inc(ready.sem, 1)
                act.wait_ge(taken.sem, taken.at(n + 1))
                act.activation(out, w, ACT.Ln).then_inc(ready.sem, 1)

        @block.vector
        def _(dve):
            step = Chain(dve, s.dve_chain)
            for n, (x, out, e, w, d, sigmoid) in enumerate(jobs):
                dve.wait_ge(ready.sem, ready.at(2 * n + 1))
                dve.tensor_scalar(w, e, 1.0, None, ALU.add).then_inc(taken.sem, 1)
                dve.wait_ge(taken.sem, taken.at(n + 1))
                step(dve.tensor_scalar(d, w, 1.0, None, ALU.subtract))
                step(dve.tensor_tensor(d, e, d, ALU.subtract))
                dve.wait_ge(ready.sem, ready.at(2 * n + 2))
                step(dve.reciprocal(w, w))
                step(dve.tensor_tensor(d, d, w, ALU.mult))
                step(dve.tensor_tensor(d, d, out, ALU.add))
                step(dve.tensor_scalar(e, x, 0.0, None, ALU.min if sigmoid else ALU.max))
                step(dve.tensor_tensor(out, e, d, ALU.subtract if sigmoid else ALU.add))
    ready.passed(2 * len(jobs))
    taken.passed(len(jobs))


def load_start(s):
    with s.nc.Block() as block:
        @block.sync
        def _(sync):
            for dst, src in ((s.base[:], s.I["base"]), (s.par[:], s.I["params"]), (s.xflat, s.I["x"])):
                sync.dma_start(dst, src).then_inc(s.loaded.sem, 16)
            sync.wait_ge(s.loaded.sem, s.loaded.at(48))
    s.loaded.passed(48)


def causal_conv(s, dve, step, dst, src, taps, t):
    n = len(taps)
    step(dve.tensor_scalar(dst, src(0), taps[0][:, t], None, ALU.mult))
    for k in range(1, n):
        ins = dve.scalar_tensor_tensor(dst, src(k), taps[k][:, t], dst, ALU.mult, ALU.add)
        if k < n - 1:
            step(ins)
    return ins


def first_projection(s):
    v = s.view
    s.sz, s.qk, s.sg = v(0, 8), v(21, 8), v(29, 8)
    s.xbc = s.arena[:, 8 * T:8 * T + 12 * (T + 3)].rearrange("p (a t) -> p a t", a=12)
    s.vt = v(37, 8).rearrange("p a t -> p (a t)").rearrange("p (t c) -> p t c", t=TT)
    s.dt_raw = s.arena[0:SSD_HEADS, 45 * T:46 * T]
    with s.nc.Block() as block:
        @block.gpsimd
        def _(pool):
            pool.memset(s.xbc[:, :, 0:3], 0.0)
    x = lambda k: s.x[:, k, :]

    def store_v(act, step, t, ps):
        return act.activation(s.vt[:, t % TT, (t // TT) * 512:(t // TT) * 512 + 512], ps, ACT.Copy)

    linears(s, [
        part("w_z", x, store(lambda t: s.sz[:, t, :], ACT.Silu)),
        part("w_xbc", x, store(lambda t: s.xbc[:, t, 3:3 + T])),
        part("w_dt", x, store(lambda t: s.dt_raw, ACT.Identity, lambda t: s.col("dt_bias")[0:SSD_HEADS, :]), tile=SSD_HEADS),
        part("w_qk", x, store(lambda t: s.qk[:, t, :])),
        part("w_g", x, store(lambda t: s.sg[:, t, :], ACT.Silu)),
        part("w_v", x, store_v, tokens=TT),
    ])


def ssd_prepare(s):
    v = s.view
    s.xs = v(46, 12)
    row = lambda k: s.arena[0:SSD_HEADS, k * T:(k + 1) * T]
    s.dt, s.acs, e, w, d = row(71), row(72), row(58), row(59), row(60)
    conv_ready, = s.one_sem
    with s.nc.Block() as block:
        @block.vector
        def _(dve):
            step = Chain(dve, s.dve_chain)
            taps = [s.col(f"ssd_conv{k}") for k in range(SSD_CONV)]
            with step.loop(12, SSD_CONV - 1) as t:
                causal_conv(s, dve, step, s.xs[:, t, :], lambda k: s.xbc[:, t, k:k + T], taps, bass.ds(t, 1)).then_inc(conv_ready.sem, 1)

        @block.scalar
        def _(act):
            with act.Fori(0, 12) as t:
                act.wait_ge(conv_ready.sem, conv_ready.at(t + 1))
                act.sem_inc(s.held, 1)
                act.activation(s.xs[:, t, :], s.xs[:, t, :], ACT.Silu, bias=s.col("ssd_conv_b")[:, bass.ds(t, 1)])
    conv_ready.passed(12)
    softplus_rows(s, [(s.dt_raw, s.dt, e, w, d, False)])
    with s.nc.Block() as block:
        @block.scalar
        def _(act):
            act.activation(s.small[0:SSD_HEADS, 0:1], s.col("a_log")[0:SSD_HEADS, :], ACT.Exp).then_inc(s.pair_sems[0].sem, 1)

        @block.vector
        def _(dve):
            step = Chain(dve, s.dve_chain)
            step(dve.memset(w, 1.0))
            dve.wait_ge(s.pair_sems[0].sem, s.pair_sems[0].at(1))
            step(dve.tensor_scalar(d, s.dt, s.small[0:SSD_HEADS, 0:1], -1.0, ALU.mult, ALU.mult))
            step(dve.tensor_tensor_scan(s.acs, w, d, 0.0, ALU.mult, ALU.add))
    s.pair_sems[0].passed(1)


def ssd_turn(s):
    v = s.view
    s.dt_col, s.acs_col = (s.small[:, 64 + 64 * k:128 + 64 * k].rearrange("p (a h) -> p a h", a=TT) for k in range(2))
    s.xdt = v(63, 8).rearrange("p a t -> p (a t)").rearrange("p (t c) -> p t c", t=TT)
    s.cb = s.arena[:, 16 * T:16 * T + 2 * SEG_LEN].rearrange("p (g n) -> p g n", g=2)
    rows_ready, cols_ready, x_ready, x_done, cb_ready, cb_done = s.norm_sems
    with s.nc.Block() as block:
        @block.tensor
        def _(pe):
            for k, src in enumerate((s.dt, s.acs)):
                for a in range(TT):
                    mm = pe.transpose(s.ps[k][:, a * SSD_HEADS:(a + 1) * SSD_HEADS], src[:, a * P:(a + 1) * P], s.eye[0:SSD_HEADS, 0:SSD_HEADS])
            mm.then_inc(rows_ready.sem, 1)
            for a in range(TT):
                for half in range(2):
                    n = 2 * a + half
                    if n >= 2:
                        pe.wait_ge(x_done.sem, x_done.at(n - 1))
                    for u in range(4):
                        mm = pe.transpose(s.ps[2 + half][:, u * P:(u + 1) * P], s.xs[:, half * 4 + u, a * P:(a + 1) * P], s.eye)
                    mm.then_inc(x_ready.sem, 1)
            for g in range(2):
                for a in range(TT):
                    n = 4 * g + a
                    if n >= 4:
                        pe.wait_ge(cb_done.sem, cb_done.at(n - 3))
                    pe.matmul(s.ps[4 + a][:, 0:seg_width(a)], s.xs[:, 8 + g, a * P:(a + 1) * P], s.xs[:, 10 + g, a * P:T],
                              start=True, stop=True).then_inc(cb_ready.sem, 1)

        @block.vector
        def _(dve):
            dve.wait_ge(rows_ready.sem, rows_ready.at(1))
            dve.tensor_copy(s.acs_col.rearrange("p a h -> p (a h)"), s.ps[1][:, 0:64])
            dve.tensor_copy(s.dt_col.rearrange("p a h -> p (a h)"), s.ps[0][:, 0:64]).then_inc(cols_ready.sem, 1)
            dve.wait_ge(cols_ready.sem, cols_ready.at(1))
            for a in range(TT):
                for half in range(2):
                    dve.wait_ge(x_ready.sem, x_ready.at(2 * a + half + 1))
                    out = s.xdt[:, a, half * 512:half * 512 + 512].rearrange("p (h d) -> p h d", h=8)
                    dve.tensor_tensor(out, s.ps[2 + half][:].rearrange("p (h d) -> p h d", h=8),
                                      s.dt_col[:, a, half * 8:half * 8 + 8].unsqueeze(2).broadcast_to([P, 8, SSD_HD]),
                                      ALU.mult).then_inc(x_done.sem, 1)
            for g in range(2):
                for a in range(TT):
                    dve.wait_ge(cb_ready.sem, cb_ready.at(4 * g + a + 1))
                    seg = s.cb[:, g, SEG[a]:SEG[a] + seg_width(a)]
                    if a < TT - 1:
                        dve.tensor_copy(seg[:, P:], s.ps[4 + a][:, P:seg_width(a)])
                    dve.tensor_tensor(seg[:, 0:P], s.ps[4 + a][:, 0:P], s.causal, ALU.mult).then_inc(cb_done.sem, 1)
    for c, n in ((rows_ready, 1), (cols_ready, 1), (x_ready, 8), (x_done, 8), (cb_ready, 8), (cb_done, 8)):
        c.passed(n)


def ssd_heads(s):
    s.u = s.view(8, 8)
    s.att = [s.arena[:, 58 * T + k * SEG_LEN:58 * T + (k + 1) * SEG_LEN] for k in range(2)]
    bc_ready, diff_ready, exp_ready, att_ready, y_ready, y_done = s.norm_sems
    with s.nc.Block() as block:
        @block.tensor
        def _(pe):
            def sums(h):
                if h >= 2:
                    pe.wait_ge(diff_ready.sem, diff_ready.at(h - 1))
                pe.matmul(s.ps[h % 2][:], s.eye[0:SSD_HEADS, h:h + 1].broadcast_to([SSD_HEADS, P]), s.acs, start=True, stop=True).then_inc(bc_ready.sem, 1)

            sums(0)
            for h in range(SSD_HEADS):
                if h + 1 < SSD_HEADS:
                    sums(h + 1)
                j, lo = h // 2, (h % 2) * SSD_HD
                if h % 2 == 0 and j >= 2:
                    pe.wait_ge(y_done.sem, y_done.at(j - 1))
                pe.wait_ge(att_ready.sem, att_ready.at(h + 1))
                for a in range(TT):
                    mm = pe.matmul(s.ps[2 + j % 2][lo:lo + SSD_HD, a * P:T], s.xdt[:, a, h * SSD_HD:(h + 1) * SSD_HD],
                                   s.att[h % 2][:, SEG[a]:SEG[a] + seg_width(a)], start=a == 0, stop=a == TT - 1, skip_group_check=True)
                mm.then_inc(y_ready.sem, 1)

        @block.scalar
        def _(act):
            for h in range(SSD_HEADS):
                act.wait_ge(diff_ready.sem, diff_ready.at(h + 1))
                act.activation(s.att[h % 2], s.att[h % 2], ACT.Exp).then_inc(exp_ready.sem, 1)

        @block.vector
        def _(dve):
            step = Chain(dve, s.dve_chain)

            def differences(h):
                dve.wait_ge(bc_ready.sem, bc_ready.at(h + 1))
                if h >= 2:
                    dve.wait_ge(y_ready.sem, y_ready.at(h - 1))
                for a in range(TT):
                    ins = dve.tensor_scalar(s.att[h % 2][:, SEG[a]:SEG[a] + seg_width(a)], s.ps[h % 2][:, a * P:T],
                                            s.acs_col[:, a, h:h + 1], 0.0, ALU.subtract, ALU.min)
                ins.then_inc(diff_ready.sem, 1)

            differences(0)
            for h in range(SSD_HEADS):
                if h + 1 < SSD_HEADS:
                    differences(h + 1)
                dve.wait_ge(exp_ready.sem, exp_ready.at(h + 1))
                dve.tensor_tensor(s.att[h % 2], s.att[h % 2], s.cb[:, h // 8, :], ALU.mult).then_inc(att_ready.sem, 1)
                if h % 2:
                    j = h // 2
                    dve.wait_ge(y_ready.sem, y_ready.at(h + 1))
                    ins = dve.scalar_tensor_tensor(s.u[:, j, :], s.xs[:, j, :], s.col("ssd_d")[:, j:j + 1], s.ps[2 + j % 2][:], ALU.mult, ALU.add)
                    ins.then_inc(y_done.sem, 1)
                    dve.wait_ge(y_done.sem, y_done.at(j + 1))
                    step(dve.tensor_tensor(s.u[:, j, :], s.u[:, j, :], s.sz[:, j, :], ALU.mult))
    for c, n in ((bc_ready, 16), (diff_ready, 16), (exp_ready, 16), (att_ready, 16), (y_ready, 16), (y_done, 8)):
        c.passed(n)


def rotate(s):
    rope = s.view(63, 2)
    turned_ready, done = s.pair_sems
    tmp = s.view(66, 2)
    with s.nc.Block() as block:
        @block.sync
        def _(sync):
            sync.dma_start(rope.rearrange("p a t -> p (a t)"), s.I["rope"]).then_inc(s.loaded.sem, 16)

        @block.tensor
        def _(pe):
            for t in range(8):
                if t >= 2:
                    pe.wait_ge(done.sem, done.at(t - 1))
                pe.matmul(s.ps[t % 2][:], s.turn, s.qk[:, t, :], start=True, stop=True).then_inc(turned_ready.sem, 1)

        @block.vector
        def _(dve):
            step = Chain(dve, s.dve_chain)
            dve.wait_ge(s.loaded.sem, s.loaded.at(16))
            for t in range(8):
                dve.wait_ge(turned_ready.sem, turned_ready.at(t + 1))
                step(dve.tensor_tensor(tmp[:, t % 2, :], s.ps[t % 2][:], rope[:, 1, :], ALU.mult))
                step(dve.tensor_tensor(s.qk[:, t, :], s.qk[:, t, :], rope[:, 0, :], ALU.mult))
                dve.tensor_tensor(s.qk[:, t, :], s.qk[:, t, :], tmp[:, t % 2, :], ALU.add).then_inc(done.sem, 1)
    s.loaded.passed(16)
    turned_ready.passed(8)
    done.passed(8)


def retention(s):
    decay = s.view(46, 8)
    s.yr = s.view(63, 8)
    s_ready, s_done, y_ready, y_done, _, _ = s.norm_sems
    with s.nc.Block() as block:
        @block.sync
        def _(sync):
            sync.dma_start(decay.rearrange("p a t -> p (a t)"), s.I["decay"]).then_inc(s.loaded.sem, 16)

        @block.tensor
        def _(pe):
            def scores(h):
                j, lo = h // 2, (h % 2) * RET_QK
                for a in range(TT):
                    if h >= 1:
                        pe.wait_ge(s_done.sem, s_done.at(4 * (h - 1) + a + 1))
                    pe.matmul(s.ps[a][:, 0:seg_width(a)], s.qk[lo:lo + RET_QK, 4 + j, a * P:(a + 1) * P],
                              s.qk[lo:lo + RET_QK, j, a * P:T], start=True, stop=True).then_inc(s_ready.sem, 1)

            scores(0)
            for h in range(RET_HEADS):
                if h >= 2:
                    pe.wait_ge(y_done.sem, y_done.at(h - 1))
                for a in range(TT):
                    pe.wait_ge(s_done.sem, s_done.at(4 * h + a + 1))
                    mm = pe.matmul(s.ps[4 + h % 2][:, a * P:T], s.vt[:, a, h * RET_DV:(h + 1) * RET_DV],
                                   s.att[h % 2][:, SEG[a]:SEG[a] + seg_width(a)], start=a == 0, stop=a == TT - 1, skip_group_check=True)
                mm.then_inc(y_ready.sem, 1)
                if h + 1 < RET_HEADS:
                    scores(h + 1)

        @block.vector
        def _(dve):
            dve.wait_ge(s.loaded.sem, s.loaded.at(16))
            for h in range(RET_HEADS):
                if h >= 2:
                    dve.wait_ge(y_ready.sem, y_ready.at(h - 1))
                for a in range(TT):
                    dve.wait_ge(s_ready.sem, s_ready.at(4 * h + a + 1))
                    dve.tensor_tensor(s.att[h % 2][:, SEG[a]:SEG[a] + seg_width(a)], s.ps[a][:, 0:seg_width(a)],
                                      decay[:, h, 0:seg_width(a)], ALU.mult).then_inc(s_done.sem, 1)

        @block.scalar
        def _(act):
            for h in range(RET_HEADS):
                act.wait_ge(y_ready.sem, y_ready.at(h + 1))
                act.activation(s.yr[:, h, :], s.ps[4 + h % 2][:], ACT.Copy).then_inc(y_done.sem, 1)
    s.loaded.passed(16)
    for c, n in ((s_ready, 32), (s_done, 32), (y_ready, 8), (y_done, 8)):
        c.passed(n)


def first_mixer(s):
    first_projection(s)
    ssd_prepare(s)
    ssd_turn(s)
    ssd_heads(s)
    norm(s, s.u, 8, 4, s.u, s.view(46, 6), False, 0, s.col("ssd_norm"))
    rotate(s)
    retention(s)
    norm(s, s.yr, 8, 1, s.yr, s.view(46, 3), True, 0, s.col("gn_w"), s.col("gn_b"), s.sg)
    linears(s, [part("w_mix", lambda k: s.u[:, k, :] if k < 8 else s.yr[:, k - 8, :], residual(s, ALPHA), by="dve")])
    norm(s, s.x, 8, 8, s.x, s.view(0, 10), True, 0, s.col("ln1_g"), s.col("ln1_b"))


def attention_unit(q, k, keys, table, slope, ok, scale, v, pieces, channels, row, causal, out):
    u = Names()
    u.q, u.k, u.keys, u.table, u.slope, u.ok, u.scale = q, k, keys, table, slope, ok, scale
    u.v, u.pieces, u.channels, u.row, u.causal, u.out = v, pieces, channels, row, causal, out
    return u


def attention(s, units):
    nc = s.nc
    sc_ready, shifted, exp_ready, p_ready, pt_ready, pt_done = s.norm_sems
    o_ready, o_done = s.pair_sems
    steps = [(n, u, a) for n, (u, a) in enumerate((u, a) for u in range(len(units)) for a in range(TT))]
    outs = [(u, m) for u in range(len(units)) for m in range(units[u].pieces)]
    with nc.Block() as block:
        @block.tensor
        def _(pe):
            def scores(n, u, a):
                if n >= 2:
                    pe.wait_ge(shifted.sem, shifted.at(n - 1))
                q, k = units[u].q(a), units[u].k
                w = units[u].keys(a)
                for m in range(len(q)):
                    mm = pe.matmul(s.ps[n % 2][:, 0:w], q[m], k[m][:, 0:w], start=m == 0, stop=m == len(q) - 1)
                mm.then_inc(sc_ready.sem, 1)

            def turned(n, u, a):
                if n >= 2:
                    pe.wait_ge(pt_done.sem, pt_done.at(n - 1))
                pe.wait_ge(p_ready.sem, p_ready.at(n + 1))
                w = units[u].keys(a)
                for st in range(-(-w // P)):
                    ww = min(P, w - st * P)
                    mm = pe.transpose(s.ps[2 + n % 2][0:ww, st * P:(st + 1) * P], s.prob[n % 2][:, st * P:st * P + ww], s.eye)
                mm.then_inc(pt_ready.sem, 1)

            def values(u):
                pe.wait_ge(pt_done.sem, pt_done.at(TT * (u + 1)))
                w = units[u].keys(TT - 1)
                n_st = -(-w // P)
                for m in range(units[u].pieces):
                    o = outs.index((u, m))
                    if o >= 2:
                        pe.wait_ge(o_done.sem, o_done.at(o - 1))
                    for st in range(n_st):
                        ww = min(P, w - st * P)
                        lo = st * P if units[u].causal else 0
                        ch = units[u].channels
                        row = units[u].row
                        mm = pe.matmul(s.ps[4 + o % 2][row:row + ch, lo:T], units[u].v(st, m), s.pt[u % 2][0:ww, st, lo:T],
                                       start=st == 0, stop=st == n_st - 1, skip_group_check=True)
                    mm.then_inc(o_ready.sem, 1)

            scores(*steps[0])
            for n, u, a in steps:
                if n + 1 < len(steps):
                    scores(*steps[n + 1])
                turned(n, u, a)
                if a == TT - 1:
                    values(u)

        @block.vector
        def _(dve):
            step = Chain(dve, s.dve_chain)

            def shift(n, u, a):
                dve.wait_ge(sc_ready.sem, sc_ready.at(n + 1))
                w, un = units[u].keys(a), units[u]
                sc, neg = s.prob[n % 2][:, 0:w], s.small[:, 8 + n % 2:9 + n % 2]
                if n >= 2:
                    dve.wait_ge(pt_ready.sem, pt_ready.at(n - 1))
                if un.table is not None:
                    step(dve.scalar_tensor_tensor(sc, un.table(a), un.slope, s.ps[n % 2][:, 0:w], ALU.mult, ALU.add))
                else:
                    step(dve.tensor_scalar(sc, s.ps[n % 2][:, 0:w], un.scale, None, ALU.mult))
                step(dve.tensor_reduce(neg, sc, AX.X, ALU.max))
                dve.tensor_scalar(neg, neg, -1.0, None, ALU.mult).then_inc(shifted.sem, 1)

            shift(*steps[0])
            for n, u, a in steps:
                if n + 1 < len(steps):
                    shift(*steps[n + 1])
                dve.wait_ge(exp_ready.sem, exp_ready.at(n + 1))
                w, un = units[u].keys(a), units[u]
                total = s.small[:, 10 + n % 2:11 + n % 2]
                step(dve.reciprocal(total, total))
                pr = s.prob[n % 2][:, 0:w]
                if un.ok is not None:
                    ins = dve.scalar_tensor_tensor(pr, pr, total, un.ok(a), ALU.mult, ALU.mult)
                else:
                    ins = dve.tensor_scalar(pr, pr, total, None, ALU.mult)
                ins.then_inc(p_ready.sem, 1)

        @block.scalar
        def _(act):
            def exps(n, u, a):
                act.wait_ge(shifted.sem, shifted.at(n + 1))
                if n >= 2:
                    act.wait_ge(p_ready.sem, p_ready.at(n - 1))
                pr = s.prob[n % 2][:, 0:units[u].keys(a)]
                act.activation(pr, pr, ACT.Exp, bias=s.small[:, 8 + n % 2:9 + n % 2],
                               accum_out=s.small[:, 10 + n % 2:11 + n % 2]).then_inc(exp_ready.sem, 1)

            exps(*steps[0])
            for n, u, a in steps:
                if n + 1 < len(steps):
                    exps(*steps[n + 1])
                act.wait_ge(pt_ready.sem, pt_ready.at(n + 1))
                w = units[u].keys(a)
                if a == 0 and u >= 2:
                    act.wait_ge(o_ready.sem, o_ready.at(outs.index((u - 1, 0))))
                n_st, ww = -(-w // P), min(P, w)
                act.activation(s.pt[u % 2][0:ww, 0:n_st, a * P:(a + 1) * P],
                               s.ps[2 + n % 2][0:ww, 0:n_st * P].rearrange("p (s q) -> p s q", s=n_st), ACT.Copy).then_inc(pt_done.sem, 1)
                if a == TT - 1:
                    for m in range(units[u].pieces):
                        o = outs.index((u, m))
                        act.wait_ge(o_ready.sem, o_ready.at(o + 1))
                        row = units[u].row
                        act.activation(units[u].out(m), s.ps[4 + o % 2][row:row + units[u].channels, :], ACT.Copy).then_inc(o_done.sem, 1)
    for c in s.norm_sems:
        c.passed(len(steps))
    for c in s.pair_sems:
        c.passed(len(outs))


def cross_attention(s):
    v = s.view
    mem = v(0, 4).rearrange("p a t -> p (a t)").rearrange("p (k m) -> p k m", k=DT)
    xk = v(4, 4).rearrange("p a t -> p (a t)").rearrange("p (k m) -> p k m", k=DT)
    xv = v(8, 4).rearrange("p a t -> p (a t)").rearrange("p (t c) -> p t c", t=2)
    xq, o = v(12, 8), v(20, 8)
    s.prob = [s.arena[:, (28 + k) * T:(29 + k) * T] for k in range(2)]
    s.pt = [v(30 + 4 * k, 4) for k in range(2)]
    with s.nc.Block() as block:
        @block.sync
        def _(sync):
            sync.dma_start(mem.rearrange("p k m -> p (k m)"), s.I["mem"]).then_inc(s.loaded.sem, 16)
            sync.wait_ge(s.loaded.sem, s.loaded.at(16))
    s.loaded.passed(16)

    def store_v(act, step, t, ps):
        return act.activation(xv[:, t % 2, (t // 2) * 512:(t // 2) * 512 + 512], ps, ACT.Copy)

    linears(s, [
        part("w_xk", lambda k: mem[:, k, :], store(lambda t: xk[:, t, :]), n=MEM),
        part("w_xv", lambda k: mem[:, k, :], store_v, tokens=2),
        part("w_xq", lambda k: s.x[:, k, :], store(lambda t: xq[:, t, :])),
    ])

    def unit(h):
        return attention_unit(
            q=lambda a: [xq[:, 2 * h + m, a * P:(a + 1) * P] for m in range(2)], k=[xk[:, 2 * h + m, :] for m in range(2)],
            keys=lambda a: MEM, table=None, slope=None, ok=None, scale=XHD ** -0.5,
            v=lambda st, m: xv[:, st, h * XHD + m * P:h * XHD + (m + 1) * P], pieces=2, channels=P, row=0, causal=False,
            out=lambda m: o[:, 2 * h + m, :])

    attention(s, [unit(h) for h in range(XH)])
    linears(s, [part("w_xo", lambda k: o[:, k, :], residual(s, ALPHA), by="dve")])
    norm(s, s.x, 8, 8, s.x, v(0, 10), True, 0, s.col("ln2_g"), s.col("ln2_b"))


def conv_glu(s):
    v = s.view
    gated = v(0, FF_TILES)
    up = s.arena[:, 22 * T:22 * T + 4 * (T + 2)].rearrange("p (n t) -> p n t", n=4)
    acc = v(27, 4)
    part_ready, acc_ready, act_ready = s.norm_sems[0:3]
    nc = s.nc
    with nc.Block() as block:
        @block.gpsimd
        def _(pool):
            pool.memset(up[:, :, 0:2], 0.0)

    def evac(dve, step, t, ps):
        odd = evac.turn % 2
        evac.turn += 1
        slot = evac.turn
        src, dst = up[:, odd, :], acc[:, odd, :]
        one = (lambda c: c[:, bass.ds(t, 1)]) if not isinstance(t, int) else (lambda c: c[:, t:t + 1])
        step(dve.tensor_scalar(src[:, 2:2 + T], ps, one(s.col("b_up")), None, ALU.add))
        step(dve.tensor_scalar(dst, src[:, 0:T], one(s.col("ffn_conv0")), None, ALU.mult))
        step(dve.scalar_tensor_tensor(dst, src[:, 1:1 + T], one(s.col("ffn_conv1")), dst, ALU.mult, ALU.add))
        step(dve.scalar_tensor_tensor(dst, src[:, 2:2 + T], one(s.col("ffn_conv2")), dst, ALU.mult, ALU.add))
        return dve.tensor_scalar(gated_raw[odd](t), dst, one(s.col("ffn_conv_b")), None, ALU.add)

    evac.turn = 0
    wide = v(31, FF_TILES)
    half = lambda t: t // 2
    gated_raw = (lambda t: gated[:, half(t), :], lambda t: wide[:, half(t), :])
    linears(s, [part("w_up", lambda k: s.x[:, k, :], evac, by="dve", steps=4)])
    with nc.Block() as block:
        @block.scalar
        def _(act):
            with act.Fori(0, FF_TILES) as t:
                act.activation(gated[:, t, :], gated[:, t, :], ACT.Silu).then_inc(act_ready.sem, 1)

        @block.vector
        def _(dve):
            with dve.Fori(0, FF_TILES) as t:
                dve.wait_ge(act_ready.sem, act_ready.at(t + 1))
                dve.tensor_tensor(gated[:, t, :], gated[:, t, :], wide[:, t, :], ALU.mult)
    act_ready.passed(FF_TILES)
    linears(s, [part("w_down", lambda k: gated[:, k, :], residual(s, ALPHA), by="dve")])
    norm(s, s.x, 8, 8, s.x, v(0, 10), True, 0, s.col("ln3_g"), s.col("ln3_b"))


def store_out(s, out):
    with s.nc.Block() as block:
        @block.sync
        def _(sync):
            sync.dma_start(out, s.xflat).then_inc(s.loaded.sem, 16)
            sync.wait_ge(s.loaded.sem, s.loaded.at(16))
    s.loaded.passed(16)


def build(nc, I, at, out, upto=99):
    s = Names()
    s.nc, s.I, s.next_part, s.tiles, s.slab_end, s.first_slab = nc, I, 0, 0, [], [0]
    for name, _, _ in PLAN:
        s.first_slab.append(s.first_slab[-1] + I[name].shape[0])
    s.x = nc.alloc_sbuf_tensor("x_res", [P, DT, T], F32)[:]
    s.xflat = s.x.rearrange("p k t -> p (k t)")
    s.ring = nc.alloc_sbuf_tensor("weight_ring", [P, RING, SLAB], F32)[:]
    s.base = nc.alloc_sbuf_tensor("base_tables", [P, 4 * P + 2], F32)
    s.par = nc.alloc_sbuf_tensor("params_sb", [P, I["params"].shape[1]], F32)
    s.small = nc.alloc_sbuf_tensor("small", [P, 256], F32)
    s.arena = nc.alloc_sbuf_tensor("arena", [P, 73 * T], F32)
    s.ps = [nc.alloc_psum_tensor(f"bank{b}", [P, T], F32) for b in range(8)]
    s.eye, s.turn, s.causal, s.ones = (s.base[:, k * P:(k + 1) * P] for k in range(4))
    s.eps = [s.base[:, 4 * P + k:4 * P + k + 1] for k in range(2)]
    s.col = lambda name: s.par[:, at[name][0]:at[name][0] + at[name][1]]
    s.view = lambda o, n: s.arena[:, o * T:(o + n) * T].rearrange("p (a t) -> p a t", t=T)
    s.slab_ready = [nc.alloc_semaphore(f"slab_ready{k}") for k in range(RING)]
    names = ("loaded", "tiles_done", "evac_done", "act_chain", "dve_chain", "pool_chain")
    s.loaded, s.tiles_done, s.evac_done, s.act_chain, s.dve_chain, s.pool_chain = (Counter(nc, n) for n in names)
    s.norm_sems = [Counter(nc, f"step{k}_ready") for k in range(6)]
    s.pair_sems = [Counter(nc, f"pair{k}_ready") for k in range(2)]
    s.gathered = [Counter(nc, f"gathered{k}") for k in range(2 * GATHER)]
    s.held = nc.alloc_semaphore("held")
    s.one_sem = [Counter(nc, "conv_ready")]
    stages = STAGES[:upto]
    load_start(s)
    for stage in stages:
        stage(s)
    store_out(s, out)


def second_inputs_projected(s):
    v = s.view
    s.n = v(0, 8)
    norm(s, s.x, 8, 8, s.n, v(8, 10), False, 1, s.col("norm_mix"))
    s.ax, s.ab, s.ry = v(8, 8), v(25, 8), v(44, RT)
    s.cx = s.arena[:, 16 * T:16 * T + 8 * (T + 2)].rearrange("p (a t) -> p a t", a=8)
    s.rx = s.arena[:, 33 * T:33 * T + RT * (T + 3)].rearrange("p (a t) -> p a t", a=RT)
    with s.nc.Block() as block:
        @block.gpsimd
        def _(pool):
            pool.memset(s.cx[:, :, 0:2], 0.0)
            pool.memset(s.rx[:, :, 0:3], 0.0)
    n = lambda k: s.n[:, k, :]

    linears(s, [part("w2_ax", n, store(lambda t: s.ax[:, t, :]))])
    linears(s, [
        part("w2_ac", n, lambda dve, step, t, ps: dve.tensor_tensor(s.cx[:, t, 2:2 + T], ps, s.ax[:, t, :], ALU.mult), by="dve"),
        part("w2_ab", n, store(lambda t: s.ab[:, t, :])),
        part("w2_rx", n, store(lambda t: s.rx[:, t, 3:3 + T])),
        part("w2_ry", n, store(lambda t: s.ry[:, t, :], ACT.Gelu_apprx_tanh)),
    ])


def second_convolutions(s):
    s.rc = s.view(54, RT)
    cols = [s.small[:, 16 + 16 * k:16 + 16 * k + RT] for k in range(6)]
    neg_lam, s.rate, e, w, d, s.neg_rate = cols
    with s.nc.Block() as block:
        @block.vector
        def _(dve):
            step = Chain(dve, s.dve_chain)
            taps = [s.col(f"conv_a{k}") for k in range(3)]
            with step.loop(8, 4) as t:
                step(causal_conv(s, dve, step, s.ax[:, t, :], lambda k: s.cx[:, t, k:k + T], taps, bass.ds(t, 1)))
                step(dve.tensor_tensor(s.ab[:, t, :], s.ab[:, t, :], s.ax[:, t, :], ALU.mult))
            taps = [s.col(f"rnn_conv{k}") for k in range(4)]
            with step.loop(RT, 5) as t:
                step(causal_conv(s, dve, step, s.rc[:, t, :], lambda k: s.rx[:, t, k:k + T], taps, bass.ds(t, 1)))
                step(dve.tensor_scalar(s.rc[:, t, :], s.rc[:, t, :], s.col("rnn_conv_b")[:, bass.ds(t, 1)], None, ALU.add))
            step(dve.tensor_scalar(neg_lam, s.col("lru_lambda"), -1.0, None, ALU.mult))
    softplus_rows(s, [(neg_lam, s.rate, e, w, d, False)])
    with s.nc.Block() as block:
        @block.vector
        def _(dve):
            step = Chain(dve, s.dve_chain)
            step(dve.tensor_scalar(s.neg_rate, s.rate, -8.0, None, ALU.mult))
            step(dve.tensor_scalar(s.rate, s.rate, 8.0, None, ALU.mult))


def recurrence(s):
    v = s.view
    r, gate, a = v(33, RT), v(8, RT), v(8, RT)
    rc = lambda k: s.rc[:, k, :]
    linears(s, [
        part("w2_rg", rc, store(lambda t: r[:, t, :], ACT.Sigmoid, lambda t: s.col("b_rg")[:, t:t + 1]), block_diag=True),
        part("w2_ig", rc, store(lambda t: gate[:, t, :], ACT.Sigmoid, lambda t: s.col("b_ig")[:, t:t + 1]), block_diag=True),
    ])
    square = v(64, 2)
    gated, a_ready, tanh_ready, room_ready, root_ready, _ = s.norm_sems
    with s.nc.Block() as block:
        @block.scalar
        def _(act):
            act.wait_ge(gated.sem, gated.at(1))
            for t in range(RT):
                act.activation(a[:, t, :], r[:, t, :], ACT.Exp, scale=s.neg_rate[:, t:t + 1]).then_inc(a_ready.sem, 1)
            for t in range(RT):
                act.activation(r[:, t, :], r[:, t, :], ACT.Tanh, scale=s.rate[:, t:t + 1]).then_inc(tanh_ready.sem, 1)
            for t in range(RT):
                act.wait_ge(room_ready.sem, room_ready.at(t + 1))
                act.activation(r[:, t, :], r[:, t, :], ACT.Sqrt).then_inc(root_ready.sem, 1)

        @block.vector
        def _(dve):
            step = Chain(dve, s.dve_chain)
            dve.tensor_tensor(s.rc, s.rc, gate, ALU.mult).then_inc(gated.sem, 1)
            for t in range(RT):
                sq = square[:, t % 2, :]
                dve.wait_ge(a_ready.sem, a_ready.at(t + 1))
                step(dve.tensor_tensor(sq, a[:, t, :], a[:, t, :], ALU.mult))
                dve.wait_ge(tanh_ready.sem, tanh_ready.at(t + 1))
                step(dve.scalar_tensor_tensor(r[:, t, :], sq, 1.0, r[:, t, :], ALU.add, ALU.mult))
                dve.tensor_scalar(r[:, t, :], r[:, t, :], 0.0, None, ALU.max).then_inc(room_ready.sem, 1)
            dve.wait_ge(gated.sem, gated.at(1))
            for t in range(RT):
                dve.wait_ge(root_ready.sem, root_ready.at(t + 1))
                step(dve.tensor_tensor(s.rc[:, t, :], s.rc[:, t, :], r[:, t, :], ALU.mult))
                step(dve.tensor_tensor_scan(r[:, t, :], a[:, t, :], s.rc[:, t, :], 0.0, ALU.mult, ALU.add))
                dve.tensor_tensor(s.ry[:, t, :], s.ry[:, t, :], r[:, t, :], ALU.mult)
    gated.passed(1)
    for c in (a_ready, tanh_ready, room_ready, root_ready):
        c.passed(RT)


def second_mixer(s):
    v = s.view
    second_inputs_projected(s)
    second_convolutions(s)
    recurrence(s)
    ga, gb, merged = v(54, 8), v(62, 8), v(8, 8)
    n = lambda k: s.n[:, k, :]
    linears(s, [
        part("w2_ga", n, store(lambda t: ga[:, t, :], ACT.Sigmoid)),
        part("w2_gb", n, store(lambda t: gb[:, t, :], ACT.Sigmoid)),
    ])

    def add_b(dve, step, t, ps):
        step(dve.tensor_tensor(gb[:, t, :], ps, gb[:, t, :], ALU.mult))
        return dve.tensor_tensor(merged[:, t, :], merged[:, t, :], gb[:, t, :], ALU.add)

    linears(s, [
        part("w2_out_a", lambda k: s.ab[:, k, :], lambda dve, step, t, ps: dve.tensor_tensor(merged[:, t, :], ps, ga[:, t, :], ALU.mult), by="dve"),
        part("w2_out_b", lambda k: s.ry[:, k, :], add_b, by="dve", steps=1),
    ])
    linears(s, [part("w2_o", lambda k: merged[:, k, :], residual(s), by="dve")])


def turn_tiles(s, src, dst):
    ready, taken = s.pair_sems
    with s.nc.Block() as block:
        @block.tensor
        def _(pe):
            for n in range(2 * TT):
                a, half = n // 2, n % 2
                if n >= 2:
                    pe.wait_ge(taken.sem, taken.at(n - 1))
                for u in range(4):
                    mm = pe.transpose(s.ps[n % 2][:, u * P:(u + 1) * P], src[:, half * 4 + u, a * P:(a + 1) * P], s.eye)
                mm.then_inc(ready.sem, 1)

        @block.vector
        def _(dve):
            for n in range(2 * TT):
                dve.wait_ge(ready.sem, ready.at(n + 1))
                dve.tensor_copy(dst[:, n // 2, (n % 2) * 512:(n % 2) * 512 + 512], s.ps[n % 2][:]).then_inc(taken.sem, 1)
    ready.passed(2 * TT)
    taken.passed(2 * TT)


def choose_experts(s):
    v = s.view
    q = v(8, 16)
    score = lambda a, c: s.ps[4 * (a % 2) + c // 4][:, (c % 4) * P:(c % 4 + 1) * P]
    flat = lambda x: x.rearrange("p h k -> p (h k)")
    keys = s.arena[:, 24 * T:28 * T].rearrange("p (c n) -> p c n", n=NKEYS)
    f = lambda o, n: s.arena[:, o:o + n]
    o = 44 * T
    val = f(o, 256).rearrange("p (c k) -> p c k", k=PEER_K)
    ind = f(o + 256, 256).bitcast(U32).rearrange("p (c k) -> p c k", k=PEER_K)
    indf = f(o + 512, 256).rearrange("p (c k) -> p c k", k=PEER_K)
    rest = [f(o + 768 + 256 * k, 256) for k in range(2)]
    cand, number = f(o + 1280, 256), f(o + 1536, 256)
    junk = f(36 * T, PEER_K * 256).rearrange("p (k n) -> p k n", k=PEER_K)
    top = [f(o + 2048 + 1024 * k, SLOTS).rearrange("p (h k) -> p h k", k=PEER_K) for k in range(2)]
    pos = f(o + 2176, PEER_K).bitcast(U32)
    posf = f(o + 2192, PEER_K)
    chosen = f(o + 2304, SLOTS)
    total = f(o + 2432, PEER_H)
    iota = f(o + 2560, 256)
    sc_ready, sorted_, shifted, exp_ready, _, _ = s.norm_sems
    with s.nc.Block() as block:
        @block.sync
        def _(sync):
            sync.dma_start(keys.rearrange("p c n -> p (c n)"), s.I["keys"]).then_inc(s.loaded.sem, 16)
            sync.dma_start(iota, s.I["iota"]).then_inc(s.loaded.sem, 16)

        @block.tensor
        def _(pe):
            pe.wait_ge(s.loaded.sem, s.loaded.at(32))
            for a in range(TT):
                if a >= 2:
                    pe.wait_ge(sorted_.sem, sorted_.at(a - 1))
                for c in range(2 * PEER_H):
                    mm = pe.matmul(score(a, c), q[:, c, a * P:(a + 1) * P], keys[:, c, :], start=True, stop=True)
                mm.then_inc(sc_ready.sem, 1)

        @block.scalar
        def _(act):
            for a in range(TT):
                act.wait_ge(shifted.sem, shifted.at(a + 1))
                act.activation(flat(top[a % 2]), flat(top[a % 2]), ACT.Exp).then_inc(exp_ready.sem, 1)

        @block.vector
        def _(dve):
            step = Chain(dve, s.dve_chain)
            dve.wait_ge(s.loaded.sem, s.loaded.at(32))

            def best(values, numbers, src, spare):
                step(dve.max(values[:, 0:8], src))
                dve.max_index(numbers[:, 0:8], values[:, 0:8], src)
                step(dve.match_replace(spare, values[:, 0:8], src, -3.0e38))
                step(dve.max(values[:, 8:16], spare))
                step(dve.max_index(numbers[:, 8:16], values[:, 8:16], spare))

            def weights(a):
                dve.wait_ge(exp_ready.sem, exp_ready.at(a + 1))
                t = top[a % 2]
                step(dve.tensor_reduce(total, t, AX.X, ALU.add))
                step(dve.reciprocal(total, total))
                step(dve.tensor_tensor(s.gate[:, a * SLOTS:(a + 1) * SLOTS].rearrange("p (h k) -> p h k", k=PEER_K), t,
                                       total.unsqueeze(2).broadcast_to([P, PEER_H, PEER_K]), ALU.mult))

            for a in range(TT):
                dve.wait_ge(sc_ready.sem, sc_ready.at(a + 1))
                t = top[a % 2]
                for h in range(PEER_H):
                    for c in (2 * h, 2 * h + 1):
                        best(val[:, c, :], ind[:, c, :], score(a, c), rest[0][:, 0:NKEYS])
                    step(dve.tensor_copy(indf[:, 2 * h:2 * h + 2, :], ind[:, 2 * h:2 * h + 2, :]))
                    first = lambda x: x[:, 2 * h, :].unsqueeze(2).broadcast_to([P, PEER_K, PEER_K])
                    second = lambda x: x[:, 2 * h + 1, :].unsqueeze(1).broadcast_to([P, PEER_K, PEER_K])
                    grid = lambda x: x.rearrange("p (i j) -> p i j", i=PEER_K)
                    dve.tensor_tensor(grid(cand), first(val), second(val), ALU.add)
                    step(dve.scalar_tensor_tensor(grid(number), first(indf), float(NKEYS), second(indf), ALU.mult, ALU.add))
                    best(t[:, h, :], pos, cand, rest[1])
                    step(dve.tensor_copy(posf, pos))
                    for k in range(PEER_K):
                        ins = dve.scalar_tensor_tensor(junk[:, k, :], iota, posf[:, k:k + 1], number, ALU.is_equal, ALU.mult,
                                                       accum_out=chosen[:, h * PEER_K + k:h * PEER_K + k + 1])
                    step(ins)
                dve.tensor_copy(posf[:, 0:PEER_H], t[:, :, 0]).then_inc(sorted_.sem, 1)
                dve.wait_ge(sorted_.sem, sorted_.at(a + 1))
                dve.tensor_copy(s.expert[:, a * SLOTS:(a + 1) * SLOTS], chosen)
                dve.tensor_tensor(t, t, posf[:, 0:PEER_H].unsqueeze(2).broadcast_to([P, PEER_H, PEER_K]), ALU.subtract).then_inc(shifted.sem, 1)
                if a:
                    weights(a - 1)
            weights(TT - 1)
    s.loaded.passed(32)
    for c in (sc_ready, sorted_, shifted, exp_ready):
        c.passed(TT)


def experts(s, table, use, in_turn):
    place = s.small[:, 192:192 + 2 * GATHER].bitcast(U32)
    numbers_ready, used = s.pair_sems
    body = 2 * GATHER
    per_tile = SLOTS // body
    turns = TT * per_tile
    with s.nc.Block() as block:
        @block.scalar
        def _(act):
            def place_numbers(turn, half):
                act.activation(place[:, half * GATHER:(half + 1) * GATHER],
                               s.expert[:, bass.ds(turn * body + half * GATHER, GATHER)], ACT.Copy).then_inc(numbers_ready.sem, 1)

            for half in range(2):
                place_numbers(0, half)
            with act.Fori(1, turns) as turn:
                for half in range(2):
                    for j in range(half * GATHER, (half + 1) * GATHER):
                        act.wait_ge(s.gathered[j].sem, s.gathered[j].at(16 * turn))
                    act.sem_inc(s.held, 1)
                    place_numbers(turn, half)

        @block.gpsimd
        def _(pool):
            def gather(turn, j):
                if j % GATHER == 0:
                    pool.wait_ge(numbers_ready.sem, numbers_ready.at(2 * turn + j // GATHER + 1))
                if not isinstance(turn, int):
                    pool.wait_ge(used.sem, used.at(body * turn - body + j + 1))
                    pool.sem_inc(s.held, 1)
                pool.indirect_dma_start(out=s.rows[:, j, :], out_offset=None, in_=table,
                                        in_offset=bass.IndirectOffsetOnAxis(ap=place[:, j:j + 1], axis=0)).then_inc(s.gathered[j].sem, 16)

            for j in range(body):
                gather(0, j)
            with pool.Fori(1, turns) as turn:
                for j in range(body):
                    gather(turn, j)

        @block.vector
        def _(dve):
            with dve.Fori(0, TT) as a:
                with dve.Fori(0, per_tile) as b:
                    for j in range(body):
                        slot = a * SLOTS + b * body + j
                        dve.wait_ge(s.gathered[j].sem, s.gathered[j].at((a * per_tile + b + 1) * 16))
                        if in_turn:
                            dve.wait_ge(used.sem, used.at(slot))
                        use(dve, a, slot, s.rows[:, j, :]).then_inc(used.sem, 1)
    numbers_ready.passed(2 * turns)
    used.passed(body * turns)
    for c in s.gathered:
        c.passed(16 * turns)


def peer(s):
    v = s.view
    n, q = v(0, 8), v(8, 16)
    tokens = lambda o: v(o, 8).rearrange("p a t -> p (a t)").rearrange("p (a c) -> p a c", a=TT)
    n_tok, y = tokens(28), tokens(0)
    s.rows = v(36, 32).rearrange("p a t -> p (a t)").rearrange("p (j d) -> p j d", d=D)
    s.expert = s.arena[:, 70 * T:71 * T].bitcast(U32)
    s.gate, act_ = s.arena[:, 71 * T:72 * T], s.arena[:, 72 * T:73 * T]
    norm(s, s.x, 8, 8, n, v(8, 10), False, 1, s.col("norm_ffn"))
    linears(s, [part("w2_q", lambda k: n[:, k, :], store(lambda t: q[:, t, :]))])
    turn_tiles(s, n, n_tok)
    choose_experts(s)

    def dot(dve, a, slot, row):
        return dve.scalar_tensor_tensor(row, row, 1.0, n_tok[:, a, :], ALU.mult, ALU.mult, accum_out=act_[:, bass.ds(slot, 1)])

    experts(s, s.I["expert_u"], dot, False)
    gelu_ready, cleared = s.pair_sems
    with s.nc.Block() as block:
        @block.gpsimd
        def _(pool):
            pool.memset(y, 0.0)

        @block.scalar
        def _(act):
            act.activation(act_, act_, ACT.Gelu_apprx_tanh).then_inc(gelu_ready.sem, 1)

        @block.vector
        def _(dve):
            dve.wait_ge(gelu_ready.sem, gelu_ready.at(1))
            dve.tensor_tensor(s.gate, s.gate, act_, ALU.mult)
    gelu_ready.passed(1)

    def add(dve, a, slot, row):
        return dve.scalar_tensor_tensor(y[:, a, :], row, s.gate[:, bass.ds(slot, 1)], y[:, a, :], ALU.mult, ALU.add)

    experts(s, s.I["expert_v"], add, True)

    ready, taken = s.pair_sems
    with s.nc.Block() as block:
        @block.tensor
        def _(pe):
            for k in range(DT):
                if k >= 2:
                    pe.wait_ge(taken.sem, taken.at(k - 1))
                for a in range(TT):
                    mm = pe.transpose(s.ps[k % 2][:, a * P:(a + 1) * P], y[:, a, k * P:(k + 1) * P], s.eye)
                mm.then_inc(ready.sem, 1)

        @block.vector
        def _(dve):
            for k in range(DT):
                dve.wait_ge(ready.sem, ready.at(k + 1))
                dve.tensor_tensor(s.x[:, k, :], s.x[:, k, :], s.ps[k % 2][:], ALU.add).then_inc(taken.sem, 1)
    ready.passed(DT)
    taken.passed(DT)
    norm(s, s.x, 8, 8, s.x, v(10, 10), False, 1, s.col("norm_final"))


def modulation(s):
    mod = s.small[:, 64:64 + 6 * DT]
    cond = s.small[:, 120:120 + DT]
    silu_ready, = s.one_sem
    with s.nc.Block() as block:
        @block.sync
        def _(sync):
            sync.dma_start(cond, s.I["c"]).then_inc(s.loaded.sem, 16)

        @block.scalar
        def _(act):
            act.wait_ge(s.loaded.sem, s.loaded.at(16))
            act.activation(cond, cond, ACT.Silu)
    s.loaded.passed(16)
    linears(s, [part("w3_ada", lambda k: cond[:, k:k + 1],
                     store(lambda t: mod[:, bass.ds(t, 1)], ACT.Identity, lambda t: s.col("b_ada")[:, bass.ds(t, 1)]), n=1)])
    s.shift1, s.gain1, s.gate1, s.shift2, s.gain2, s.gate2 = (mod[:, k * DT:(k + 1) * DT] for k in range(6))
    with s.nc.Block() as block:
        @block.vector
        def _(dve):
            dve.scalar_tensor_tensor(s.gain1, s.gain1, 1.0, s.col("g_norm1"), ALU.add, ALU.mult)
            dve.scalar_tensor_tensor(s.gain2, s.gain2, 1.0, s.col("g_norm2"), ALU.add, ALU.mult)


def third_projection(s):
    v = s.view
    s.h = v(0, 8)
    norm(s, s.x, 8, 8, s.h, v(8, 10), False, 1, s.gain1, s.shift1)
    s.gu, s.gv, s.mv, s.mo, s.nq, s.kvc, s.ksw = v(8, 4), v(12, 4), v(25, 4), v(29, 4), v(35, 4), v(39, 2), v(41, 4)
    s.mqk = s.arena[:, 16 * T:16 * T + 8 * (T + 3)].rearrange("p (a t) -> p a t", a=8)

    s.vsw = s.arena[:, 45 * T:47 * T].rearrange("p (a c) -> p a c", a=TT)
    s.mi, s.mf, s.ng = s.arena[0:4, 33 * T:34 * T], s.arena[0:4, 34 * T:35 * T], s.arena[0:24, 47 * T:48 * T]
    with s.nc.Block() as block:
        @block.gpsimd
        def _(pool):
            pool.memset(s.mqk[:, :, 0:3], 0.0)
    h = lambda k: s.h[:, k, :]
    linears(s, [
        part("w3_gu", h, store(lambda t: s.gu[:, t, :], ACT.Gelu_apprx_tanh)),
        part("w3_gv", h, store(lambda t: s.gv[:, t, :], ACT.Gelu_apprx_tanh)),
        part("w3_mqk", h, store(lambda t: s.mqk[:, t, 3:3 + T])),
        part("w3_mv", h, store(lambda t: s.mv[:, t, :]), tokens=TT),
        part("w3_mo", h, store(lambda t: s.mo[:, t, :], ACT.Sigmoid)),
        part("w3_mi", h, store(lambda t: s.mi, ACT.Identity, lambda t: s.col("ml_bi")[0:4, :]), tile=4),
        part("w3_mf", h, store(lambda t: s.mf, ACT.Identity, lambda t: s.col("ml_bf")[0:4, :]), tile=4),
        part("w3_nq", h, store(lambda t: s.nq[:, t, :], scale=NSA_DH ** -0.5)),
        part("w3_kvc", h, store(lambda t: s.kvc[:, t, :])),
        part("w3_ksw", h, store(lambda t: s.ksw[:, t, :])),
        part("w3_vsw", h, store(lambda t: s.vsw[:, t, :]), tokens=TT),
        part("w3_ng", h, store(lambda t: s.ng, ACT.Sigmoid), tile=24),
    ])


def spatial_gating(s):
    v = s.view
    norm(s, s.gv, 4, 4, s.gv, v(56, 6), True, 1, s.col("gm_ln_g"), s.col("gm_ln_b"))
    by_token = v(56, 4)
    w = s.arena[:, 60 * T:61 * T].rearrange("p (g t) -> p g t", g=4)
    b = s.arena[:, 61 * T:62 * T].rearrange("p (g t) -> p g t", g=4)
    tmp = v(62, 4)
    turned, taken, masked, mixed, _, _ = s.norm_sems
    with s.nc.Block() as block:
        @block.sync
        def _(sync):
            sync.dma_start(w.rearrange("p g t -> p (g t)"), s.I["gm_w"]).then_inc(s.loaded.sem, 16)
            sync.dma_start(b.rearrange("p g t -> p (g t)"), s.I["gm_b"]).then_inc(s.loaded.sem, 16)

        @block.tensor
        def _(pe):
            for a in range(TT):
                for g in range(4):
                    mm = pe.transpose(s.ps[a][:, g * P:(g + 1) * P], s.gv[:, g, a * P:(a + 1) * P], s.eye)
                mm.then_inc(turned.sem, 1)
            pe.wait_ge(taken.sem, taken.at(TT))
            pe.wait_ge(masked.sem, masked.at(1))
            for g in range(4):
                for a in range(TT):
                    mm = pe.matmul(s.ps[4 + g][:, a * P:(a + 1) * P], by_token[:, a, g * P:(g + 1) * P], w[:, g, :], start=True, stop=True)
                mm.then_inc(mixed.sem, 1)

        @block.vector
        def _(dve):
            step = Chain(dve, s.dve_chain)
            dve.wait_ge(s.loaded.sem, s.loaded.at(32))
            dve.tensor_tensor(w, w, s.causal.unsqueeze(1).broadcast_to([P, 4, P]), ALU.mult).then_inc(masked.sem, 1)
            for a in range(TT):
                dve.wait_ge(turned.sem, turned.at(a + 1))
                dve.tensor_copy(by_token[:, a, :], s.ps[a][:]).then_inc(taken.sem, 1)
            for g in range(4):
                dve.wait_ge(mixed.sem, mixed.at(g + 1))
                step(dve.tensor_tensor(tmp[:, g, :].rearrange("p (a t) -> p a t", a=TT), s.ps[4 + g][:].rearrange("p (a t) -> p a t", a=TT),
                                       b[:, g, :].unsqueeze(1).broadcast_to([P, TT, P]), ALU.add))
                dve.tensor_tensor(s.gu[:, g, :], s.gu[:, g, :], tmp[:, g, :], ALU.mult)
    s.loaded.passed(32)
    for c, n in ((turned, TT), (taken, TT), (masked, 1), (mixed, 4)):
        c.passed(n)


def mlstm(s):
    v = s.view
    qk = v(48, 8)
    s.yb = v(12, 4)
    row = lambda k: s.arena[0:4, k * T:(k + 1) * T]
    lf, e, w, d, F, g, M, m = (row(56 + k) for k in range(8))
    g_col = s.small[:, 128:144].rearrange("p (a h) -> p a h", a=TT)
    att = s.arena[:, 64 * T:64 * T + SEG_LEN]
    floor, rec = s.arena[:, 67 * T:68 * T], s.arena[:, 68 * T:69 * T]
    conv_ready, = s.one_sem
    with s.nc.Block() as block:
        @block.vector
        def _(dve):
            step = Chain(dve, s.dve_chain)
            taps = [s.col(f"ml_conv{k}") for k in range(4)]
            with step.loop(8, 3) as t:
                causal_conv(s, dve, step, qk[:, t, :], lambda k: s.mqk[:, t, k:k + T], taps, bass.ds(t, 1)).then_inc(conv_ready.sem, 1)

        @block.scalar
        def _(act):
            with act.Fori(0, 8) as t:
                act.wait_ge(conv_ready.sem, conv_ready.at(t + 1))
                act.sem_inc(s.held, 1)
                act.activation(qk[:, t, :], qk[:, t, :], ACT.Silu, bias=s.col("ml_conv_b")[:, bass.ds(t, 1)])
    conv_ready.passed(8)
    softplus_rows(s, [(s.mf, lf, e, w, d, True)])
    with s.nc.Block() as block:
        @block.vector
        def _(dve):
            step = Chain(dve, s.dve_chain)
            step(dve.memset(w, 1.0))
            step(dve.tensor_tensor_scan(F, w, lf, 0.0, ALU.mult, ALU.add))
            step(dve.tensor_tensor(g, s.mi, F, ALU.subtract))
            step(dve.tensor_tensor_scan(M, w, g, 0.0, ALU.mult, ALU.max))
            step(dve.tensor_tensor(m, F, M, ALU.add))
    cols_ready, = s.one_sem
    m_ready, s_ready, exp_ready, att_ready, sums_ready, done = s.norm_sems
    diff_ready, abs_ready = s.pair_sems
    heads = 4
    with s.nc.Block() as block:
        @block.tensor
        def _(pe):
            for a in range(TT):
                mm = pe.transpose(s.ps[7][:, a * heads:(a + 1) * heads], g[:, a * P:(a + 1) * P], s.eye[0:heads, 0:heads])
            mm.then_inc(cols_ready.sem, 1)
            for h in range(heads):
                if h:
                    pe.wait_ge(exp_ready.sem, exp_ready.at(h))
                pick = s.eye[0:heads, h:h + 1].broadcast_to([heads, P])
                pe.matmul(s.ps[0][:], pick, M, start=True, stop=True)
                pe.matmul(s.ps[1][:], pick, m, start=True, stop=True).then_inc(m_ready.sem, 1)
                if h:
                    pe.wait_ge(att_ready.sem, att_ready.at(h))
                for a in range(TT):
                    mm = pe.matmul(s.ps[2 + a][:, 0:seg_width(a)], qk[:, heads + h, a * P:(a + 1) * P], qk[:, h, a * P:T], start=True, stop=True)
                mm.then_inc(s_ready.sem, 1)
                pe.wait_ge(att_ready.sem, att_ready.at(h + 1))
                if h:
                    pe.wait_ge(done.sem, done.at(h))
                for a in range(TT):
                    seg = att[:, SEG[a]:SEG[a] + seg_width(a)]
                    pe.matmul(s.ps[6][:, a * P:T], s.mv[:, a, h * P:(h + 1) * P], seg, start=a == 0, stop=a == TT - 1, skip_group_check=True)
                    mm = pe.matmul(s.ps[7][:, a * P:T], s.ones, seg, start=a == 0, stop=a == TT - 1, skip_group_check=True)
                mm.then_inc(sums_ready.sem, 1)

        @block.scalar
        def _(act):
            for h in range(heads):
                act.wait_ge(m_ready.sem, m_ready.at(h + 1))
                if h:
                    act.wait_ge(done.sem, done.at(h))
                act.activation(floor, s.ps[1][:], ACT.Exp, scale=-1.0)
                act.wait_ge(diff_ready.sem, diff_ready.at(h + 1))
                act.activation(att, att, ACT.Exp, scale=-1.0).then_inc(exp_ready.sem, 1)
                act.wait_ge(sums_ready.sem, sums_ready.at(h + 1))
                act.activation(rec, s.ps[7][:], ACT.Abs).then_inc(abs_ready.sem, 1)

        @block.vector
        def _(dve):
            step = Chain(dve, s.dve_chain)
            dve.wait_ge(cols_ready.sem, cols_ready.at(1))
            step(dve.tensor_copy(g_col.rearrange("p a h -> p (a h)"), s.ps[7][:, 0:TT * heads]))
            for h in range(heads):
                dve.wait_ge(m_ready.sem, m_ready.at(h + 1))
                if h:
                    dve.wait_ge(sums_ready.sem, sums_ready.at(h))
                for a in range(TT):
                    ins = dve.tensor_scalar(att[:, SEG[a]:SEG[a] + seg_width(a)], s.ps[0][:, a * P:T], g_col[:, a, h:h + 1], 0.0, ALU.subtract, ALU.max)
                ins.then_inc(diff_ready.sem, 1)
                dve.wait_ge(exp_ready.sem, exp_ready.at(h + 1))
                dve.wait_ge(s_ready.sem, s_ready.at(h + 1))
                for a in range(TT):
                    seg = att[:, SEG[a]:SEG[a] + seg_width(a)]
                    ins = dve.scalar_tensor_tensor(seg, s.ps[2 + a][:, 0:seg_width(a)], P ** -0.5, seg, ALU.mult, ALU.mult)
                step(ins)
                for a in range(TT):
                    seg = att[:, SEG[a]:SEG[a] + P]
                    ins = dve.tensor_tensor(seg, seg, s.causal, ALU.mult)
                ins.then_inc(att_ready.sem, 1)
                dve.wait_ge(abs_ready.sem, abs_ready.at(h + 1))
                step(dve.tensor_tensor(rec, rec, floor, ALU.max))
                step(dve.reciprocal(rec, rec))
                dve.tensor_tensor(s.yb[:, h, :], s.ps[6][:], rec, ALU.mult).then_inc(done.sem, 1)
    cols_ready.passed(1)
    for c in s.norm_sems + s.pair_sems:
        c.passed(heads)
    norm(s, s.yb, 4, 1, s.yb, v(56, 3), True, 1, s.col("ml_norm"), None, s.mo)


def compress(s):
    v = s.view
    blocks = [s.arena[:, (48 + 2 * k) * T:(48 + 2 * k) * T + CMP_BLOCK * N_CMP].rearrange("p (i n) -> p i n", i=CMP_BLOCK) for k in range(2)]
    phi1 = [s.arena[:, (52 + 4 * k) * T:(56 + 4 * k) * T].rearrange("p (i e) -> p i e", i=CMP_BLOCK) for k in range(2)]
    phi_k2, phi_v2 = s.arena[0:64, 60 * T:60 * T + 128], s.arena[0:64, 60 * T + 128:60 * T + 192]
    hidden = s.arena[0:64, 61 * T:61 * T + 4 * N_CMP].rearrange("p (c n) -> p c n", c=4)
    s.k_cmp = s.arena[:, 62 * T:62 * T + 2 * N_CMP].rearrange("p (g n) -> p g n", g=2)
    s.v_cmp = s.arena[0:N_CMP, 63 * T:63 * T + 128].rearrange("p (g e) -> p g e", g=2)
    blocks_ready, summed, hidden_ready, second_ready, _, _ = s.norm_sems
    with s.nc.Block() as block:
        @block.sync
        def _(sync):
            for dst, src in ((phi1[0].rearrange("p i e -> p (i e)"), "phi_k1"), (phi1[1].rearrange("p i e -> p (i e)"), "phi_v1"),
                             (phi_k2, "phi_k2"), (phi_v2, "phi_v2")):
                sync.dma_start(dst, s.I[src]).then_inc(s.loaded.sem, 16)

        @block.vector
        def _(dve):
            for k, pe_name in enumerate(("pe_k", "pe_v")):
                tokens = s.kvc[:, k, :].rearrange("p (m l) -> p l m", l=CMP_STRIDE)
                for hi in range(2):
                    part_ = slice(hi * CMP_STRIDE, (hi + 1) * CMP_STRIDE)
                    ins = dve.tensor_tensor(blocks[k][:, part_, :], tokens[:, :, hi:hi + N_CMP],
                                            s.col(pe_name)[:, part_].unsqueeze(2).broadcast_to([P, CMP_STRIDE, N_CMP]), ALU.add)
            ins.then_inc(blocks_ready.sem, 1)
            dve.wait_ge(second_ready.sem, second_ready.at(1))
            for g in range(2):
                dve.tensor_copy(s.k_cmp[:, g, :], s.ps[4 + g][:, 0:N_CMP])
                dve.tensor_copy(s.v_cmp[:, g, :], s.ps[6 + g][0:N_CMP, 0:64])

        @block.tensor
        def _(pe):
            pe.wait_ge(s.loaded.sem, s.loaded.at(64))
            pe.wait_ge(blocks_ready.sem, blocks_ready.at(1))
            for k in range(2):
                for g in range(2):
                    lo = g * 64
                    for i in range(CMP_BLOCK):
                        mm = pe.matmul(s.ps[2 * k + g][0:64, 0:N_CMP], phi1[k][lo:lo + 64, i, :], blocks[k][lo:lo + 64, i, :],
                                       start=i == 0, stop=i == CMP_BLOCK - 1)
            mm.then_inc(summed.sem, 1)
            pe.wait_ge(hidden_ready.sem, hidden_ready.at(1))
            for g in range(2):
                pe.matmul(s.ps[4 + g][:, 0:N_CMP], phi_k2, hidden[:, g, :], start=True, stop=True)
                mm = pe.matmul(s.ps[6 + g][0:N_CMP, 0:64], hidden[:, 2 + g, :], phi_v2, start=True, stop=True)
            mm.then_inc(second_ready.sem, 1)

        @block.scalar
        def _(act):
            act.wait_ge(summed.sem, summed.at(1))
            for c in range(4):
                ins = act.activation(hidden[:, c, :], s.ps[c][0:64, 0:N_CMP], ACT.Gelu_apprx_tanh)
            ins.then_inc(hidden_ready.sem, 1)
    s.loaded.passed(64)
    for c in (blocks_ready, summed, hidden_ready, second_ready):
        c.passed(1)


def sparse_attention(s):
    v = s.view
    compress(s)
    o = v(16, 12)
    s.prob = [s.arena[:, (64 + k) * T:(65 + k) * T] for k in range(2)]
    s.pt = [v(48 + 4 * k, 4) for k in range(2)]
    alibi = s.arena[:, 56 * T:57 * T]
    dist, ok = (s.arena[:, (57 + k) * T:(57 + k) * T + TT * N_CMP].rearrange("p (a n) -> p a n", a=TT) for k in range(2))
    sel = s.arena[0:24, 59 * T:62 * T].rearrange("p (c q) -> p c q", q=P)
    with s.nc.Block() as block:
        @block.sync
        def _(sync):
            for dst, src in ((alibi, "alibi"), (dist.rearrange("p a n -> p (a n)"), "cmp_dist"), (ok.rearrange("p a n -> p (a n)"), "cmp_ok"),
                             (sel.rearrange("p c q -> p (c q)"), "gate_sel")):
                sync.dma_start(dst, s.I[src]).then_inc(s.loaded.sem, 16)
            sync.wait_ge(s.loaded.sem, s.loaded.at(64))
    s.loaded.passed(64)

    def unit(h, branch):
        lo, g = (h % 2) * 64, h // 4
        common = dict(q=lambda a: [s.nq[lo:lo + 64, h // 2, a * P:(a + 1) * P]], slope=2.0 ** -(h + 1.0), scale=1.0, pieces=1, channels=64,
                      row=lo, out=lambda m: o[lo:lo + 64, branch * 4 + h // 2, :])
        if branch == 0:
            return attention_unit(k=[s.k_cmp[lo:lo + 64, g, :]], keys=lambda a: N_CMP, table=lambda a: dist[:, a, :], ok=lambda a: ok[:, a, :],
                                   v=lambda st, m: s.v_cmp[:, g, :], causal=False, **common)
        return attention_unit(k=[s.ksw[lo:lo + 64, 2 * (branch - 1) + g, :]], keys=lambda a: (a + 1) * P,
                               table=lambda a: alibi[:, (TT - 1 - a) * P:T], ok=None,
                               v=lambda st, m: s.vsw[:, st, (branch - 1) * P + g * 64:(branch - 1) * P + g * 64 + 64], causal=True, **common)

    attention(s, [unit(h, b) for h in range(NSA_H) for b in range(3)])
    gate_ready, used = s.pair_sems
    s.yc = v(16, 4)
    with s.nc.Block() as block:
        @block.tensor
        def _(pe):
            for c in range(12):
                if c >= 4:
                    pe.wait_ge(used.sem, used.at(c - 3))
                pe.matmul(s.ps[c % 4][:], sel[:, c, :], s.ng, start=True, stop=True).then_inc(gate_ready.sem, 1)

        @block.vector
        def _(dve):
            for c in range(12):
                dve.wait_ge(gate_ready.sem, gate_ready.at(c + 1))
                dve.tensor_tensor(o[:, c, :], o[:, c, :], s.ps[c % 4][:], ALU.mult).then_inc(used.sem, 1)
            step = Chain(dve, s.dve_chain)
            dve.wait_ge(used.sem, used.at(12))
            step(dve.tensor_tensor(s.yc, s.yc, o[:, 4:8, :], ALU.add))
            step(dve.tensor_tensor(s.yc, s.yc, o[:, 8:12, :], ALU.add))
    gate_ready.passed(12)
    used.passed(12)


def gated_residual(s, gate):
    def evac(dve, step, t, ps):
        return dve.scalar_tensor_tensor(s.x[:, t, :], ps, gate[:, bass.ds(t, 1)], s.x[:, t, :], ALU.mult, ALU.add)
    return evac


def third_mixer(s):
    v = s.view
    modulation(s)
    third_projection(s)
    spatial_gating(s)
    mlstm(s)
    sparse_attention(s)
    ga, gb, gc, merged = v(28, 8), v(36, 8), v(44, 8), v(52, 8)
    h = lambda k: s.h[:, k, :]
    linears(s, [part("w3_" + name, h, store(lambda t, dst=dst: dst[:, t, :], ACT.Sigmoid)) for name, dst in (("ga", ga), ("gb", gb), ("gc", gc))])

    def add(gate):
        def evac(dve, step, t, ps):
            step(dve.tensor_tensor(gate[:, t, :], ps, gate[:, t, :], ALU.mult))
            return dve.tensor_tensor(merged[:, t, :], merged[:, t, :], gate[:, t, :], ALU.add)
        return evac

    linears(s, [
        part("w3_up_a", lambda k: s.gu[:, k, :], lambda dve, step, t, ps: dve.tensor_tensor(merged[:, t, :], ps, ga[:, t, :], ALU.mult), by="dve"),
        part("w3_up_b", lambda k: s.yb[:, k, :], add(gb), by="dve", steps=1),
        part("w3_up_c", lambda k: s.yc[:, k, :], add(gc), by="dve", steps=1),
    ])
    linears(s, [part("w3_out", lambda k: merged[:, k, :], gated_residual(s, s.gate1), by="dve")])


def squared_relu_mlp(s):
    v = s.view
    h, wide = v(0, 8), v(8, FF3_TILES)
    norm(s, s.x, 8, 8, h, v(8, 10), False, 1, s.gain2, s.shift2)

    def evac(dve, step, t, ps):
        step(dve.tensor_scalar(wide[:, t, :], ps, 0.0, None, ALU.max))
        return dve.tensor_tensor(wide[:, t, :], wide[:, t, :], wide[:, t, :], ALU.mult)

    linears(s, [part("w3_mlp1", lambda k: h[:, k, :], evac, by="dve", steps=1)])
    linears(s, [part("w3_mlp2", lambda k: wide[:, k, :], gated_residual(s, s.gate2), by="dve")])
    norm(s, s.x, 8, 8, s.x, v(0, 10), False, 1, s.col("g_final"))
STAGES = [first_mixer, cross_attention, conv_glu, second_mixer, peer, third_mixer, squared_relu_mlp]


def kernel(**inputs):
    from concourse import bacc
    from concourse.bass_utils import run_bass_kernel_spmd

    nc = bacc.Bacc("TRN2", target_bir_lowering=False, num_devices=1)
    arrays, at = lay_out({k: np.asarray(v) for k, v in inputs.items()})
    aps = {k: nc.dram_tensor("in_" + k, v.shape, F32, kind="ExternalInput").ap() for k, v in arrays.items()}
    out = nc.dram_tensor("out", (P, DT * T), F32, kind="ExternalOutput").ap()
    build(nc, aps, at, out)
    r = run_bass_kernel_spmd(nc, [{"in_" + k: v for k, v in arrays.items()}], core_ids=[0])
    got = r.results[0]["out"]
    return got.reshape(P, DT, T).transpose(2, 1, 0).reshape(1, T, D)
```

```python
from contextlib import contextmanager

import numpy as np

import concourse.bass as bass
import concourse.mybir as mybir

F32 = mybir.dt.float32
F32R = mybir.dt.float32r
U32 = mybir.dt.uint32
ACT = mybir.ActivationFunctionType
ALU = mybir.AluOpType
AX = mybir.AxisListType

P = 128
T = 512
TT = T // P
D = 1024
DT = D // P
MEM = 256
SLAB = 2816
BANKS = 4

SSD_INNER, SSD_HEADS, SSD_HD, SSD_CONV = 1024, 16, 64, 4
XBC = 1536
RET_HEADS, RET_QK, RET_DV = 8, 64, 128
D_FF, FF_TILES = 2752, 22
ALPHA = 2.0 ** 0.25
XH, XHD = 4, 256
D_RNN, RT = 1280, 10
PEER_H, PEER_K = 8, 16
NKEYS = 128
SLOTS = PEER_H * PEER_K
GATHER = 8
NSA_H, NSA_DH, N_CMP, CMP_BLOCK, CMP_STRIDE = 8, 64, 31, 32, 16
FF3_TILES = 32
NEG = -1e30

SEG = [0, 512, 896, 1152]
SEG_LEN = 1280


def seg_width(s):
    return T - s * P


def cols(v, tiles):
    v = np.asarray(v).reshape(-1)
    out = np.zeros((tiles * P,), np.float32)
    out[: v.size] = v
    return out.reshape(tiles, P).T


def rows(v):
    out = np.zeros((P, 1), np.float32)
    out[: np.size(v), 0] = np.asarray(v).reshape(-1)
    return out


def slabs(w, width):
    k, n = w.shape
    kt, ns = -(-k // P), -(-n // width)
    if (kt * P, ns * width) != (k, n):
        w = np.pad(w, ((0, kt * P - k), (0, ns * width - n)))
    return np.ascontiguousarray(w.reshape(kt, P, ns, width).transpose(2, 1, 0, 3).reshape(ns, P, kt * width))


def channel_major(x):
    t, c = x.shape
    return np.ascontiguousarray(x.T.reshape(c // P, P, t).transpose(1, 0, 2).reshape(P, -1))


def lay_out(i):
    a, par, at = {}, [], {}

    def param(name, v):
        at[name] = (sum(p.shape[1] for p in par), v.shape[1])
        par.append(np.asarray(v, np.float32))

    w = i["w_in"][0]
    o = np.cumsum([0, 1024, 1536, 16, 512, 512, 1024, 1024])
    a["x"] = channel_major(i["x"][0])
    a["mem"] = channel_major(i["mem"][0])
    a["w_z"] = slabs(w[:, o[0]:o[1]], 256)
    a["w_xbc"] = slabs(w[:, o[1]:o[2]], 256)
    a["w_dt"] = slabs(w[:, o[2]:o[3]], 16)
    a["w_qk"] = slabs(w[:, o[3]:o[5]], 256)
    a["w_v"] = slabs(w[:, o[5]:o[6]], 256)
    a["w_g"] = slabs(w[:, o[6]:o[7]], 256)
    a["w_mix"] = slabs(i["w_mix_out"][0], 128)
    a["w_xk"], a["w_xv"] = slabs(i["w_xk"][0], 256), slabs(i["w_xv"][0], 256)
    a["w_xq"], a["w_xo"] = slabs(i["w_xq"][0], 256), slabs(i["w_xo"][0], 256)
    up, pad = i["w_ffn_up"][0], FF_TILES * P - D_FF

    def pairs(v):
        v = np.pad(v.reshape(-1, 2, D_FF), ((0, 0), (0, 0), (0, pad)))
        return v.reshape(-1, 2, FF_TILES, P).transpose(0, 2, 1, 3).reshape(v.shape[0], -1)

    a["w_up"] = slabs(pairs(up), 256)
    a["w_down"] = slabs(i["w_ffn_down"][0], 128)
    for k in range(SSD_CONV):
        param(f"ssd_conv{k}", cols(i["ssd_conv_w"][0, k], 12))
    param("ssd_conv_b", cols(i["ssd_conv_b"][0], 12))
    param("dt_bias", rows(i["ssd_dt_bias"]))
    param("a_log", rows(i["ssd_a_log"]))
    param("ssd_d", cols(np.repeat(np.asarray(i["ssd_d"][0]), SSD_HD), 8))
    param("ssd_norm", cols(i["ssd_norm_w"], 8))
    param("gn_w", cols(i["ret_gn_w"], 8))
    param("gn_b", cols(i["ret_gn_b"], 8))
    for n in (1, 2, 3):
        param(f"ln{n}_g", cols(i[f"ln{n}_g"], 8))
        param(f"ln{n}_b", cols(i[f"ln{n}_b"], 8))
    param("b_up", cols(pairs(np.asarray(i["b_ffn_up"])), 2 * FF_TILES))
    for k in range(3):
        param(f"ffn_conv{k}", cols(pairs(np.asarray(i["ffn_conv_w"][0, k:k + 1])), 2 * FF_TILES))
    param("ffn_conv_b", cols(pairs(np.asarray(i["ffn_conv_b"])), 2 * FF_TILES))

    w = i["w_in_2"][0]
    o = np.cumsum([0, 1024, 1024, 1024, 1280, 1280, 1024, 1024])
    for n, name in enumerate(("ax", "ab", "ac", "rx", "ry", "ga", "gb")):
        a["w2_" + name] = slabs(w[:, o[n]:o[n + 1]], 256)
    a["w2_out_a"], a["w2_o"] = slabs(i["w_out_a_2"][0], 256), slabs(i["w_o_2"][0], 256)
    a["w2_out_b"] = slabs(i["w_out_b_2"][0], 256)
    a["w2_q"] = slabs(i["w_q_2"][0], 256)
    a["w2_rg"] = np.ascontiguousarray(np.asarray(i["w_rg_2"][0]).transpose(1, 0, 2).reshape(1, P, -1))
    a["w2_ig"] = np.ascontiguousarray(np.asarray(i["w_ig_2"][0]).transpose(1, 0, 2).reshape(1, P, -1))
    k1, k2 = np.asarray(i["sub_keys_1_2"][0]), np.asarray(i["sub_keys_2_2"][0])
    a["keys"] = np.ascontiguousarray(np.stack([k1, k2], 1).transpose(3, 0, 1, 2).reshape(P, -1))
    a["expert_u"], a["expert_v"] = i["expert_u_2"][0], i["expert_v_2"][0]
    param("norm_mix", cols(i["norm_mix_2"], 8))
    for k in range(3):
        param(f"conv_a{k}", cols(i["conv_a_w_2"][0, k], 8))
    for k in range(4):
        param(f"rnn_conv{k}", cols(i["rnn_conv_w_2"][0, k], RT))
    for name in ("rnn_conv_b", "b_rg", "b_ig", "lru_lambda"):
        param(name, cols(i[name + "_2"], RT))
    param("norm_ffn", cols(i["norm_ffn_2"], 8))
    param("norm_final", cols(i["norm_final_2"], 8))

    w = np.asarray(i["w_in_3"][0])
    o = np.cumsum([0, 512, 512, 512, 512, 512, 512, 4, 4, 512] + [128] * 6 + [24, 1024, 1024, 1024])
    a["w3_ada"] = slabs(i["w_ada_3"][0], 256)
    a["c"] = channel_major(np.asarray(i["c_3"]))
    a["w3_gu"], a["w3_gv"] = slabs(w[:, o[0]:o[1]], 256), slabs(w[:, o[1]:o[2]], 256)
    a["w3_mqk"] = slabs(w[:, o[2]:o[4]], 256)
    a["w3_mv"], a["w3_mo"] = slabs(w[:, o[4]:o[5]], 256), slabs(w[:, o[5]:o[6]], 256)
    a["w3_mi"], a["w3_mf"] = slabs(w[:, o[6]:o[7]], 4), slabs(w[:, o[7]:o[8]], 4)
    a["w3_nq"] = slabs(w[:, o[8]:o[9]], 256)
    kc, vc, ks, vs, kw, vw = (w[:, o[9 + n]:o[10 + n]] for n in range(6))
    a["w3_kvc"] = slabs(np.concatenate([kc, vc], 1), 256)
    a["w3_ksw"] = slabs(np.concatenate([k[:, g * 64:g * 64 + 64] for k in (ks, kw) for g in (0, 0, 1, 1)], 1), 256)
    a["w3_vsw"] = slabs(np.concatenate([vs, vw], 1), 256)
    a["w3_ng"] = slabs(w[:, o[15]:o[16]], 24)
    for n, name in enumerate(("ga", "gb", "gc")):
        a["w3_" + name] = slabs(w[:, o[16 + n]:o[17 + n]], 256)
        a["w3_up_" + name[1]] = slabs(i[f"w_up_{name[1]}_3"][0], 512)
    a["w3_out"] = slabs(i["w_out_3"][0], 256)
    half = FF3_TILES // 2 * P
    for n, name in enumerate("ab"):
        a["w3_mlp1" + name] = slabs(i["w_mlp1_3"][0][:, n * half:(n + 1) * half], 256)
        a["w3_mlp2" + name] = slabs(i["w_mlp2_3"][0][n * half:(n + 1) * half], 128)
    param("b_ada", cols(i["b_ada_3"], 48))
    for name in ("g_norm1", "g_norm2", "g_final"):
        param(name, cols(i[name + "_3"], 8))
    param("gm_ln_g", cols(i["gm_ln_g_3"], 4))
    param("gm_ln_b", cols(i["gm_ln_b_3"], 4))
    a["gm_w"] = np.ascontiguousarray(np.asarray(i["gm_ws_3"][0]).transpose(2, 0, 1).reshape(P, -1))
    a["gm_b"] = np.ascontiguousarray(np.broadcast_to(np.asarray(i["gm_bs_3"][0]).reshape(1, -1), (P, 512)))
    for k in range(4):
        param(f"ml_conv{k}", cols(i["ml_conv_w_3"][0, k], 8))
    param("ml_conv_b", cols(i["ml_conv_b_3"], 8))
    param("ml_bi", rows(np.asarray(i["ml_gate_b_3"])[0, :4]))
    param("ml_bf", rows(np.asarray(i["ml_gate_b_3"])[0, 4:]))
    param("ml_norm", cols(i["ml_norm_g_3"], 4))
    for n in "kv":
        pe = np.asarray(i[f"nsa_pe_{n}_3"][0]).T
        param(f"pe_{n}", np.concatenate([pe, pe], 0))
        phi = np.asarray(i[f"nsa_phi_{n}1_3"][0]).reshape(CMP_BLOCK, 64, 64).transpose(1, 0, 2).reshape(64, -1)
        a[f"phi_{n}1"] = np.ascontiguousarray(np.concatenate([phi, phi], 0))
        a[f"phi_{n}2"] = np.ascontiguousarray(i[f"nsa_phi_{n}2_3"][0])
    a["phi_k2"] = np.concatenate([a["phi_k2"], a["phi_k2"]], 1)
    a["params"] = np.ascontiguousarray(np.concatenate(par, 1))
    a.update(constants())
    return {k: np.ascontiguousarray(v) for k, v in a.items()}, at


def constants():
    c = {}
    p, j = np.arange(P)[:, None], np.arange(T)[None, :]
    eye = np.eye(P)
    turn = np.zeros((P, P))
    for m in range(P):
        d = m % RET_QK
        if d < 32:
            turn[m + 32, m] = -1.0
        else:
            turn[m - 32, m] = 1.0
    causal = (p <= np.arange(P)[None, :]).astype(float)
    eps = np.tile(np.array([[1e-5, 1e-6]]), (P, 1))
    c["base"] = np.concatenate([eye, turn, causal, np.ones((P, P)), eps], 1)
    freqs = (1.0 / (np.float32(10000.0) ** np.linspace(0.0, 1.0, 32, dtype=np.float32))).astype(np.float32)
    ang = (np.arange(T, dtype=np.float32)[None, :] * freqs[:, None]).astype(np.float32)
    ang = np.tile(ang.astype(np.float64), (4, 1))
    c["rope"] = np.concatenate([np.cos(ang), np.sin(ang)], 1)
    gamma = np.log1p(-np.exp2(-5.0 - np.arange(RET_HEADS)))
    dist = j - p
    c["decay"] = np.concatenate(
        [np.where(dist >= 0, np.exp(np.maximum(dist, 0) * g), 0.0) * RET_QK ** -0.5 for g in gamma], 1)
    alibi = j - p - 384.0
    c["alibi"] = np.where(alibi > 0, NEG, alibi)
    t = np.arange(T)
    n = np.arange(N_CMP)
    ok = (n * CMP_STRIDE + CMP_BLOCK - 1)[None, :] <= t[:, None]
    center = n * CMP_STRIDE + (CMP_BLOCK - 1) * 0.5
    cd = np.where(ok, center[None, :] - t[:, None], NEG)
    for name, v in (("cmp_dist", cd), ("cmp_ok", ok.astype(float))):
        c[name] = v.reshape(TT, P, N_CMP).transpose(1, 0, 2).reshape(P, -1)
    sel = np.zeros((24, 12, P))
    for b in range(3):
        for tile in range(4):
            for q in range(P):
                sel[(2 * tile + q // 64) * 3 + b, b * 4 + tile, q] = 1.0
    c["gate_sel"] = sel.reshape(24, -1)
    c["iota"] = np.tile(np.arange(float(PEER_K))[None, :], (P, 1))
    return {k: np.ascontiguousarray(v, dtype=np.float32) for k, v in c.items()}


class Names:
    pass


class Counter:

    def __init__(self, nc, name):
        self.sem, self.base = nc.alloc_semaphore(name), 0

    def at(self, n):
        return self.base + n

    def passed(self, n):
        self.base += n


class Chain:

    def __init__(self, eng, counter):
        self.eng, self.counter, self.turn = eng, counter, 0

    def __call__(self, ins):
        self.counter.base += 1
        ins.then_inc(self.counter.sem, 1)
        self.eng.wait_ge(self.counter.sem, self.counter.base + self.turn)

    @contextmanager
    def loop(self, count, steps):
        start, outer = self.counter.base, self.turn
        with self.eng.Fori(0, count) as i:
            self.turn = outer + i * steps
            yield i
        assert self.counter.base == start + steps, (self.counter.base - start, steps)
        self.turn = outer
        self.counter.base = start + steps * count


PLAN = [
    ("w_z", 8, 256), ("w_xbc", 8, 256), ("w_dt", 8, 16), ("w_qk", 8, 256), ("w_g", 8, 256), ("w_v", 8, 256),
    ("w_mix", 16, 128), ("w_xk", 8, 256), ("w_xv", 8, 256), ("w_xq", 8, 256), ("w_xo", 8, 256),
    ("w_up", 8, 256), ("w_down", 22, 128),
    ("w2_ax", 8, 256), ("w2_ac", 8, 256), ("w2_ab", 8, 256), ("w2_rx", 8, 256), ("w2_ry", 8, 256),
    ("w2_rg", 1, 1280), ("w2_ig", 1, 1280), ("w2_ga", 8, 256), ("w2_gb", 8, 256), ("w2_out_a", 8, 256),
    ("w2_out_b", 10, 256), ("w2_o", 8, 256), ("w2_q", 8, 256),
    ("w3_ada", 8, 256), ("w3_gu", 8, 256), ("w3_gv", 8, 256), ("w3_mqk", 8, 256), ("w3_mv", 8, 256),
    ("w3_mo", 8, 256), ("w3_mi", 8, 4), ("w3_mf", 8, 4), ("w3_nq", 8, 256), ("w3_kvc", 8, 256),
    ("w3_ksw", 8, 256), ("w3_vsw", 8, 256), ("w3_ng", 8, 24),
    ("w3_ga", 8, 256), ("w3_gb", 8, 256), ("w3_gc", 8, 256),
    ("w3_up_a", 4, 512), ("w3_up_b", 4, 512), ("w3_up_c", 4, 512), ("w3_out", 8, 256),
    ("w3_mlp1a", 8, 256), ("w3_mlp2a", 16, 128), ("w3_mlp1b", 8, 256), ("w3_mlp2b", 16, 128),
]
RING = 2
UNITS = 2
UNIT_K = 8


class Split:

    def __init__(self, src, tiles, hi, lo):
        self.src, self.tiles, self.hi, self.lo, self.made = src, tiles, hi, lo, False


def part(name, act, evac, tile=P, n=T, tokens=0, by="act", steps=0, block_diag=False, side=None, side_steps=0, side_after=None):
    p = Names()
    p.side, p.side_steps, p.side_after = side, side_steps, side_after
    p.name, p.act, p.evac, p.tile, p.n, p.tokens, p.by, p.steps, p.block_diag = name, act, evac, tile, n, tokens, by, steps, block_diag
    p.split = act if isinstance(act, Split) else None
    return p


def linears(s, parts, before={}, after={}):
    nc = s.nc
    fresh = []
    for p in parts:
        p.index = [w[0] for w in PLAN].index(p.name)
        assert p.index == s.next_part, p.name
        s.next_part += 1
        _, p.kt, p.width = PLAN[p.index]
        p.first = s.first_slab[p.index]
        p.slabs = s.first_slab[p.index + 1] - p.first
        p.per_slab = p.tokens or p.width // p.tile
        p.chunks = [(k, min(k + UNIT_K, p.kt)) for k in range(0, p.kt, UNIT_K)] if p.split else [(0, p.kt)]
        p.upt = len(p.chunks)
        p.tile0, p.unit0, p.split0 = s.tiles, s.units, s.split_units
        s.tiles += p.slabs * p.per_slab
        s.units += p.slabs * p.per_slab * p.upt
        p.body = 4 if p.per_slab == 1 else 2
        p.bodies = p.slabs // p.body if p.slabs >= 2 * p.body and p.tokens <= 1 and p.tile0 else 0
        p.tiles = p.body * p.per_slab
        for k in range(p.slabs):
            done = (k + 1) * p.per_slab * p.upt
            s.slab_end.append((s.lo_made, p.split0 + done) if p.split else (s.units_done, p.unit0 + done))
        if p.split:
            s.split_units += p.slabs * p.per_slab * p.upt
            if not p.split.made:
                p.split.made = True
                fresh.append((p, p.split, sum(f[1].tiles for f in fresh)))
        p.peel = 1 if p is parts[0] and p.bodies else 0

    def bodies(eng, p, slab):
        for i in range(p.peel):
            for j in range(p.body):
                slab(i, j)
        if p.bodies > p.peel:
            with eng.Fori(p.peel, p.bodies) as i:
                for j in range(p.body):
                    slab(i, j)
        for j in range(p.bodies * p.body, p.slabs):
            slab(0, j)

    def load(sync, ring_free, index, k, slot):
        if ring_free is not None:
            sync.wait_ge(ring_free[0].sem, ring_free[1])
        _, kt, width = PLAN[index]
        sync.dma_start(s.ring[:, slot, 0:kt * width], s.I[PLAN[index][0]][k]).then_inc(s.slab_ready[slot], 16)

    def load_static(sync, slab):
        if slab < s.first_slab[-1]:
            index = max(j for j in range(len(PLAN)) if s.first_slab[j] <= slab)
            load(sync, s.slab_end[slab - RING] if slab >= RING else None, index, slab - s.first_slab[index], slab % RING)

    def raw_and_split(p, i, j, u, c):
        unit = (j * p.per_slab + u) * p.upt + c
        k0, k1 = p.chunks[c]
        raw = s.ring[:, (p.first + j) % RING, 0:p.kt * p.width].rearrange("p (k n) -> p k n", k=p.kt)[:, k0:k1, u * P:(u + 1) * P]
        hi, lo = (x[(p.split0 + unit) % UNITS][:, 0:(k1 - k0) * P].rearrange("p (k n) -> p k n", n=P) for x in (s.w_hi, s.w_lo))
        return unit, i * (p.tiles * p.upt), raw, hi, lo

    def wait_for_slab(eng, p, i, j):
        slab = p.first + j
        eng.wait_ge(s.slab_ready[slab % RING], (slab // RING + 1) * 16 + i * (p.body // RING) * 16)

    def high_parts(eng, p, i, j, u, c):
        unit, before, raw, hi, lo = raw_and_split(p, i, j, u, c)
        if u == 0 and c == 0:
            wait_for_slab(eng, p, i, j)
        if not isinstance(i, int) or p.unit0 + unit + before >= UNITS:
            eng.wait_ge(s.units_done.sem, p.unit0 + unit + 1 - UNITS + before)
        ins = eng.activation(hi, raw, ACT.Copy) if p.by == "dve" else eng.tensor_copy(hi, raw)
        ins.then_inc(s.hi_made.sem, 1)

    def low_parts(eng, p, i, j, u, c):
        unit, before, raw, hi, lo = raw_and_split(p, i, j, u, c)
        eng.wait_ge(s.hi_made.sem, p.split0 + unit + 1 + before)
        eng.tensor_tensor(lo, raw, hi.bitcast(F32), ALU.subtract).then_inc(s.lo_made.sem, 1)

    def split_units(eng, p, steps, others, chain=None):
        for q in parts:
            if p.side and q.name == p.side_after:
                eng.wait_ge(s.evac_done.sem, q.tile0 + q.slabs * q.per_slab)

        def slab(i, j):
            for u in range(p.per_slab):
                for c in range(p.upt):
                    for step in steps:
                        step(eng, p, i, j, u, c)
                    unit = (j * p.per_slab + u) * p.upt + c
                    if isinstance(i, int) and i == 0 and unit < 2:
                        others(unit)
                if p.side and chain:
                    p.side(eng, chain, p, i * p.tiles + j * p.per_slab + u, j * p.per_slab + u)

        if p.side and chain and p.bodies and p.by == "act":
            with chain.loop(p.bodies, p.side_steps) as i:
                for j in range(p.body):
                    slab(i, j)
            for j in range(p.bodies * p.body, p.slabs):
                slab(0, j)
        else:
            bodies(eng, p, slab)

    def activations(split_tiles):
        def others(unit):
            for p, split, at in fresh:
                if (p is parts[0]) == (unit == 0):
                    split_tiles(split, at)
        return others

    def high_tiles(act):
        def tiles(split, at):
            for k in range(split.tiles):
                act.activation(split.hi(k), split.src(k), ACT.Copy).then_inc(s.act_hi.sem, 1)
        return tiles

    def low_tiles(dve):
        def tiles(split, at):
            for k in range(split.tiles):
                dve.wait_ge(s.act_hi.sem, s.act_hi.at(at + k + 1))
                dve.tensor_tensor(split.lo(k), split.src(k), split.hi(k).bitcast(F32), ALU.subtract).then_inc(s.act_lo.sem, 1)
        return tiles

    def extra(programs, name, eng):
        if name in programs:
            programs[name](eng)

    with nc.Block() as block:
        @block.sync
        def _(sync):
            extra(before, "sync", sync)
            for p in parts:
                if p.first == 0:
                    for slab in range(RING):
                        load_static(sync, slab)
                inside = max(p.slabs - RING, 0)
                pairs = inside // RING if inside >= 2 * RING else 0
                if pairs:
                    end = s.slab_end[p.first]
                    step = p.per_slab * p.upt
                    with sync.Fori(0, pairs) as i:
                        for j in range(RING):
                            load(sync, (end[0], end[1] + (i * RING + j) * step), p.index, i * RING + j + RING, (p.first + j) % RING)
                for k in range(pairs * RING, p.slabs):
                    load_static(sync, p.first + k + RING)

        @block.tensor
        def _(pe):
            def products(p, i, j):
                if not p.split:
                    wait_for_slab(pe, p, i, j)
                w = s.ring[:, (p.first + j) % RING, 0:p.kt * p.width].rearrange("p (k n) -> p k n", k=p.kt)
                for u in range(p.per_slab):
                    t = j * p.per_slab + u
                    bank = s.ps[(p.tile0 + t) % BANKS]
                    if not isinstance(i, int) or p.tile0 + i * p.tiles + t >= BANKS:
                        pe.wait_ge(s.evac_done.sem, p.tile0 + t - BANKS + 1 + i * p.tiles)
                    for c, (k0, k1) in enumerate(p.chunks):
                        unit, before, _, hi, lo = raw_and_split(p, i, j, u, c) if p.split else (None, None, None, None, None)
                        if p.split:
                            pe.wait_ge(s.lo_made.sem, p.split0 + unit + 1 + before)
                        for k in range(k0, k1):
                            first, last = k == 0, k == p.kt - 1
                            if p.split:
                                if fresh and p is parts[0] and fresh[0][0] is p and isinstance(i, int) and i == 0 and t == 0:
                                    pe.wait_ge(s.act_lo.sem, s.act_lo.at(k + 1))
                                out, x = bank[:, 0:p.n], p.split
                                pe.matmul(out, hi[:, k - k0, :], x.hi(k), start=first, stop=False)
                                pe.matmul(out, hi[:, k - k0, :], x.lo(k), start=False, stop=False)
                                mm = pe.matmul(out, lo[:, k - k0, :], x.hi(k), start=False, stop=last)
                            elif p.tokens:
                                mm = pe.matmul(bank[0:p.tile, 0:p.width], p.act(k)[:, u * P:u * P + p.tile], w[:, k, :], start=first, stop=last)
                            else:
                                mm = pe.matmul(bank[0:p.tile, 0:p.n], w[:, k, u * p.tile:(u + 1) * p.tile],
                                               p.act(u if p.block_diag else k), start=first, stop=last)
                        mm.then_inc(s.units_done.sem, 1)

            extra(before, "tensor", pe)
            for n, p in enumerate(parts):
                if n and parts[n - 1].by != p.by:
                    pe.wait_ge(s.evac_done.sem, p.tile0)
                for q, split, at in fresh:
                    if q is p and n:
                        pe.wait_ge(s.act_lo.sem, s.act_lo.at(at + split.tiles))
                bodies(pe, p, lambda i, j: products(p, i, j))
            extra(after, "tensor", pe)

        def evacuate(eng, chain, p):
            def one(t, bank):
                eng.wait_ge(s.units_done.sem, p.unit0 + (t + 1) * p.upt)
                if not isinstance(t, int) and p.by == "act":
                    eng.sem_inc(s.held, 1)
                ps = s.ps[bank]
                ps = ps[0:p.tile, 0:p.width if p.tokens else p.n]
                p.evac(eng, chain, t, ps).then_inc(s.evac_done.sem, 1)

            if p.bodies:
                with chain.loop(p.bodies, int(p.steps * p.tiles)) as i:
                    for u in range(p.tiles):
                        one(i * p.tiles + u, (p.tile0 + u) % BANKS)
            for t in range(p.bodies * p.tiles, p.slabs * p.per_slab):
                one(t, (p.tile0 + t) % BANKS)

        @block.scalar
        def _(act):
            chain = Chain(act, s.act_chain)
            extra(before, "scalar", act)
            others = activations(high_tiles(act))
            for p in parts:
                mine = others if p is parts[0] else lambda unit: None
                if p.by == "dve" and p.split:
                    split_units(act, p, [high_parts], mine, chain)
                else:
                    mine(0)
                    mine(1)
                if p.by == "act":
                    evacuate(act, chain, p)
            extra(after, "scalar", act)

        @block.vector
        def _(dve):
            chain = Chain(dve, s.dve_chain)
            extra(before, "vector", dve)
            others = activations(low_tiles(dve))
            for p in parts:
                mine = others if p is parts[0] else lambda unit: None
                if p.by == "act" and p.split:
                    split_units(dve, p, [high_parts, low_parts], mine, chain)
                else:
                    mine(0)
                    mine(1)
                if p.by == "dve":
                    evacuate(dve, chain, p)
            extra(after, "vector", dve)

        @block.gpsimd
        def _(pool):
            for p in parts:
                if p.by == "dve" and p.split:
                    split_units(pool, p, [low_parts], lambda unit: None)
    for p, split, at in fresh:
        s.act_hi.passed(split.tiles)
        s.act_lo.passed(split.tiles)


def residual(s, scale=1.0):
    def evac(dve, step, t, ps):
        return dve.scalar_tensor_tensor(s.x[:, t, :], s.x[:, t, :], scale, ps, ALU.mult, ALU.add)
    return evac


def store(dst, func=ACT.Copy, bias=None, scale=1.0):
    def evac(act, step, t, ps):
        if bias is None:
            return act.activation(dst(t), ps, func, scale=scale)
        return act.activation(dst(t), ps, func, bias=bias(t), scale=scale)
    return evac


def store_by_token(dst, tiles, width=256):
    def evac(act, step, t, ps):
        return act.activation(dst[:, t % tiles, (t // tiles) * width:(t // tiles + 1) * width], ps, ACT.Copy)
    return evac


def norm(s, src, tiles, group, dst, scratch, center, eps, gain, bias=None, post=None):
    n, groups = group * P, tiles // group
    squares = max(group, 2)
    sq, std = scratch[:, 0:squares, :], scratch[:, squares:squares + 2, :]
    mean_ready, cen_ready, sq_ready, var_ready, std_ready, out_ready = s.norm_sems
    scaled, _ = s.pair_sems
    late_bias = bias is not None and post is None
    with s.nc.Block() as block:
        @block.tensor
        def _(pe):
            def mean(g):
                if g >= 2:
                    pe.wait_ge(cen_ready.sem, cen_ready.at((g - 1) * group))
                for u in range(group):
                    mm = pe.matmul(s.ps[4 + g % 2][:], s.ones, src[:, g * group + u, :], start=u == 0, stop=u == group - 1)
                mm.then_inc(mean_ready.sem, 1)

            if center:
                mean(0)
            for g in range(groups):
                if center and g + 1 < groups:
                    mean(g + 1)
                if g >= 2:
                    pe.wait_ge(std_ready.sem, std_ready.at(g - 1))
                for u in range(group):
                    t = g * group + u
                    pe.wait_ge(sq_ready.sem, sq_ready.at(t + 1))
                    mm = pe.matmul(s.ps[6 + g % 2][:], s.ones, sq[:, t % squares, :], start=u == 0, stop=u == group - 1)
                mm.then_inc(var_ready.sem, 1)

        @block.scalar
        def _(act):
            def root(g):
                act.wait_ge(var_ready.sem, var_ready.at(g + 1))
                if g >= 2:
                    act.wait_ge(out_ready.sem, out_ready.at(g - 1))
                act.activation(std[:, g % 2, :], s.ps[6 + g % 2][:], ACT.Sqrt, bias=s.eps[eps], scale=1.0 / n).then_inc(std_ready.sem, 1)

            for g in range(groups):
                for t in range(g * group, (g + 1) * group):
                    if center:
                        act.wait_ge(cen_ready.sem, cen_ready.at(t + 1))
                    if t >= squares:
                        act.wait_ge(var_ready.sem, var_ready.at((t - squares) // group + 1))
                    act.activation(sq[:, t % squares, :], src[:, t, :], ACT.Square).then_inc(sq_ready.sem, 1)
                if g:
                    root(g - 1)
            root(groups - 1)
            if late_bias:
                for t in range(tiles):
                    act.wait_ge(scaled.sem, scaled.at(t + 1))
                    act.activation(dst[:, t, :], dst[:, t, :], ACT.Identity, bias=bias[:, t:t + 1])

        @block.vector
        def _(dve):
            step = Chain(dve, s.dve_chain)

            def centre(g):
                dve.wait_ge(mean_ready.sem, mean_ready.at(g + 1))
                for u in range(group):
                    t = src[:, g * group + u, :]
                    dve.scalar_tensor_tensor(t, s.ps[4 + g % 2][:], -1.0 / n, t, ALU.mult, ALU.add).then_inc(cen_ready.sem, 1)

            if center:
                centre(0)
            for g in range(groups):
                if center and g + 1 < groups:
                    centre(g + 1)
                dve.wait_ge(std_ready.sem, std_ready.at(g + 1))
                if center:
                    dve.wait_ge(cen_ready.sem, cen_ready.at((g + 1) * group))
                r = std[:, g % 2, :]
                step(dve.reciprocal(r, r))
                both = range(g * group, (g + 1) * group)
                for t in both:
                    ins = dve.scalar_tensor_tensor(dst[:, t, :], src[:, t, :], gain[:, t:t + 1], r, ALU.mult, ALU.mult)
                    if late_bias:
                        ins.then_inc(scaled.sem, 1)
                if late_bias:
                    continue
                if bias is not None or post is not None:
                    step(ins)
                    for t in both:
                        if bias is not None and post is not None:
                            ins = dve.scalar_tensor_tensor(dst[:, t, :], dst[:, t, :], bias[:, t:t + 1], post[:, t, :], ALU.add, ALU.mult)
                        else:
                            ins = dve.tensor_tensor(dst[:, t, :], dst[:, t, :], post[:, t, :], ALU.mult)
                ins.then_inc(out_ready.sem, 1)
    sq_ready.passed(tiles)
    for c in (var_ready, std_ready):
        c.passed(groups)
    if late_bias:
        assert groups == 1
        scaled.passed(tiles)
    else:
        out_ready.passed(groups)
    if center:
        mean_ready.passed(groups)
        cen_ready.passed(tiles)


def softplus_rows(s, jobs):
    ready, taken = s.pair_sems
    with s.nc.Block() as block:
        @block.scalar
        def _(act):
            step = Chain(act, s.act_chain)
            for n, (x, out, e, w, d, sigmoid) in enumerate(jobs):
                step(act.activation(e, x, ACT.Abs))
                act.activation(e, e, ACT.Exp, scale=-1.0).then_inc(ready.sem, 1)
                act.wait_ge(taken.sem, taken.at(n + 1))
                act.activation(out, w, ACT.Ln).then_inc(ready.sem, 1)

        @block.vector
        def _(dve):
            step = Chain(dve, s.dve_chain)
            for n, (x, out, e, w, d, sigmoid) in enumerate(jobs):
                dve.wait_ge(ready.sem, ready.at(2 * n + 1))
                dve.tensor_scalar(w, e, 1.0, None, ALU.add).then_inc(taken.sem, 1)
                dve.wait_ge(taken.sem, taken.at(n + 1))
                step(dve.tensor_scalar(d, w, 1.0, None, ALU.subtract))
                step(dve.tensor_tensor(d, e, d, ALU.subtract))
                dve.wait_ge(ready.sem, ready.at(2 * n + 2))
                step(dve.reciprocal(w, w))
                step(dve.tensor_tensor(d, d, w, ALU.mult))
                step(dve.tensor_tensor(d, d, out, ALU.add))
                step(dve.tensor_scalar(e, x, 0.0, None, ALU.min if sigmoid else ALU.max))
                step(dve.tensor_tensor(out, e, d, ALU.subtract if sigmoid else ALU.add))
    ready.passed(2 * len(jobs))
    taken.passed(len(jobs))


def load_start(s):
    with s.nc.Block() as block:
        @block.sync
        def _(sync):
            for dst, src in ((s.base[:], s.I["base"]), (s.par[:], s.I["params"]), (s.xflat, s.I["x"])):
                sync.dma_start(dst, src).then_inc(s.loaded.sem, 16)
            sync.wait_ge(s.loaded.sem, s.loaded.at(48))
    s.loaded.passed(48)


def causal_conv(s, dve, step, dst, src, taps, t):
    n = len(taps)
    step(dve.tensor_scalar(dst, src(0), taps[0][:, t], None, ALU.mult))
    for k in range(1, n):
        ins = dve.scalar_tensor_tensor(dst, src(k), taps[k][:, t], dst, ALU.mult, ALU.add)
        if k < n - 1:
            step(ins)
    return ins


def first_projection(s):
    v = s.view
    s.sz, s.qk, s.sg = v(0, 8), v(21, 8), v(29, 8)
    s.xbc = s.arena[:, 8 * T:8 * T + 12 * (T + 3)].rearrange("p (a t) -> p a t", a=12)
    s.vt = v(37, 8).rearrange("p a t -> p (a t)").rearrange("p (t c) -> p t c", t=TT)
    s.dt_raw = s.arena[0:SSD_HEADS, 45 * T:46 * T]
    with s.nc.Block() as block:
        @block.gpsimd
        def _(pool):
            pool.memset(s.xbc[:, :, 0:3], 0.0)
    whole = lambda k: s.x[:, k, :]
    x = Split(whole, DT, s.rounded(58), s.rounded(66))
    s.xs = v(46, 12)

    def conv(dve, step, t):
        ins = causal_conv(s, dve, step, s.xs[:, t, :], lambda k: s.xbc[:, t, k:k + T], taps, bass.ds(t, 1))
        ins.then_inc(s.convolved.sem, 1)

    def store_v(act, step, t, ps):
        if t < 12:
            act.wait_ge(s.convolved.sem, s.convolved.at(t + 1))
            act.activation(s.xs[:, t, :], s.xs[:, t, :], ACT.Silu, bias=s.col("ssd_conv_b")[:, t:t + 1])
        return store_by_token(s.vt, TT)(act, step, t, ps)

    def first_convs(dve, step, p, t, u):
        conv(dve, step, t)

    def last_convs(dve, step, p, t, u):
        if u % 2 == 0:
            conv(dve, step, 8 + t // 2)

    taps = [s.col(f"ssd_conv{k}") for k in range(SSD_CONV)]

    linears(s, [
        part("w_z", x, store(lambda t: s.sz[:, t, :], ACT.Silu)),
        part("w_xbc", x, store(lambda t: s.xbc[:, t, 3:3 + T])),
        part("w_dt", whole, store(lambda t: s.dt_raw, ACT.Identity, lambda t: s.col("dt_bias")[0:SSD_HEADS, :]), tile=SSD_HEADS),
        part("w_qk", x, store(lambda t: s.qk[:, t, :]), side=first_convs, side_steps=12, side_after="w_xbc"),
        part("w_g", x, store(lambda t: s.sg[:, t, :], ACT.Silu), side=last_convs, side_steps=6),
        part("w_v", whole, store_v, tokens=TT),
    ])
    s.convolved.passed(12)


def ssd_prepare(s):
    v = s.view
    row = lambda k: s.arena[0:SSD_HEADS, k * T:(k + 1) * T]
    s.dt, s.acs, e, w, d = row(71), row(72), row(58), row(59), row(60)
    softplus_rows(s, [(s.dt_raw, s.dt, e, w, d, False)])
    with s.nc.Block() as block:
        @block.scalar
        def _(act):
            act.activation(s.small[0:SSD_HEADS, 0:1], s.col("a_log")[0:SSD_HEADS, :], ACT.Exp).then_inc(s.pair_sems[0].sem, 1)

        @block.vector
        def _(dve):
            step = Chain(dve, s.dve_chain)
            step(dve.memset(w, 1.0))
            dve.wait_ge(s.pair_sems[0].sem, s.pair_sems[0].at(1))
            step(dve.tensor_scalar(d, s.dt, s.small[0:SSD_HEADS, 0:1], -1.0, ALU.mult, ALU.mult))
            step(dve.tensor_tensor_scan(s.acs, w, d, 0.0, ALU.mult, ALU.add))
    s.pair_sems[0].passed(1)


def ssd_turn(s):
    v = s.view
    s.dt_col, s.acs_col = (s.small[:, 64 + 64 * k:128 + 64 * k].rearrange("p (a h) -> p a h", a=TT) for k in range(2))
    s.xdt = v(63, 8).rearrange("p a t -> p (a t)").rearrange("p (t c) -> p t c", t=TT)
    s.cb = s.arena[:, 16 * T:16 * T + 2 * SEG_LEN].rearrange("p (g n) -> p g n", g=2)
    rows_ready, cols_ready, x_ready, x_done, cb_ready, cb_done = s.norm_sems
    with s.nc.Block() as block:
        @block.tensor
        def _(pe):
            for k, src in enumerate((s.dt, s.acs)):
                for a in range(TT):
                    mm = pe.transpose(s.ps[k][:, a * SSD_HEADS:(a + 1) * SSD_HEADS], src[:, a * P:(a + 1) * P], s.eye[0:SSD_HEADS, 0:SSD_HEADS])
            mm.then_inc(rows_ready.sem, 1)
            for a in range(TT):
                for half in range(2):
                    n = 2 * a + half
                    if n >= 2:
                        pe.wait_ge(x_done.sem, x_done.at(n - 1))
                    for u in range(4):
                        mm = pe.transpose(s.ps[2 + half][:, u * P:(u + 1) * P], s.xs[:, half * 4 + u, a * P:(a + 1) * P], s.eye)
                    mm.then_inc(x_ready.sem, 1)
            for g in range(2):
                for a in range(TT):
                    n = 4 * g + a
                    if n >= 4:
                        pe.wait_ge(cb_done.sem, cb_done.at(n - 3))
                    pe.matmul(s.ps[4 + a][:, 0:seg_width(a)], s.xs[:, 8 + g, a * P:(a + 1) * P], s.xs[:, 10 + g, a * P:T],
                              start=True, stop=True).then_inc(cb_ready.sem, 1)

        @block.vector
        def _(dve):
            dve.wait_ge(rows_ready.sem, rows_ready.at(1))
            dve.tensor_copy(s.acs_col.rearrange("p a h -> p (a h)"), s.ps[1][:, 0:64])
            dve.tensor_copy(s.dt_col.rearrange("p a h -> p (a h)"), s.ps[0][:, 0:64]).then_inc(cols_ready.sem, 1)
            dve.wait_ge(cols_ready.sem, cols_ready.at(1))
            for a in range(TT):
                for half in range(2):
                    dve.wait_ge(x_ready.sem, x_ready.at(2 * a + half + 1))
                    out = s.xdt[:, a, half * 512:half * 512 + 512].rearrange("p (h d) -> p h d", h=8)
                    dve.tensor_tensor(out, s.ps[2 + half][:].rearrange("p (h d) -> p h d", h=8),
                                      s.dt_col[:, a, half * 8:half * 8 + 8].unsqueeze(2).broadcast_to([P, 8, SSD_HD]),
                                      ALU.mult).then_inc(x_done.sem, 1)
            for g in range(2):
                for a in range(TT):
                    dve.wait_ge(cb_ready.sem, cb_ready.at(4 * g + a + 1))
                    seg = s.cb[:, g, SEG[a]:SEG[a] + seg_width(a)]
                    if a < TT - 1:
                        dve.tensor_copy(seg[:, P:], s.ps[4 + a][:, P:seg_width(a)])
                    dve.tensor_tensor(seg[:, 0:P], s.ps[4 + a][:, 0:P], s.causal, ALU.mult).then_inc(cb_done.sem, 1)
    for c, n in ((rows_ready, 1), (cols_ready, 1), (x_ready, 8), (x_done, 8), (cb_ready, 8), (cb_done, 8)):
        c.passed(n)


def ssd_heads(s):
    s.u = s.view(8, 8)
    s.att = [s.arena[:, 58 * T + k * SEG_LEN:58 * T + (k + 1) * SEG_LEN] for k in range(2)]
    bc_ready, diff_ready, exp_ready, att_ready, y_ready, y_done = s.norm_sems
    with s.nc.Block() as block:
        @block.tensor
        def _(pe):
            def sums(h):
                if h >= 2:
                    pe.wait_ge(diff_ready.sem, diff_ready.at(h - 1))
                pe.matmul(s.ps[h % 2][:], s.eye[0:SSD_HEADS, h:h + 1].broadcast_to([SSD_HEADS, P]), s.acs, start=True, stop=True).then_inc(bc_ready.sem, 1)

            sums(0)
            for h in range(SSD_HEADS):
                if h + 1 < SSD_HEADS:
                    sums(h + 1)
                j, lo = h // 2, (h % 2) * SSD_HD
                if h % 2 == 0 and j >= 2:
                    pe.wait_ge(y_done.sem, y_done.at(j - 1))
                pe.wait_ge(att_ready.sem, att_ready.at(h + 1))
                for a in range(TT):
                    mm = pe.matmul(s.ps[2 + j % 2][lo:lo + SSD_HD, a * P:T], s.xdt[:, a, h * SSD_HD:(h + 1) * SSD_HD],
                                   s.att[h % 2][:, SEG[a]:SEG[a] + seg_width(a)], start=a == 0, stop=a == TT - 1, skip_group_check=True)
                mm.then_inc(y_ready.sem, 1)

        @block.scalar
        def _(act):
            for h in range(SSD_HEADS):
                act.wait_ge(diff_ready.sem, diff_ready.at(h + 1))
                act.activation(s.att[h % 2], s.att[h % 2], ACT.Exp).then_inc(exp_ready.sem, 1)

        @block.vector
        def _(dve):
            step = Chain(dve, s.dve_chain)

            def differences(h):
                dve.wait_ge(bc_ready.sem, bc_ready.at(h + 1))
                if h >= 2:
                    dve.wait_ge(y_ready.sem, y_ready.at(h - 1))
                for a in range(TT):
                    ins = dve.tensor_scalar(s.att[h % 2][:, SEG[a]:SEG[a] + seg_width(a)], s.ps[h % 2][:, a * P:T],
                                            s.acs_col[:, a, h:h + 1], 0.0, ALU.subtract, ALU.min)
                ins.then_inc(diff_ready.sem, 1)

            differences(0)
            for h in range(SSD_HEADS):
                if h + 1 < SSD_HEADS:
                    differences(h + 1)
                dve.wait_ge(exp_ready.sem, exp_ready.at(h + 1))
                dve.tensor_tensor(s.att[h % 2], s.att[h % 2], s.cb[:, h // 8, :], ALU.mult).then_inc(att_ready.sem, 1)
                if h % 2:
                    j = h // 2
                    dve.wait_ge(y_ready.sem, y_ready.at(h + 1))
                    ins = dve.scalar_tensor_tensor(s.u[:, j, :], s.xs[:, j, :], s.col("ssd_d")[:, j:j + 1], s.ps[2 + j % 2][:], ALU.mult, ALU.add)
                    ins.then_inc(y_done.sem, 1)
                    dve.wait_ge(y_done.sem, y_done.at(j + 1))
                    step(dve.tensor_tensor(s.u[:, j, :], s.u[:, j, :], s.sz[:, j, :], ALU.mult))
    for c, n in ((bc_ready, 16), (diff_ready, 16), (exp_ready, 16), (att_ready, 16), (y_ready, 16), (y_done, 8)):
        c.passed(n)


def rotate(s):
    rope = s.view(63, 2)
    turned_ready, done = s.pair_sems
    tmp = s.view(66, 2)
    with s.nc.Block() as block:
        @block.sync
        def _(sync):
            sync.dma_start(rope.rearrange("p a t -> p (a t)"), s.I["rope"]).then_inc(s.loaded.sem, 16)

        @block.tensor
        def _(pe):
            for t in range(8):
                if t >= 2:
                    pe.wait_ge(done.sem, done.at(t - 1))
                pe.matmul(s.ps[t % 2][:], s.turn, s.qk[:, t, :], start=True, stop=True).then_inc(turned_ready.sem, 1)

        @block.vector
        def _(dve):
            step = Chain(dve, s.dve_chain)
            dve.wait_ge(s.loaded.sem, s.loaded.at(16))
            for t in range(8):
                dve.wait_ge(turned_ready.sem, turned_ready.at(t + 1))
                step(dve.tensor_tensor(tmp[:, t % 2, :], s.ps[t % 2][:], rope[:, 1, :], ALU.mult))
                step(dve.tensor_tensor(s.qk[:, t, :], s.qk[:, t, :], rope[:, 0, :], ALU.mult))
                dve.tensor_tensor(s.qk[:, t, :], s.qk[:, t, :], tmp[:, t % 2, :], ALU.add).then_inc(done.sem, 1)
    s.loaded.passed(16)
    turned_ready.passed(8)
    done.passed(8)


def retention(s):
    decay = s.view(46, 8)
    s.yr = s.view(63, 8)
    s_ready, s_done, y_ready, y_done, _, _ = s.norm_sems
    with s.nc.Block() as block:
        @block.sync
        def _(sync):
            sync.dma_start(decay.rearrange("p a t -> p (a t)"), s.I["decay"]).then_inc(s.loaded.sem, 16)

        @block.tensor
        def _(pe):
            def scores(h):
                j, lo = h // 2, (h % 2) * RET_QK
                for a in range(TT):
                    if h >= 1:
                        pe.wait_ge(s_done.sem, s_done.at(4 * (h - 1) + a + 1))
                    pe.matmul(s.ps[a][:, 0:seg_width(a)], s.qk[lo:lo + RET_QK, 4 + j, a * P:(a + 1) * P],
                              s.qk[lo:lo + RET_QK, j, a * P:T], start=True, stop=True).then_inc(s_ready.sem, 1)

            scores(0)
            for h in range(RET_HEADS):
                if h >= 2:
                    pe.wait_ge(y_done.sem, y_done.at(h - 1))
                for a in range(TT):
                    pe.wait_ge(s_done.sem, s_done.at(4 * h + a + 1))
                    mm = pe.matmul(s.ps[4 + h % 2][:, a * P:T], s.vt[:, a, h * RET_DV:(h + 1) * RET_DV],
                                   s.att[h % 2][:, SEG[a]:SEG[a] + seg_width(a)], start=a == 0, stop=a == TT - 1, skip_group_check=True)
                mm.then_inc(y_ready.sem, 1)
                if h + 1 < RET_HEADS:
                    scores(h + 1)

        @block.vector
        def _(dve):
            dve.wait_ge(s.loaded.sem, s.loaded.at(16))
            for h in range(RET_HEADS):
                if h >= 2:
                    dve.wait_ge(y_ready.sem, y_ready.at(h - 1))
                for a in range(TT):
                    dve.wait_ge(s_ready.sem, s_ready.at(4 * h + a + 1))
                    dve.tensor_tensor(s.att[h % 2][:, SEG[a]:SEG[a] + seg_width(a)], s.ps[a][:, 0:seg_width(a)],
                                      decay[:, h, 0:seg_width(a)], ALU.mult).then_inc(s_done.sem, 1)

        @block.scalar
        def _(act):
            for h in range(RET_HEADS):
                act.wait_ge(y_ready.sem, y_ready.at(h + 1))
                act.activation(s.yr[:, h, :], s.ps[4 + h % 2][:], ACT.Copy).then_inc(y_done.sem, 1)
    s.loaded.passed(16)
    for c, n in ((s_ready, 32), (s_done, 32), (y_ready, 8), (y_done, 8)):
        c.passed(n)


def first_mixer(s):
    first_projection(s)
    ssd_prepare(s)
    ssd_turn(s)
    ssd_heads(s)
    norm(s, s.u, 8, 4, s.u, s.view(46, 6), False, 0, s.col("ssd_norm"))
    rotate(s)
    retention(s)
    norm(s, s.yr, 8, 1, s.yr, s.view(46, 4), True, 0, s.col("gn_w"), s.col("gn_b"), s.sg)
    both = Split(lambda k: s.u[:, k, :] if k < 8 else s.yr[:, k - 8, :], 16, s.rounded(46),
                 lambda k: s.rounded(8)(k) if k < 8 else s.rounded(63 - 8)(k))
    linears(s, [part("w_mix", both, residual(s, ALPHA), by="dve")])
    norm(s, s.x, 8, 8, s.x, s.view(0, 10), True, 0, s.col("ln1_g"), s.col("ln1_b"))


def attention_unit(q, k, keys, table, slope, ok, scale, v, pieces, channels, row, causal, out):
    u = Names()
    u.q, u.k, u.keys, u.table, u.slope, u.ok, u.scale = q, k, keys, table, slope, ok, scale
    u.v, u.pieces, u.channels, u.row, u.causal, u.out = v, pieces, channels, row, causal, out
    return u


AHEAD = 2
PROBS = 4


def attention(s, units):
    nc = s.nc
    sc_ready, shifted, exp_ready, p_ready, pt_ready, pt_done = s.norm_sems
    o_ready, o_done = s.pair_sems
    steps = [(n, u, a) for n, (u, a) in enumerate((u, a) for u in range(len(units)) for a in range(TT))]
    outs = [(u, m) for u in range(len(units)) for m in range(units[u].pieces)]
    with nc.Block() as block:
        @block.tensor
        def _(pe):
            def scores(n, u, a):
                if n >= 3:
                    pe.wait_ge(shifted.sem, shifted.at(n - 2))
                q, k = units[u].q(a), units[u].k
                w = units[u].keys(a)
                for m in range(len(q)):
                    mm = pe.matmul(s.ps[n % 3][:, 0:w], q[m], k[m][:, 0:w], start=m == 0, stop=m == len(q) - 1)
                mm.then_inc(sc_ready.sem, 1)

            def turned(n, u, a):
                if n >= 3:
                    pe.wait_ge(pt_done.sem, pt_done.at(n - 2))
                pe.wait_ge(p_ready.sem, p_ready.at(n + 1))
                w = units[u].keys(a)
                for st in range(-(-w // P)):
                    ww = min(P, w - st * P)
                    mm = pe.transpose(s.ps[3 + n % 3][0:ww, st * P:(st + 1) * P], s.prob[n % PROBS][:, st * P:st * P + ww], s.eye)
                mm.then_inc(pt_ready.sem, 1)

            def values(u):
                pe.wait_ge(pt_done.sem, pt_done.at(TT * (u + 1)))
                w = units[u].keys(TT - 1)
                n_st = -(-w // P)
                for m in range(units[u].pieces):
                    o = outs.index((u, m))
                    if o >= 2:
                        pe.wait_ge(o_done.sem, o_done.at(o - 1))
                    for st in range(n_st):
                        ww = min(P, w - st * P)
                        lo = st * P if units[u].causal else 0
                        ch = units[u].channels
                        row = units[u].row
                        mm = pe.matmul(s.ps[6 + o % 2][row:row + ch, lo:T], units[u].v(st, m), s.pt[u % 2][0:ww, st, lo:T],
                                       start=st == 0, stop=st == n_st - 1, skip_group_check=True)
                    mm.then_inc(o_ready.sem, 1)

            for m in steps[:AHEAD + 1]:
                scores(*m)
            for n, u, a in steps:
                if n + AHEAD + 1 < len(steps):
                    scores(*steps[n + AHEAD + 1])
                turned(n, u, a)
                if a == 0 and u:
                    values(u - 1)
            values(len(units) - 1)

        @block.vector
        def _(dve):
            step = Chain(dve, s.dve_chain)

            def shift(n, u, a):
                dve.wait_ge(sc_ready.sem, sc_ready.at(n + 1))
                w, un = units[u].keys(a), units[u]
                sc, neg = s.prob[n % PROBS][:, 0:w], s.small[:, 8 + n % PROBS:9 + n % PROBS]
                if n >= PROBS:
                    dve.wait_ge(pt_ready.sem, pt_ready.at(n - PROBS + 1))
                if un.table is not None:
                    step(dve.scalar_tensor_tensor(sc, un.table(a), un.slope, s.ps[n % 3][:, 0:w], ALU.mult, ALU.add))
                else:
                    step(dve.tensor_scalar(sc, s.ps[n % 3][:, 0:w], un.scale, None, ALU.mult))
                dve.tensor_reduce(neg, sc, AX.X, ALU.max, negate=True).then_inc(shifted.sem, 1)

            for m in steps[:AHEAD]:
                shift(*m)
            for n, u, a in steps:
                if n + AHEAD < len(steps):
                    shift(*steps[n + AHEAD])
                dve.wait_ge(exp_ready.sem, exp_ready.at(n + 1))
                w, un = units[u].keys(a), units[u]
                total = s.small[:, 12 + n % PROBS:13 + n % PROBS]
                step(dve.reciprocal(total, total))
                pr = s.prob[n % PROBS][:, 0:w]
                if un.ok is not None:
                    ins = dve.scalar_tensor_tensor(pr, pr, total, un.ok(a), ALU.mult, ALU.mult)
                else:
                    ins = dve.tensor_scalar(pr, pr, total, None, ALU.mult)
                ins.then_inc(p_ready.sem, 1)

        @block.scalar
        def _(act):
            def exps(n, u, a):
                act.wait_ge(shifted.sem, shifted.at(n + 1))
                if n >= PROBS:
                    act.wait_ge(p_ready.sem, p_ready.at(n - PROBS + 1))
                pr = s.prob[n % PROBS][:, 0:units[u].keys(a)]
                act.activation(pr, pr, ACT.Exp, bias=s.small[:, 8 + n % PROBS:9 + n % PROBS],
                               accum_out=s.small[:, 12 + n % PROBS:13 + n % PROBS]).then_inc(exp_ready.sem, 1)

            def take(u):
                for m in range(units[u].pieces):
                    o = outs.index((u, m))
                    act.wait_ge(o_ready.sem, o_ready.at(o + 1))
                    row = units[u].row
                    act.activation(units[u].out(m), s.ps[6 + o % 2][row:row + units[u].channels, :], ACT.Copy).then_inc(o_done.sem, 1)

            for m in steps[:AHEAD]:
                exps(*m)
            for n, u, a in steps:
                if n + AHEAD < len(steps):
                    exps(*steps[n + AHEAD])
                act.wait_ge(pt_ready.sem, pt_ready.at(n + 1))
                w = units[u].keys(a)
                if a == 0 and u >= 2:
                    act.wait_ge(o_ready.sem, o_ready.at(outs.index((u - 1, 0))))
                n_st, ww = -(-w // P), min(P, w)
                act.activation(s.pt[u % 2][0:ww, 0:n_st, a * P:(a + 1) * P],
                               s.ps[3 + n % 3][0:ww, 0:n_st * P].rearrange("p (s q) -> p s q", s=n_st), ACT.Copy).then_inc(pt_done.sem, 1)
                if a == 1 and u:
                    take(u - 1)
            take(len(units) - 1)
    for c in s.norm_sems:
        c.passed(len(steps))
    for c in s.pair_sems:
        c.passed(len(outs))


def cross_attention(s):
    v = s.view
    mem = v(0, 4).rearrange("p a t -> p (a t)").rearrange("p (k m) -> p k m", k=DT)
    xk = v(4, 4).rearrange("p a t -> p (a t)").rearrange("p (k m) -> p k m", k=DT)
    xv = v(8, 4).rearrange("p a t -> p (a t)").rearrange("p (t c) -> p t c", t=2)
    xq, o = v(12, 8), v(20, 8)
    s.prob = [s.arena[:, (28 + k) * T:(29 + k) * T] for k in range(PROBS)]
    s.pt = [v(32 + 4 * k, 4) for k in range(2)]
    with s.nc.Block() as block:
        @block.sync
        def _(sync):
            sync.dma_start(mem.rearrange("p k m -> p (k m)"), s.I["mem"]).then_inc(s.loaded.sem, 16)
            sync.wait_ge(s.loaded.sem, s.loaded.at(16))
    s.loaded.passed(16)

    half = lambda at: lambda k: s.rounded(at)(k // 2)[:, (k % 2) * MEM:(k % 2 + 1) * MEM]
    mem_split = Split(lambda k: mem[:, k, :], DT, half(40), half(44))
    x_split = Split(lambda k: s.x[:, k, :], DT, s.rounded(48), s.rounded(56))
    linears(s, [
        part("w_xk", mem_split, store(lambda t: xk[:, t, :]), n=MEM),
        part("w_xv", lambda k: mem[:, k, :], store_by_token(xv, 2), tokens=2),
        part("w_xq", x_split, store(lambda t: xq[:, t, :])),
    ])

    def unit(h):
        return attention_unit(
            q=lambda a: [xq[:, 2 * h + m, a * P:(a + 1) * P] for m in range(2)], k=[xk[:, 2 * h + m, :] for m in range(2)],
            keys=lambda a: MEM, table=None, slope=None, ok=None, scale=XHD ** -0.5,
            v=lambda st, m: xv[:, st, h * XHD + m * P:h * XHD + (m + 1) * P], pieces=2, channels=P, row=0, causal=False,
            out=lambda m: o[:, 2 * h + m, :])

    attention(s, [unit(h) for h in range(XH)])
    linears(s, [part("w_xo", Split(lambda k: o[:, k, :], DT, s.rounded(40), s.rounded(20)), residual(s, ALPHA), by="dve")])
    norm(s, s.x, 8, 8, s.x, v(0, 10), True, 0, s.col("ln2_g"), s.col("ln2_b"))


def conv_glu(s):
    v = s.view
    gated = v(0, FF_TILES)
    up = s.arena[:, 22 * T:22 * T + 2 * (T + 2)].rearrange("p (n t) -> p n t", n=2)
    acc = v(27, 2)
    silu_ready = s.norm_sems[0]
    nc = s.nc
    with nc.Block() as block:
        @block.gpsimd
        def _(pool):
            pool.memset(up[:, :, 0:2], 0.0)

    one = lambda name, t: s.col(name)[:, bass.ds(t, 1)]

    def evac(dve, step, t, ps):
        odd = evac.turn % 2
        evac.turn += 1
        src, dst = up[:, odd, :], acc[:, odd, :]
        step(dve.tensor_scalar(src[:, 2:2 + T], ps, one("b_up", t), None, ALU.add))
        step(dve.tensor_scalar(dst, src[:, 0:T], one("ffn_conv0", t), None, ALU.mult))
        step(dve.scalar_tensor_tensor(dst, src[:, 1:1 + T], one("ffn_conv1", t), dst, ALU.mult, ALU.add))
        ins = dve.scalar_tensor_tensor(dst, src[:, 2:2 + T], one("ffn_conv2", t), dst, ALU.mult, ALU.add)
        if not odd:
            return ins
        step(ins)
        dve.wait_ge(silu_ready.sem, silu_ready.at(t // 2 + 1))
        return dve.scalar_tensor_tensor(gated[:, t // 2, :], dst, one("ffn_conv_b", t), gated[:, t // 2, :], ALU.add, ALU.mult)

    def silu(act, tile0, t):
        act.wait_ge(s.evac_done.sem, tile0 + t + 1)
        if not isinstance(t, int):
            act.sem_inc(s.held, 1)
        act.activation(gated[:, t // 2, :], acc[:, 0, :], ACT.Silu, bias=one("ffn_conv_b", t)).then_inc(silu_ready.sem, 1)

    def side(act, step, p, t, u):
        if u % 2 == 0 and not (isinstance(t, int) and t < 2):
            silu(act, p.tile0, t - 2)

    def last_silu(act):
        silu(act, s.tiles - 2 * FF_TILES, 2 * FF_TILES - 2)

    evac.turn = 0
    linears(s, [part("w_up", Split(lambda k: s.x[:, k, :], DT, s.rounded(53), s.rounded(61)), evac, by="dve", steps=3.5, side=side)], after=dict(scalar=last_silu))
    silu_ready.passed(FF_TILES)
    linears(s, [part("w_down", Split(lambda k: gated[:, k, :], FF_TILES, s.rounded(22), s.rounded(0)), residual(s, ALPHA), by="dve")])
    norm(s, s.x, 8, 8, s.x, v(0, 10), True, 0, s.col("ln3_g"), s.col("ln3_b"))


def store_out(s, out):
    with s.nc.Block() as block:
        @block.sync
        def _(sync):
            sync.dma_start(out, s.xflat).then_inc(s.loaded.sem, 16)
            sync.wait_ge(s.loaded.sem, s.loaded.at(16))
    s.loaded.passed(16)


def rounded_tile(s, t, arena_at):
    if t not in s.rounded_tiles:
        s.rounded_tiles[t] = s.nc.alloc_sbuf_tensor_at(f"rounded{t}", [P, T], F32R, offset=arena_at + 4 * T * t)[:]
    return s.rounded_tiles[t]


def build(nc, I, at, out, upto=99):
    s = Names()
    s.nc, s.I, s.next_part, s.tiles, s.units, s.split_units, s.slab_end, s.first_slab = nc, I, 0, 0, 0, 0, [], [0]
    for name, _, _ in PLAN:
        s.first_slab.append(s.first_slab[-1] + I[name].shape[0])
    s.x = nc.alloc_sbuf_tensor("x_res", [P, DT, T], F32)[:]
    s.xflat = s.x.rearrange("p k t -> p (k t)")
    s.ring = nc.alloc_sbuf_tensor("weight_ring", [P, RING, SLAB], F32)[:]
    s.base = nc.alloc_sbuf_tensor("base_tables", [P, 4 * P + 2], F32)
    s.par = nc.alloc_sbuf_tensor("params_sb", [P, I["params"].shape[1]], F32)
    s.small = nc.alloc_sbuf_tensor("small", [P, 256], F32)
    arena_at = nc.sbuf_base
    s.arena = nc.alloc_sbuf_tensor("arena", [P, 74 * T], F32)
    s.rounded_tiles = {}
    s.rounded = lambda at: lambda k: rounded_tile(s, at + k, arena_at)
    s.w_hi, s.w_lo = ([nc.alloc_sbuf_tensor(f"weights_{name}{k}", [P, UNIT_K * P], F32R)[:] for k in range(UNITS)] for name in ("hi", "lo"))
    s.ps = [nc.alloc_psum_tensor(f"bank{b}", [P, T], F32) for b in range(8)]
    s.eye, s.turn, s.causal, s.ones = (s.base[:, k * P:(k + 1) * P] for k in range(4))
    s.eps = [s.base[:, 4 * P + k:4 * P + k + 1] for k in range(2)]
    s.col = lambda name: s.par[:, at[name][0]:at[name][0] + at[name][1]]
    s.view = lambda o, n: s.arena[:, o * T:(o + n) * T].rearrange("p (a t) -> p a t", t=T)
    s.slab_ready = [nc.alloc_semaphore(f"slab_ready{k}") for k in range(RING)]
    names = ("loaded", "units_done", "evac_done", "hi_made", "lo_made", "act_hi", "act_lo", "act_chain", "dve_chain")
    (s.loaded, s.units_done, s.evac_done, s.hi_made, s.lo_made, s.act_hi, s.act_lo, s.act_chain, s.dve_chain) = (Counter(nc, n) for n in names)
    s.norm_sems = [Counter(nc, f"step{k}_ready") for k in range(6)]
    s.pair_sems = [Counter(nc, f"pair{k}_ready") for k in range(2)]
    s.gathered = [Counter(nc, f"gathered{k}") for k in range(2 * GATHER)]
    s.held = nc.alloc_semaphore("held")
    s.mod_sems = [Counter(nc, n) for n in ("silu_ready", "row_turned")]
    s.convolved = Counter(nc, "convolved")
    s.cond_loaded, s.cols_ready = Counter(nc, "cond_loaded"), Counter(nc, "cols_ready")
    stages = STAGES[:upto]
    load_start(s)
    for stage in stages:
        stage(s)
    store_out(s, out)


def second_inputs_projected(s):
    v = s.view
    s.n = v(0, 8)
    norm(s, s.x, 8, 8, s.n, v(8, 10), False, 1, s.col("norm_mix"))
    s.ab, s.ry, s.ax = v(16, 8), v(35, RT), v(45, 8)
    s.rx = s.arena[:, 24 * T:24 * T + RT * (T + 3)].rearrange("p (a t) -> p a t", a=RT)
    s.cx = s.arena[:, 53 * T:53 * T + 8 * (T + 2)].rearrange("p (a t) -> p a t", a=8)
    with s.nc.Block() as block:
        @block.gpsimd
        def _(pool):
            pool.memset(s.cx[:, :, 0:2], 0.0)
            pool.memset(s.rx[:, :, 0:3], 0.0)
    n = s.n_split = Split(lambda k: s.n[:, k, :], DT, s.rounded(8), s.rounded(0))

    s.rc = s.view(45, RT)

    def conv_a(dve, step, p, t, u):
        if not (isinstance(t, int) and t >= 8):
            taps = [s.col(f"conv_a{k}") for k in range(3)]
            step(causal_conv(s, dve, step, s.ax[:, t, :], lambda k: s.cx[:, t, k:k + T], taps, bass.ds(t, 1)))
            step(dve.tensor_tensor(s.ab[:, t, :], s.ab[:, t, :], s.ax[:, t, :], ALU.mult))

    def conv_r(dve, step, p, t, u):
        taps = [s.col(f"rnn_conv{k}") for k in range(4)]
        step(causal_conv(s, dve, step, s.rc[:, t, :], lambda k: s.rx[:, t, k:k + T], taps, bass.ds(t, 1)))
        step(dve.tensor_scalar(s.rc[:, t, :], s.rc[:, t, :], s.col("rnn_conv_b")[:, bass.ds(t, 1)], None, ALU.add))

    linears(s, [part("w2_ax", n, store(lambda t: s.ax[:, t, :]))])
    linears(s, [
        part("w2_ac", n, lambda dve, step, t, ps: dve.tensor_tensor(s.cx[:, t, 2:2 + T], ps, s.ax[:, t, :], ALU.mult), by="dve"),
        part("w2_ab", n, store(lambda t: s.ab[:, t, :])),
        part("w2_rx", n, store(lambda t: s.rx[:, t, 3:3 + T]), side=conv_a, side_steps=16, side_after="w2_ab"),
        part("w2_ry", n, store(lambda t: s.ry[:, t, :], ACT.Gelu_apprx_tanh), side=conv_r, side_steps=20, side_after="w2_rx"),
    ])


def rates(s):
    cols = [s.small[:, 16 + 16 * k:16 + 16 * k + RT] for k in range(6)]
    neg_lam, s.rate, e, w, d, s.neg_rate = cols
    with s.nc.Block() as block:
        @block.vector
        def _(dve):
            step = Chain(dve, s.dve_chain)
            step(dve.tensor_scalar(neg_lam, s.col("lru_lambda"), -1.0, None, ALU.mult))
    softplus_rows(s, [(neg_lam, s.rate, e, w, d, False)])
    with s.nc.Block() as block:
        @block.vector
        def _(dve):
            step = Chain(dve, s.dve_chain)
            step(dve.tensor_scalar(s.neg_rate, s.rate, -8.0, None, ALU.mult))
            step(dve.tensor_scalar(s.rate, s.rate, 8.0, None, ALU.mult))


def recurrence(s):
    v = s.view
    r, gate, a = v(24, RT), v(55, RT), v(55, RT)
    rc = lambda k: s.rc[:, k, :]
    linears(s, [
        part("w2_rg", rc, store(lambda t: r[:, t, :], ACT.Sigmoid, lambda t: s.col("b_rg")[:, t:t + 1]), block_diag=True),
        part("w2_ig", rc, store(lambda t: gate[:, t, :], ACT.Sigmoid, lambda t: s.col("b_ig")[:, t:t + 1]), block_diag=True),
    ])
    square = v(65, 2)
    gated, a_ready, tanh_ready, room_ready, root_ready, _ = s.norm_sems
    with s.nc.Block() as block:
        @block.scalar
        def _(act):
            act.wait_ge(gated.sem, gated.at(1))
            for t in range(RT):
                act.activation(a[:, t, :], r[:, t, :], ACT.Exp, scale=s.neg_rate[:, t:t + 1]).then_inc(a_ready.sem, 1)
            for t in range(RT):
                act.activation(r[:, t, :], r[:, t, :], ACT.Tanh, scale=s.rate[:, t:t + 1]).then_inc(tanh_ready.sem, 1)
            for t in range(RT):
                act.wait_ge(room_ready.sem, room_ready.at(t + 1))
                act.activation(r[:, t, :], r[:, t, :], ACT.Sqrt).then_inc(root_ready.sem, 1)

        @block.vector
        def _(dve):
            step = Chain(dve, s.dve_chain)
            dve.tensor_tensor(s.rc, s.rc, gate, ALU.mult).then_inc(gated.sem, 1)
            for t in range(RT):
                sq = square[:, t % 2, :]
                dve.wait_ge(a_ready.sem, a_ready.at(t + 1))
                step(dve.tensor_tensor(sq, a[:, t, :], a[:, t, :], ALU.mult))
                dve.wait_ge(tanh_ready.sem, tanh_ready.at(t + 1))
                step(dve.scalar_tensor_tensor(r[:, t, :], sq, 1.0, r[:, t, :], ALU.add, ALU.mult))
                dve.tensor_scalar(r[:, t, :], r[:, t, :], 0.0, None, ALU.max).then_inc(room_ready.sem, 1)
            dve.wait_ge(gated.sem, gated.at(1))
            for t in range(RT):
                dve.wait_ge(root_ready.sem, root_ready.at(t + 1))
                step(dve.tensor_tensor(s.rc[:, t, :], s.rc[:, t, :], r[:, t, :], ALU.mult))
                step(dve.tensor_tensor_scan(r[:, t, :], a[:, t, :], s.rc[:, t, :], 0.0, ALU.mult, ALU.add))
                dve.tensor_tensor(s.ry[:, t, :], s.ry[:, t, :], r[:, t, :], ALU.mult)
    gated.passed(1)
    for c in (a_ready, tanh_ready, room_ready, root_ready):
        c.passed(RT)


def second_mixer(s):
    v = s.view
    second_inputs_projected(s)
    rates(s)
    recurrence(s)
    ga, gb, merged = v(45, 8), v(53, 8), v(61, 8)
    linears(s, [
        part("w2_ga", s.n_split, store(lambda t: ga[:, t, :], ACT.Sigmoid)),
        part("w2_gb", s.n_split, store(lambda t: gb[:, t, :], ACT.Sigmoid)),
    ])

    def add_b(dve, step, t, ps):
        step(dve.tensor_tensor(gb[:, t, :], ps, gb[:, t, :], ALU.mult))
        return dve.tensor_tensor(merged[:, t, :], merged[:, t, :], gb[:, t, :], ALU.add)

    linears(s, [
        part("w2_out_a", Split(lambda k: s.ab[:, k, :], DT, s.rounded(24), s.rounded(16)), lambda dve, step, t, ps: dve.tensor_tensor(merged[:, t, :], ps, ga[:, t, :], ALU.mult), by="dve"),
        part("w2_out_b", Split(lambda k: s.ry[:, k, :], RT, s.rounded(0), s.rounded(35)), add_b, by="dve", steps=1),
    ])
    linears(s, [part("w2_o", Split(lambda k: merged[:, k, :], DT, s.rounded(0), s.rounded(61)), residual(s), by="dve")])


def turn_tiles(s, src, dst):
    ready, taken = s.pair_sems
    with s.nc.Block() as block:
        @block.tensor
        def _(pe):
            for n in range(2 * TT):
                a, half = n // 2, n % 2
                if n >= 2:
                    pe.wait_ge(taken.sem, taken.at(n - 1))
                for u in range(4):
                    mm = pe.transpose(s.ps[n % 2][:, u * P:(u + 1) * P], src[:, half * 4 + u, a * P:(a + 1) * P], s.eye)
                mm.then_inc(ready.sem, 1)

        @block.vector
        def _(dve):
            for n in range(2 * TT):
                dve.wait_ge(ready.sem, ready.at(n + 1))
                dve.tensor_copy(dst[:, n // 2, (n % 2) * 512:(n % 2) * 512 + 512], s.ps[n % 2][:]).then_inc(taken.sem, 1)
    ready.passed(2 * TT)
    taken.passed(2 * TT)


PHASES = [("u", 0), ("u", 1), ("v", 0), ("u", 2), ("v", 1), ("u", 3), ("v", 2), ("v", 3)]
CHOICE = {0: (1, 0, PEER_H), 1: (2, 0, PEER_H // 2), 2: (2, PEER_H // 2, PEER_H), 3: (3, 0, PEER_H // 2), 4: (3, PEER_H // 2, PEER_H)}
ROWS = 2 * GATHER
TURNS = SLOTS // ROWS


def experts(s, q, n_tok, y, keys, scratch):
    score = lambda a, c: s.ps[4 * ((a + 1) % 2) + c // 4][:, (c % 4) * P:(c % 4 + 1) * P]
    flat = lambda x: x.rearrange("p h k -> p (h k)")
    f = lambda o, n: scratch[:, o:o + n]
    g = lambda o: s.arena[:, 68 * T + o:68 * T + o + 256].rearrange("p (c k) -> p c k", k=PEER_K)
    val, ind, indf = g(0), g(256).bitcast(U32), g(512)
    rest, cand = f(0, 256), f(256, 256)
    top = [f(512 + SLOTS * k, SLOTS).rearrange("p (h k) -> p h k", k=PEER_K) for k in range(2)]
    pos, digit = [f(768 + SLOTS * k, SLOTS).bitcast(U32) for k in range(2)]
    digitf, number, second_number = [f(1024 + SLOTS * k, SLOTS) for k in range(3)]
    biggest, total, iota = f(1408, PEER_H), f(1416, PEER_H), f(1424, PEER_K)
    match = f(1440, SLOTS * PEER_K).rearrange("p (h k i) -> p h k i", h=PEER_H, k=PEER_K)
    act_ = s.arena[:, 72 * T:73 * T]
    place = s.small[:, 192:192 + ROWS].bitcast(U32)
    of_tile = lambda x, a: x[:, a * SLOTS:(a + 1) * SLOTS]
    sc_ready, sorted_, shifted, exp_ready, chosen, gelu_ready = s.norm_sems
    numbers_ready, used = s.pair_sems
    def scores(pe, a):
        for c in range(2 * PEER_H):
            mm = pe.matmul(score(a, c), q[:, c, a * P:(a + 1) * P], keys[:, c, :], start=True, stop=True)
        mm.then_inc(sc_ready.sem, 1)

    def best(dve, step, values, numbers, src, spare):
        step(dve.max(values[:, 0:8], src))
        dve.max_index(numbers[:, 0:8], values[:, 0:8], src)
        step(dve.match_replace(spare, values[:, 0:8], src, -3.0e38))
        step(dve.max(values[:, 8:16], spare))
        step(dve.max_index(numbers[:, 8:16], values[:, 8:16], spare))

    def choose_head(dve, step, a, h):
        for c in (2 * h, 2 * h + 1):
            best(dve, step, val[:, c, :], ind[:, c, :], score(a, c), rest[:, 0:NKEYS])
        step(dve.tensor_tensor(cand.rearrange("p (i j) -> p i j", i=PEER_K),
                               val[:, 2 * h, :].unsqueeze(2).broadcast_to([P, PEER_K, PEER_K]),
                               val[:, 2 * h + 1, :].unsqueeze(1).broadcast_to([P, PEER_K, PEER_K]), ALU.add))
        best(dve, step, top[a % 2][:, h, :], pos[:, h * PEER_K:(h + 1) * PEER_K], cand, rest)

    def numbers(dve, step, a):
        t = top[a % 2]
        dve.tensor_copy(biggest, t[:, :, 0]).then_inc(sorted_.sem, 1)
        step(dve.tensor_copy(indf, ind))
        for half, found in enumerate((number, second_number)):
            if half == 0:
                step(dve.tensor_scalar(digit, pos, 4, None, ALU.logical_shift_right))
            else:
                step(dve.tensor_scalar(digit, pos, PEER_K - 1, None, ALU.bitwise_and))
            step(dve.tensor_copy(digitf, digit))
            step(dve.tensor_tensor(match.rearrange("p h k i -> p (h k) i"),
                                   iota.unsqueeze(1).broadcast_to([P, SLOTS, PEER_K]),
                                   digitf.unsqueeze(2).broadcast_to([P, SLOTS, PEER_K]), ALU.is_equal))
            keys_of = indf.rearrange("p (h two) k -> p h two k", two=2)[:, :, half, :]
            step(dve.tensor_tensor(match, match, keys_of.unsqueeze(2).broadcast_to([P, PEER_H, PEER_K, PEER_K]), ALU.mult))
            step(dve.tensor_reduce(found, match.rearrange("p h k i -> p (h k) i"), AX.X, ALU.add))
        step(dve.scalar_tensor_tensor(number, number, float(NKEYS), second_number, ALU.mult, ALU.add))
        dve.tensor_copy(of_tile(s.expert, a), number).then_inc(chosen.sem, 1)
        dve.wait_ge(sorted_.sem, sorted_.at(a + 1))
        dve.tensor_tensor(t, t, biggest.unsqueeze(2).broadcast_to([P, PEER_H, PEER_K]), ALU.subtract).then_inc(shifted.sem, 1)

    def load_keys(sync):
        sync.dma_start(keys.rearrange("p c n -> p (c n)"), s.I["keys"]).then_inc(s.loaded.sem, 16)
        sync.dma_start(iota, s.I["iota"]).then_inc(s.loaded.sem, 16)

    def first_scores(pe):
        pe.wait_ge(s.loaded.sem, s.loaded.at(32))
        scores(pe, 0)

    def first_choice(dve):
        step = Chain(dve, s.dve_chain)
        dve.wait_ge(s.loaded.sem, s.loaded.at(32))
        dve.wait_ge(sc_ready.sem, sc_ready.at(1))
        for h in range(PEER_H):
            choose_head(dve, step, 0, h)
        numbers(dve, step, 0)

    modulation(s, s.arena[0:1, 36 * T:36 * T + 6 * D], first_scores, first_choice, load_keys)
    with s.nc.Block() as block:
        @block.tensor
        def _(pe):
            for a in range(1, TT):
                if a >= 2:
                    pe.wait_ge(sorted_.sem, sorted_.at(a - 1))
                scores(pe, a)

        @block.scalar
        def _(act):
            def place_numbers(phase, turn, half):
                a = PHASES[phase][1]
                act.activation(place[:, half * GATHER:(half + 1) * GATHER],
                               s.expert[:, bass.ds(a * SLOTS + turn * ROWS + half * GATHER, GATHER)], ACT.Copy).then_inc(numbers_ready.sem, 1)

            def places_free(phase, turn, half):
                for j in range(half * GATHER, (half + 1) * GATHER):
                    act.wait_ge(s.gathered[j].sem, s.gathered[j].at(16 * (phase * TURNS + turn)))
                act.sem_inc(s.held, 1)

            def exp_top(a):
                act.wait_ge(shifted.sem, shifted.at(a + 1))
                act.activation(flat(top[a % 2]), flat(top[a % 2]), ACT.Exp).then_inc(exp_ready.sem, 1)

            for phase, (table, a) in enumerate(PHASES):
                act.wait_ge(chosen.sem, chosen.at(a + 1))
                for half in range(2):
                    if phase:
                        places_free(phase, 0, half)
                    place_numbers(phase, 0, half)
                if phase == 0:
                    exp_top(0)
                elif CHOICE.get(phase - 1, (0, 0, 0))[2] == PEER_H:
                    exp_top(CHOICE[phase - 1][0])
                if phase and PHASES[phase - 1][0] == "u":
                    b = PHASES[phase - 1][1]
                    act.wait_ge(used.sem, used.at(phase * SLOTS))
                    act.activation(of_tile(act_, b), of_tile(act_, b), ACT.Gelu_apprx_tanh).then_inc(gelu_ready.sem, 1)
                with act.Fori(1, TURNS) as turn:
                    for half in range(2):
                        places_free(phase, turn, half)
                        place_numbers(phase, turn, half)

        @block.gpsimd
        def _(pool):
            def gather(phase, turn, j):
                if j % GATHER == 0:
                    pool.wait_ge(numbers_ready.sem, numbers_ready.at(2 * (phase * TURNS + turn) + j // GATHER + 1))
                if phase or not isinstance(turn, int):
                    pool.wait_ge(used.sem, used.at(ROWS * (phase * TURNS + turn) - ROWS + j + 1))
                    pool.sem_inc(s.held, 1)
                pool.indirect_dma_start(out=s.rows[:, j, :], out_offset=None, in_=s.I["expert_" + PHASES[phase][0]],
                                        in_offset=bass.IndirectOffsetOnAxis(ap=place[:, j:j + 1], axis=0)).then_inc(s.gathered[j].sem, 16)

            for phase in range(len(PHASES)):
                for j in range(ROWS):
                    gather(phase, 0, j)
                with pool.Fori(1, TURNS) as turn:
                    for j in range(ROWS):
                        gather(phase, turn, j)

        @block.vector
        def _(dve):
            step = Chain(dve, s.dve_chain)

            def weights(a):
                dve.wait_ge(exp_ready.sem, exp_ready.at(a + 1))
                t = top[a % 2]
                step(dve.tensor_reduce(total, t, AX.X, ALU.add))
                step(dve.reciprocal(total, total))
                step(dve.tensor_tensor(of_tile(s.gate, a).rearrange("p (h k) -> p h k", k=PEER_K), t,
                                       total.unsqueeze(2).broadcast_to([P, PEER_H, PEER_K]), ALU.mult))

            def use(phase, turn):
                table, a = PHASES[phase]
                for j in range(ROWS):
                    slot, n = turn * ROWS + j, phase * TURNS + turn
                    row = s.rows[:, j, :]
                    dve.wait_ge(s.gathered[j].sem, s.gathered[j].at((n + 1) * 16))
                    if table == "u":
                        ins = dve.scalar_tensor_tensor(row, row, 1.0, n_tok[:, a, :], ALU.mult, ALU.mult,
                                                       accum_out=act_[:, bass.ds(a * SLOTS + slot, 1)])
                    else:
                        dve.wait_ge(used.sem, used.at(n * ROWS + j))
                        ins = dve.scalar_tensor_tensor(y[:, a, :], row, s.gate[:, bass.ds(a * SLOTS + slot, 1)], y[:, a, :], ALU.mult, ALU.add)
                    ins.then_inc(used.sem, 1)

            for phase, (table, a) in enumerate(PHASES):
                if phase == 1:
                    weights(0)
                if CHOICE.get(phase - 1, (0, 0, 0))[2] == PEER_H:
                    weights(CHOICE[phase - 1][0])
                if table == "v":
                    dve.wait_ge(sc_ready.sem, sc_ready.at(TT))
                    dve.wait_ge(gelu_ready.sem, gelu_ready.at(a + 1))
                    step(dve.tensor_tensor(of_tile(s.gate, a), of_tile(s.gate, a), of_tile(act_, a), ALU.mult))
                    step(dve.memset(y[:, a, :], 0.0))
                tile, h0, h1 = CHOICE.get(phase, (0, 0, 0))
                pieces = 4 if h1 else 1
                if h1:
                    dve.wait_ge(sc_ready.sem, sc_ready.at(tile + 1))
                for piece in range(pieces):
                    for h in range(h0 + piece * (h1 - h0) // pieces, h0 + (piece + 1) * (h1 - h0) // pieces):
                        choose_head(dve, step, tile, h)
                        if h == PEER_H - 1:
                            numbers(dve, step, tile)
                    with dve.Fori(piece * TURNS // pieces, (piece + 1) * TURNS // pieces) as turn:
                        use(phase, turn)
    s.loaded.passed(32)
    for c in s.norm_sems:
        c.passed(TT)
    numbers_ready.passed(2 * TURNS * len(PHASES))
    used.passed(SLOTS * len(PHASES))
    for c in s.gathered:
        c.passed(16 * TURNS * len(PHASES))


def peer(s):
    v = s.view
    n, q = v(0, 8), v(8, 16)
    tokens = lambda o: v(o, 8).rearrange("p a t -> p (a t)").rearrange("p (a c) -> p a c", a=TT)
    n_tok, y = tokens(28), tokens(8)
    s.rows = v(36, 32).rearrange("p a t -> p (a t)").rearrange("p (j d) -> p j d", d=D)
    s.expert, s.gate = s.arena[:, 70 * T:71 * T].bitcast(U32), s.arena[:, 71 * T:72 * T]
    keys = s.arena[:, 24 * T:28 * T].rearrange("p (c n) -> p c n", n=NKEYS)
    norm(s, s.x, 8, 8, n, v(8, 10), False, 1, s.col("norm_ffn"))
    linears(s, [part("w2_q", Split(lambda k: n[:, k, :], DT, s.rounded(24), s.rounded(32)), store(lambda t: q[:, t, :]))])
    turn_tiles(s, n, n_tok)
    experts(s, q, n_tok, y, keys, s.arena[:, 0:8 * T])

    ready, taken = s.pair_sems
    with s.nc.Block() as block:
        @block.tensor
        def _(pe):
            for k in range(DT):
                if k >= 2:
                    pe.wait_ge(taken.sem, taken.at(k - 1))
                for a in range(TT):
                    mm = pe.transpose(s.ps[k % 2][:, a * P:(a + 1) * P], y[:, a, k * P:(k + 1) * P], s.eye)
                mm.then_inc(ready.sem, 1)

        @block.vector
        def _(dve):
            for k in range(DT):
                dve.wait_ge(ready.sem, ready.at(k + 1))
                dve.tensor_tensor(s.x[:, k, :], s.x[:, k, :], s.ps[k % 2][:], ALU.add).then_inc(taken.sem, 1)
    ready.passed(DT)
    taken.passed(DT)
    norm(s, s.x, 8, 8, s.x, v(10, 10), False, 1, s.col("norm_final"))


def modulation(s, row, tensor, vector, sync):
    mod = s.small[:, 64:64 + 6 * DT]
    cond = s.small[:, 120:120 + DT]
    silu_ready, turned = s.mod_sems
    tiles = 6 * DT

    def load(eng):
        sync(eng)
        eng.dma_start(cond, s.I["c"]).then_inc(s.cond_loaded.sem, 16)

    def silu(act):
        act.wait_ge(s.cond_loaded.sem, s.cond_loaded.at(16))
        act.activation(cond, cond, ACT.Silu).then_inc(silu_ready.sem, 1)

    def first_scores(pe):
        tensor(pe)
        pe.wait_ge(silu_ready.sem, silu_ready.at(1))

    def turn(pe):
        pe.wait_ge(s.evac_done.sem, s.tiles)
        for t in range(tiles):
            mm = pe.matmul(s.ps[0][:, t:t + 1], row[:, t * P:(t + 1) * P], s.ones[0:1, 0:1], start=True, stop=True)
        mm.then_inc(turned.sem, 1)

    def columns(dve):
        step = Chain(dve, s.dve_chain)
        dve.wait_ge(turned.sem, turned.at(1))
        step(dve.tensor_tensor(mod, s.ps[0][:, 0:tiles], s.col("b_ada"), ALU.add))
        dve.scalar_tensor_tensor(s.gain1, s.gain1, 1.0, s.col("g_norm1"), ALU.add, ALU.mult)
        dve.scalar_tensor_tensor(s.gain2, s.gain2, 1.0, s.col("g_norm2"), ALU.add, ALU.mult)

    s.shift1, s.gain1, s.gate1, s.shift2, s.gain2, s.gate2 = (mod[:, k * DT:(k + 1) * DT] for k in range(6))
    linears(s, [part("w3_ada", lambda k: cond[:, k:k + 1], store(lambda t: row[:, bass.ds(t * 256, 256)]), tile=1, tokens=1)],
            before=dict(sync=load, scalar=silu, tensor=first_scores, vector=vector), after=dict(tensor=turn, vector=columns))
    s.cond_loaded.passed(16)
    for c in s.mod_sems:
        c.passed(1)


def third_projection(s):
    v = s.view
    s.h = v(0, 8)
    norm(s, s.x, 8, 8, s.h, v(8, 10), False, 1, s.gain1, s.shift1)
    s.gu, s.gv, s.mv, s.mo, s.nq, s.kvc, s.ksw = v(8, 4), v(12, 4), v(25, 4), v(29, 4), v(35, 4), v(39, 2), v(41, 4)
    s.mqk = s.arena[:, 16 * T:16 * T + 8 * (T + 3)].rearrange("p (a t) -> p a t", a=8)

    s.vsw = s.arena[:, 45 * T:47 * T].rearrange("p (a c) -> p a c", a=TT)
    s.mi, s.mf, s.ng = s.arena[0:4, 33 * T:34 * T], s.arena[0:4, 34 * T:35 * T], s.arena[0:24, 47 * T:48 * T]
    with s.nc.Block() as block:
        @block.gpsimd
        def _(pool):
            pool.memset(s.mqk[:, :, 0:3], 0.0)
    whole = lambda k: s.h[:, k, :]
    h = Split(whole, DT, s.rounded(56), s.rounded(64))
    s.conv_qk = v(48, 8)
    taps = [s.col(f"ml_conv{k}") for k in range(4)]

    def conv(first):
        def side(dve, step, p, t, u):
            t += first
            ins = causal_conv(s, dve, step, s.conv_qk[:, t, :], lambda k: s.mqk[:, t, k:k + T], taps, bass.ds(t, 1))
            ins.then_inc(s.convolved.sem, 1)
        return side

    def store_values(act, step, t, ps):
        for k in (2 * t, 2 * t + 1):
            act.wait_ge(s.convolved.sem, s.convolved.at(k + 1))
            act.activation(s.conv_qk[:, k, :], s.conv_qk[:, k, :], ACT.Silu, bias=s.col("ml_conv_b")[:, k:k + 1])
        return act.activation(s.vsw[:, t, :], ps, ACT.Copy)


    linears(s, [
        part("w3_gu", h, store(lambda t: s.gu[:, t, :], ACT.Gelu_apprx_tanh)),
        part("w3_gv", h, store(lambda t: s.gv[:, t, :], ACT.Gelu_apprx_tanh)),
        part("w3_mqk", h, store(lambda t: s.mqk[:, t, 3:3 + T])),
        part("w3_mv", whole, store_by_token(s.mv, TT), tokens=TT),
        part("w3_mo", h, store(lambda t: s.mo[:, t, :], ACT.Sigmoid), side=conv(0), side_after="w3_mqk"),
        part("w3_mi", whole, store(lambda t: s.mi, ACT.Identity, lambda t: s.col("ml_bi")[0:4, :]), tile=4),
        part("w3_mf", whole, store(lambda t: s.mf, ACT.Identity, lambda t: s.col("ml_bf")[0:4, :]), tile=4),
        part("w3_nq", h, store(lambda t: s.nq[:, t, :], scale=NSA_DH ** -0.5), side=conv(4)),
        part("w3_kvc", h, store(lambda t: s.kvc[:, t, :])),
        part("w3_ksw", h, store(lambda t: s.ksw[:, t, :])),
        part("w3_vsw", whole, store_values, tokens=TT),
        part("w3_ng", whole, store(lambda t: s.ng, ACT.Sigmoid), tile=24),
    ])
    s.convolved.passed(8)


def spatial_gating(s):
    v = s.view
    norm(s, s.gv, 4, 4, s.gv, v(56, 6), True, 1, s.col("gm_ln_g"), s.col("gm_ln_b"))
    by_token = v(56, 4)
    w = s.arena[:, 60 * T:61 * T].rearrange("p (g t) -> p g t", g=4)
    b = s.arena[:, 61 * T:62 * T].rearrange("p (g t) -> p g t", g=4)
    tmp = v(62, 4)
    turned, taken, masked, mixed, _, _ = s.norm_sems
    with s.nc.Block() as block:
        @block.sync
        def _(sync):
            sync.dma_start(w.rearrange("p g t -> p (g t)"), s.I["gm_w"]).then_inc(s.loaded.sem, 16)
            sync.dma_start(b.rearrange("p g t -> p (g t)"), s.I["gm_b"]).then_inc(s.loaded.sem, 16)

        @block.tensor
        def _(pe):
            for a in range(TT):
                for g in range(4):
                    mm = pe.transpose(s.ps[a][:, g * P:(g + 1) * P], s.gv[:, g, a * P:(a + 1) * P], s.eye)
                mm.then_inc(turned.sem, 1)
            pe.wait_ge(taken.sem, taken.at(TT))
            pe.wait_ge(masked.sem, masked.at(1))
            for g in range(4):
                for a in range(TT):
                    mm = pe.matmul(s.ps[4 + g][:, a * P:(a + 1) * P], by_token[:, a, g * P:(g + 1) * P], w[:, g, :], start=True, stop=True)
                mm.then_inc(mixed.sem, 1)

        @block.vector
        def _(dve):
            step = Chain(dve, s.dve_chain)
            dve.wait_ge(s.loaded.sem, s.loaded.at(32))
            dve.tensor_tensor(w, w, s.causal.unsqueeze(1).broadcast_to([P, 4, P]), ALU.mult).then_inc(masked.sem, 1)
            for a in range(TT):
                dve.wait_ge(turned.sem, turned.at(a + 1))
                dve.tensor_copy(by_token[:, a, :], s.ps[a][:]).then_inc(taken.sem, 1)
            for g in range(4):
                dve.wait_ge(mixed.sem, mixed.at(g + 1))
                step(dve.tensor_tensor(tmp[:, g, :].rearrange("p (a t) -> p a t", a=TT), s.ps[4 + g][:].rearrange("p (a t) -> p a t", a=TT),
                                       b[:, g, :].unsqueeze(1).broadcast_to([P, TT, P]), ALU.add))
                dve.tensor_tensor(s.gu[:, g, :], s.gu[:, g, :], tmp[:, g, :], ALU.mult)
    s.loaded.passed(32)
    for c, n in ((turned, TT), (taken, TT), (masked, 1), (mixed, 4)):
        c.passed(n)


def mlstm(s):
    v = s.view
    qk = s.conv_qk
    s.yb = v(12, 4)
    row = lambda k: s.arena[0:4, k * T:(k + 1) * T]
    lf, e, w, d, F, g, M, m = (row(56 + k) for k in range(8))
    g_col = s.small[:, 128:144].rearrange("p (a h) -> p a h", a=TT)
    att = s.arena[:, 64 * T:64 * T + SEG_LEN]
    floor, rec = s.arena[:, 67 * T:68 * T], s.arena[:, 68 * T:69 * T]

    softplus_rows(s, [(s.mf, lf, e, w, d, True)])
    with s.nc.Block() as block:
        @block.vector
        def _(dve):
            step = Chain(dve, s.dve_chain)
            step(dve.memset(w, 1.0))
            step(dve.tensor_tensor_scan(F, w, lf, 0.0, ALU.mult, ALU.add))
            step(dve.tensor_tensor(g, s.mi, F, ALU.subtract))
            step(dve.tensor_tensor_scan(M, w, g, 0.0, ALU.mult, ALU.max))
            step(dve.tensor_tensor(m, F, M, ALU.add))
    cols_ready = s.cols_ready
    m_ready, s_ready, exp_ready, att_ready, sums_ready, done = s.norm_sems
    diff_ready, abs_ready = s.pair_sems
    heads = 4
    with s.nc.Block() as block:
        @block.tensor
        def _(pe):
            for a in range(TT):
                mm = pe.transpose(s.ps[7][:, a * heads:(a + 1) * heads], g[:, a * P:(a + 1) * P], s.eye[0:heads, 0:heads])
            mm.then_inc(cols_ready.sem, 1)
            for h in range(heads):
                if h:
                    pe.wait_ge(exp_ready.sem, exp_ready.at(h))
                pick = s.eye[0:heads, h:h + 1].broadcast_to([heads, P])
                pe.matmul(s.ps[0][:], pick, M, start=True, stop=True)
                pe.matmul(s.ps[1][:], pick, m, start=True, stop=True).then_inc(m_ready.sem, 1)
                if h:
                    pe.wait_ge(att_ready.sem, att_ready.at(h))
                for a in range(TT):
                    mm = pe.matmul(s.ps[2 + a][:, 0:seg_width(a)], qk[:, heads + h, a * P:(a + 1) * P], qk[:, h, a * P:T], start=True, stop=True)
                mm.then_inc(s_ready.sem, 1)
                pe.wait_ge(att_ready.sem, att_ready.at(h + 1))
                if h:
                    pe.wait_ge(done.sem, done.at(h))
                for a in range(TT):
                    seg = att[:, SEG[a]:SEG[a] + seg_width(a)]
                    pe.matmul(s.ps[6][:, a * P:T], s.mv[:, a, h * P:(h + 1) * P], seg, start=a == 0, stop=a == TT - 1, skip_group_check=True)
                    mm = pe.matmul(s.ps[7][:, a * P:T], s.ones, seg, start=a == 0, stop=a == TT - 1, skip_group_check=True)
                mm.then_inc(sums_ready.sem, 1)

        @block.scalar
        def _(act):
            for h in range(heads):
                act.wait_ge(m_ready.sem, m_ready.at(h + 1))
                if h:
                    act.wait_ge(done.sem, done.at(h))
                act.activation(floor, s.ps[1][:], ACT.Exp, scale=-1.0)
                act.wait_ge(diff_ready.sem, diff_ready.at(h + 1))
                act.activation(att, att, ACT.Exp, scale=-1.0).then_inc(exp_ready.sem, 1)
                act.wait_ge(sums_ready.sem, sums_ready.at(h + 1))
                act.activation(rec, s.ps[7][:], ACT.Abs).then_inc(abs_ready.sem, 1)

        @block.vector
        def _(dve):
            step = Chain(dve, s.dve_chain)
            dve.wait_ge(cols_ready.sem, cols_ready.at(1))
            step(dve.tensor_copy(g_col.rearrange("p a h -> p (a h)"), s.ps[7][:, 0:TT * heads]))
            for h in range(heads):
                dve.wait_ge(m_ready.sem, m_ready.at(h + 1))
                if h:
                    dve.wait_ge(sums_ready.sem, sums_ready.at(h))
                for a in range(TT):
                    ins = dve.tensor_scalar(att[:, SEG[a]:SEG[a] + seg_width(a)], s.ps[0][:, a * P:T], g_col[:, a, h:h + 1], 0.0, ALU.subtract, ALU.max)
                ins.then_inc(diff_ready.sem, 1)
                dve.wait_ge(exp_ready.sem, exp_ready.at(h + 1))
                dve.wait_ge(s_ready.sem, s_ready.at(h + 1))
                for a in range(TT):
                    seg = att[:, SEG[a]:SEG[a] + seg_width(a)]
                    ins = dve.scalar_tensor_tensor(seg, s.ps[2 + a][:, 0:seg_width(a)], P ** -0.5, seg, ALU.mult, ALU.mult)
                step(ins)
                for a in range(TT):
                    seg = att[:, SEG[a]:SEG[a] + P]
                    ins = dve.tensor_tensor(seg, seg, s.causal, ALU.mult)
                ins.then_inc(att_ready.sem, 1)
                dve.wait_ge(abs_ready.sem, abs_ready.at(h + 1))
                step(dve.tensor_tensor(rec, rec, floor, ALU.max))
                step(dve.reciprocal(rec, rec))
                dve.tensor_tensor(s.yb[:, h, :], s.ps[6][:], rec, ALU.mult).then_inc(done.sem, 1)
    cols_ready.passed(1)
    for c in s.norm_sems + s.pair_sems:
        c.passed(heads)
    norm(s, s.yb, 4, 1, s.yb, v(56, 4), True, 1, s.col("ml_norm"), None, s.mo)


def compress(s):
    v = s.view
    blocks = [s.arena[:, (48 + 2 * k) * T:(48 + 2 * k) * T + CMP_BLOCK * N_CMP].rearrange("p (i n) -> p i n", i=CMP_BLOCK) for k in range(2)]
    phi1 = [s.arena[:, (52 + 4 * k) * T:(56 + 4 * k) * T].rearrange("p (i e) -> p i e", i=CMP_BLOCK) for k in range(2)]
    phi_k2, phi_v2 = s.arena[0:64, 60 * T:60 * T + 128], s.arena[0:64, 60 * T + 128:60 * T + 192]
    hidden = s.arena[0:64, 61 * T:61 * T + 4 * N_CMP].rearrange("p (c n) -> p c n", c=4)
    s.k_cmp = s.arena[:, 62 * T:62 * T + 2 * N_CMP].rearrange("p (g n) -> p g n", g=2)
    s.v_cmp = s.arena[0:N_CMP, 63 * T:63 * T + 128].rearrange("p (g e) -> p g e", g=2)
    blocks_ready, summed, hidden_ready, second_ready, _, _ = s.norm_sems
    with s.nc.Block() as block:
        @block.sync
        def _(sync):
            for dst, src in ((phi1[0].rearrange("p i e -> p (i e)"), "phi_k1"), (phi1[1].rearrange("p i e -> p (i e)"), "phi_v1"),
                             (phi_k2, "phi_k2"), (phi_v2, "phi_v2")):
                sync.dma_start(dst, s.I[src]).then_inc(s.loaded.sem, 16)

        @block.vector
        def _(dve):
            for k, pe_name in enumerate(("pe_k", "pe_v")):
                tokens = s.kvc[:, k, :].rearrange("p (m l) -> p l m", l=CMP_STRIDE)
                for hi in range(2):
                    part_ = slice(hi * CMP_STRIDE, (hi + 1) * CMP_STRIDE)
                    ins = dve.tensor_tensor(blocks[k][:, part_, :], tokens[:, :, hi:hi + N_CMP],
                                            s.col(pe_name)[:, part_].unsqueeze(2).broadcast_to([P, CMP_STRIDE, N_CMP]), ALU.add)
            ins.then_inc(blocks_ready.sem, 1)
            dve.wait_ge(second_ready.sem, second_ready.at(1))
            for g in range(2):
                dve.tensor_copy(s.k_cmp[:, g, :], s.ps[4 + g][:, 0:N_CMP])
                dve.tensor_copy(s.v_cmp[:, g, :], s.ps[6 + g][0:N_CMP, 0:64])

        @block.tensor
        def _(pe):
            pe.wait_ge(s.loaded.sem, s.loaded.at(64))
            pe.wait_ge(blocks_ready.sem, blocks_ready.at(1))
            for k in range(2):
                for g in range(2):
                    lo = g * 64
                    for i in range(CMP_BLOCK):
                        mm = pe.matmul(s.ps[2 * k + g][0:64, 0:N_CMP], phi1[k][lo:lo + 64, i, :], blocks[k][lo:lo + 64, i, :],
                                       start=i == 0, stop=i == CMP_BLOCK - 1)
            mm.then_inc(summed.sem, 1)
            pe.wait_ge(hidden_ready.sem, hidden_ready.at(1))
            for g in range(2):
                pe.matmul(s.ps[4 + g][:, 0:N_CMP], phi_k2, hidden[:, g, :], start=True, stop=True)
                mm = pe.matmul(s.ps[6 + g][0:N_CMP, 0:64], hidden[:, 2 + g, :], phi_v2, start=True, stop=True)
            mm.then_inc(second_ready.sem, 1)

        @block.scalar
        def _(act):
            act.wait_ge(summed.sem, summed.at(1))
            for c in range(4):
                ins = act.activation(hidden[:, c, :], s.ps[c][0:64, 0:N_CMP], ACT.Gelu_apprx_tanh)
            ins.then_inc(hidden_ready.sem, 1)
    s.loaded.passed(64)
    for c in (blocks_ready, summed, hidden_ready, second_ready):
        c.passed(1)


def sparse_attention(s):
    v = s.view
    compress(s)
    o = v(16, 12)
    s.prob = [s.arena[:, (64 + k) * T:(65 + k) * T] for k in range(PROBS)]
    s.pt = [v(48 + 4 * k, 4) for k in range(2)]
    alibi = s.arena[:, 56 * T:57 * T]
    dist, ok = (s.arena[:, (57 + k) * T:(57 + k) * T + TT * N_CMP].rearrange("p (a n) -> p a n", a=TT) for k in range(2))
    sel = s.arena[0:24, 59 * T:62 * T].rearrange("p (c q) -> p c q", q=P)
    with s.nc.Block() as block:
        @block.sync
        def _(sync):
            for dst, src in ((alibi, "alibi"), (dist.rearrange("p a n -> p (a n)"), "cmp_dist"), (ok.rearrange("p a n -> p (a n)"), "cmp_ok"),
                             (sel.rearrange("p c q -> p (c q)"), "gate_sel")):
                sync.dma_start(dst, s.I[src]).then_inc(s.loaded.sem, 16)
            sync.wait_ge(s.loaded.sem, s.loaded.at(64))
    s.loaded.passed(64)

    def unit(h, branch):
        lo, g = (h % 2) * 64, h // 4
        common = dict(q=lambda a: [s.nq[lo:lo + 64, h // 2, a * P:(a + 1) * P]], slope=2.0 ** -(h + 1.0), scale=1.0, pieces=1, channels=64,
                      row=lo, out=lambda m: o[lo:lo + 64, branch * 4 + h // 2, :])
        if branch == 0:
            return attention_unit(k=[s.k_cmp[lo:lo + 64, g, :]], keys=lambda a: N_CMP, table=lambda a: dist[:, a, :], ok=lambda a: ok[:, a, :],
                                   v=lambda st, m: s.v_cmp[:, g, :], causal=False, **common)
        return attention_unit(k=[s.ksw[lo:lo + 64, 2 * (branch - 1) + g, :]], keys=lambda a: (a + 1) * P,
                               table=lambda a: alibi[:, (TT - 1 - a) * P:T], ok=None,
                               v=lambda st, m: s.vsw[:, st, (branch - 1) * P + g * 64:(branch - 1) * P + g * 64 + 64], causal=True, **common)

    attention(s, [unit(h, b) for h in range(NSA_H) for b in range(3)])
    gate_ready, used = s.pair_sems
    s.yc = v(16, 4)
    with s.nc.Block() as block:
        @block.tensor
        def _(pe):
            for c in range(12):
                if c >= 4:
                    pe.wait_ge(used.sem, used.at(c - 3))
                pe.matmul(s.ps[c % 4][:], sel[:, c, :], s.ng, start=True, stop=True).then_inc(gate_ready.sem, 1)

        @block.vector
        def _(dve):
            for c in range(12):
                dve.wait_ge(gate_ready.sem, gate_ready.at(c + 1))
                dve.tensor_tensor(o[:, c, :], o[:, c, :], s.ps[c % 4][:], ALU.mult).then_inc(used.sem, 1)
            step = Chain(dve, s.dve_chain)
            dve.wait_ge(used.sem, used.at(12))
            step(dve.tensor_tensor(s.yc, s.yc, o[:, 4:8, :], ALU.add))
            step(dve.tensor_tensor(s.yc, s.yc, o[:, 8:12, :], ALU.add))
    gate_ready.passed(12)
    used.passed(12)


def gated_residual(s, gate):
    def evac(dve, step, t, ps):
        return dve.scalar_tensor_tensor(s.x[:, t, :], ps, gate[:, bass.ds(t, 1)], s.x[:, t, :], ALU.mult, ALU.add)
    return evac


def third_mixer(s):
    v = s.view
    third_projection(s)
    spatial_gating(s)
    mlstm(s)
    sparse_attention(s)
    ga, gb, gc, merged = v(28, 8), v(36, 8), v(44, 8), v(52, 8)
    h = Split(lambda k: s.h[:, k, :], DT, s.rounded(60), s.rounded(0))
    linears(s, [part("w3_" + name, h, store(lambda t, dst=dst: dst[:, t, :], ACT.Sigmoid)) for name, dst in (("ga", ga), ("gb", gb), ("gc", gc))])

    def add(gate):
        def evac(dve, step, t, ps):
            step(dve.tensor_tensor(gate[:, t, :], ps, gate[:, t, :], ALU.mult))
            return dve.tensor_tensor(merged[:, t, :], merged[:, t, :], gate[:, t, :], ALU.add)
        return evac

    linears(s, [
        part("w3_up_a", Split(lambda k: s.gu[:, k, :], 4, s.rounded(60), s.rounded(8)), lambda dve, step, t, ps: dve.tensor_tensor(merged[:, t, :], ps, ga[:, t, :], ALU.mult), by="dve"),
        part("w3_up_b", Split(lambda k: s.yb[:, k, :], 4, s.rounded(64), s.rounded(12)), add(gb), by="dve", steps=1),
        part("w3_up_c", Split(lambda k: s.yc[:, k, :], 4, s.rounded(68), s.rounded(16)), add(gc), by="dve", steps=1),
    ])
    linears(s, [part("w3_out", Split(lambda k: merged[:, k, :], DT, s.rounded(0), s.rounded(52)), gated_residual(s, s.gate1), by="dve")])


def squared_relu_mlp(s):
    v = s.view
    half = FF3_TILES // 2
    h, wide = v(0, 8), v(16, half)
    norm(s, s.x, 8, 8, h, v(8, 10), False, 1, s.gain2, s.shift2)
    h_split = Split(lambda k: h[:, k, :], DT, s.rounded(8), s.rounded(0))

    def evac(dve, step, t, ps):
        step(dve.tensor_scalar(wide[:, t, :], ps, 0.0, None, ALU.max))
        return dve.tensor_tensor(wide[:, t, :], wide[:, t, :], wide[:, t, :], ALU.mult)

    for name in "ab":
        linears(s, [part("w3_mlp1" + name, h_split, evac, by="dve", steps=1)])
        wide_split = Split(lambda k: wide[:, k, :], half, s.rounded(32), s.rounded(16))
        linears(s, [part("w3_mlp2" + name, wide_split, gated_residual(s, s.gate2), by="dve")])
    norm(s, s.x, 8, 8, s.x, v(0, 10), False, 1, s.col("g_final"))
STAGES = [first_mixer, cross_attention, conv_glu, second_mixer, peer, third_mixer, squared_relu_mlp]


def kernel(**inputs):
    from concourse import bacc
    from concourse.bass_utils import run_bass_kernel_spmd

    nc = bacc.Bacc("TRN2", target_bir_lowering=False, num_devices=1)
    arrays, at = lay_out({k: np.asarray(v) for k, v in inputs.items()})
    aps = {k: nc.dram_tensor("in_" + k, v.shape, F32, kind="ExternalInput").ap() for k, v in arrays.items()}
    out = nc.dram_tensor("out", (P, DT * T), F32, kind="ExternalOutput").ap()
    build(nc, aps, at, out)
    r = run_bass_kernel_spmd(nc, [{"in_" + k: v for k, v in arrays.items()}], core_ids=[0])
    got = r.results[0]["out"]
    return got.reshape(P, DT, T).transpose(2, 1, 0).reshape(1, T, D)
```

```python
from contextlib import contextmanager

import numpy as np

import concourse.bass as bass
import concourse.mybir as mybir

F32 = mybir.dt.float32
F32R = mybir.dt.float32r
U32 = mybir.dt.uint32
ACT = mybir.ActivationFunctionType
ALU = mybir.AluOpType
AX = mybir.AxisListType

P = 128
T = 512
TT = T // P
D = 1024
DT = D // P
MEM = 256
SLAB = 2816
HEADS = 8
BANKS = 4

SSD_HEADS, SSD_HD, SSD_CONV = 16, 64, 4
RET_HEADS, RET_QK, RET_DV = 8, 64, 128
D_FF, FF_TILES = 2752, 22
ALPHA = 2.0 ** 0.25
XH, XHD = 4, 256
RT = 10
PEER_H, PEER_K = 8, 16
NKEYS = 128
SLOTS = PEER_H * PEER_K
GATHER = 8
NSA_H, NSA_DH, N_CMP, CMP_BLOCK, CMP_STRIDE = 8, 64, 31, 32, 16
FF3_TILES = 32
NEG = -1e30

SEG = [0, 512, 896, 1152]
SEG_LEN = 1280


def seg_width(s):
    return T - s * P


def cols(v, tiles):
    v = np.asarray(v).reshape(-1)
    out = np.zeros((tiles * P,), np.float32)
    out[: v.size] = v
    return out.reshape(tiles, P).T


def rows(v):
    out = np.zeros((P, 1), np.float32)
    out[: np.size(v), 0] = np.asarray(v).reshape(-1)
    return out


def slabs(w, width):
    k, n = w.shape
    kt, ns = -(-k // P), -(-n // width)
    if (kt * P, ns * width) != (k, n):
        w = np.pad(w, ((0, kt * P - k), (0, ns * width - n)))
    return np.ascontiguousarray(w.reshape(kt, P, ns, width).transpose(2, 1, 0, 3).reshape(ns, P, kt * width))


def channel_major(x):
    t, c = x.shape
    return np.ascontiguousarray(x.T.reshape(c // P, P, t).transpose(1, 0, 2).reshape(P, -1))


def lay_out(i):
    a, par, at = {}, [], {}

    def param(name, v):
        at[name] = (sum(p.shape[1] for p in par), v.shape[1])
        par.append(np.asarray(v, np.float32))

    w = i["w_in"][0]
    o = np.cumsum([0, 1024, 1536, 16, 512, 512, 1024, 1024])
    a["x"] = channel_major(i["x"][0])
    a["mem"] = channel_major(i["mem"][0])
    a["w_z"] = slabs(w[:, o[0]:o[1]], 256)
    a["w_xbc"] = slabs(w[:, o[1]:o[2]], 256)
    a["w_dt"] = slabs(w[:, o[2]:o[3]], 16)
    a["w_qk"] = slabs(w[:, o[3]:o[5]], 256)
    a["w_v"] = slabs(w[:, o[5]:o[6]], 256)
    a["w_g"] = slabs(w[:, o[6]:o[7]], 256)
    a["w_mix"] = slabs(i["w_mix_out"][0], 128)
    a["w_xk"], a["w_xv"] = slabs(i["w_xk"][0], 256), slabs(i["w_xv"][0], 256)
    a["w_xq"], a["w_xo"] = slabs(i["w_xq"][0], 256), slabs(i["w_xo"][0], 256)
    up, pad = i["w_ffn_up"][0], FF_TILES * P - D_FF

    def pairs(v):
        v = np.pad(v.reshape(-1, 2, D_FF), ((0, 0), (0, 0), (0, pad)))
        return v.reshape(-1, 2, FF_TILES, P).transpose(0, 2, 1, 3).reshape(v.shape[0], -1)

    a["w_up"] = slabs(pairs(up), 256)
    a["w_down"] = slabs(i["w_ffn_down"][0], 128)
    for k in range(SSD_CONV):
        param(f"ssd_conv{k}", cols(i["ssd_conv_w"][0, k], 12))
    param("ssd_conv_b", cols(i["ssd_conv_b"][0], 12))
    param("dt_bias", rows(i["ssd_dt_bias"]))
    param("a_log", rows(i["ssd_a_log"]))
    param("ssd_d", cols(np.repeat(np.asarray(i["ssd_d"][0]), SSD_HD), 8))
    param("ssd_norm", cols(i["ssd_norm_w"], 8))
    param("gn_w", cols(i["ret_gn_w"], 8))
    param("gn_b", cols(i["ret_gn_b"], 8))
    for n in (1, 2, 3):
        param(f"ln{n}_g", cols(i[f"ln{n}_g"], 8))
        param(f"ln{n}_b", cols(i[f"ln{n}_b"], 8))
    param("b_up", cols(pairs(np.asarray(i["b_ffn_up"])), 2 * FF_TILES))
    for k in range(3):
        param(f"ffn_conv{k}", cols(pairs(np.asarray(i["ffn_conv_w"][0, k:k + 1])), 2 * FF_TILES))
    param("ffn_conv_b", cols(pairs(np.asarray(i["ffn_conv_b"])), 2 * FF_TILES))

    w = i["w_in_2"][0]
    o = np.cumsum([0, 1024, 1024, 1024, 1280, 1280, 1024, 1024])
    for n, name in enumerate(("ax", "ab", "ac", "rx", "ry", "ga", "gb")):
        a["w2_" + name] = slabs(w[:, o[n]:o[n + 1]], 256)
    a["w2_out_a"], a["w2_o"] = slabs(i["w_out_a_2"][0], 256), slabs(i["w_o_2"][0], 256)
    a["w2_out_b"] = slabs(i["w_out_b_2"][0], 256)
    a["w2_q"] = slabs(i["w_q_2"][0], 256)
    a["w2_rg"] = np.ascontiguousarray(np.asarray(i["w_rg_2"][0]).transpose(1, 0, 2).reshape(1, P, -1))
    a["w2_ig"] = np.ascontiguousarray(np.asarray(i["w_ig_2"][0]).transpose(1, 0, 2).reshape(1, P, -1))
    k1, k2 = np.asarray(i["sub_keys_1_2"][0]), np.asarray(i["sub_keys_2_2"][0])
    a["keys"] = np.ascontiguousarray(np.stack([k1, k2], 1).transpose(3, 0, 1, 2).reshape(P, -1))
    a["expert_u"], a["expert_v"] = i["expert_u_2"][0], i["expert_v_2"][0]
    param("norm_mix", cols(i["norm_mix_2"], 8))
    for k in range(3):
        param(f"conv_a{k}", cols(i["conv_a_w_2"][0, k], 8))
    for k in range(4):
        param(f"rnn_conv{k}", cols(i["rnn_conv_w_2"][0, k], RT))
    for name in ("rnn_conv_b", "b_rg", "b_ig", "lru_lambda"):
        param(name, cols(i[name + "_2"], RT))
    param("norm_ffn", cols(i["norm_ffn_2"], 8))
    param("norm_final", cols(i["norm_final_2"], 8))

    w = np.asarray(i["w_in_3"][0])
    o = np.cumsum([0, 512, 512, 512, 512, 512, 512, 4, 4, 512] + [128] * 6 + [24, 1024, 1024, 1024])
    a["w3_ada"] = slabs(i["w_ada_3"][0], 256)
    a["c"] = channel_major(np.asarray(i["c_3"]))
    a["w3_gu"], a["w3_gv"] = slabs(w[:, o[0]:o[1]], 256), slabs(w[:, o[1]:o[2]], 256)
    a["w3_mqk"] = slabs(w[:, o[2]:o[4]], 256)
    a["w3_mv"], a["w3_mo"] = slabs(w[:, o[4]:o[5]], 256), slabs(w[:, o[5]:o[6]], 256)
    a["w3_mi"], a["w3_mf"] = slabs(w[:, o[6]:o[7]], 4), slabs(w[:, o[7]:o[8]], 4)
    a["w3_nq"] = slabs(w[:, o[8]:o[9]], 256)
    kc, vc, ks, vs, kw, vw = (w[:, o[9 + n]:o[10 + n]] for n in range(6))
    a["w3_kvc"] = slabs(np.concatenate([kc, vc], 1), 256)
    a["w3_ksw"] = slabs(np.concatenate([k[:, g * 64:g * 64 + 64] for k in (ks, kw) for g in (0, 0, 1, 1)], 1), 256)
    a["w3_vsw"] = slabs(np.concatenate([vs, vw], 1), 256)
    a["w3_ng"] = slabs(w[:, o[15]:o[16]], 24)
    for n, name in enumerate(("ga", "gb", "gc")):
        a["w3_" + name] = slabs(w[:, o[16 + n]:o[17 + n]], 256)
        a["w3_up_" + name[1]] = slabs(i[f"w_up_{name[1]}_3"][0], 512)
    a["w3_out"] = slabs(i["w_out_3"][0], 256)
    half = FF3_TILES // 2 * P
    for n, name in enumerate("ab"):
        a["w3_mlp1" + name] = slabs(i["w_mlp1_3"][0][:, n * half:(n + 1) * half], 256)
        a["w3_mlp2" + name] = slabs(i["w_mlp2_3"][0][n * half:(n + 1) * half], 128)
    param("b_ada", cols(i["b_ada_3"], 48))
    for name in ("g_norm1", "g_norm2", "g_final"):
        param(name, cols(i[name + "_3"], 8))
    param("gm_ln_g", cols(i["gm_ln_g_3"], 4))
    param("gm_ln_b", cols(i["gm_ln_b_3"], 4))
    a["gm_w"] = np.ascontiguousarray(np.asarray(i["gm_ws_3"][0]).transpose(2, 0, 1).reshape(P, -1))
    a["gm_b"] = np.ascontiguousarray(np.broadcast_to(np.asarray(i["gm_bs_3"][0]).reshape(1, -1), (P, 512)))
    for k in range(4):
        param(f"ml_conv{k}", cols(i["ml_conv_w_3"][0, k], 8))
    param("ml_conv_b", cols(i["ml_conv_b_3"], 8))
    param("ml_bi", rows(np.asarray(i["ml_gate_b_3"])[0, :4]))
    param("ml_bf", rows(np.asarray(i["ml_gate_b_3"])[0, 4:]))
    param("ml_norm", cols(i["ml_norm_g_3"], 4))
    for n in "kv":
        pe = np.asarray(i[f"nsa_pe_{n}_3"][0]).T
        param(f"pe_{n}", np.concatenate([pe, pe], 0))
        phi = np.asarray(i[f"nsa_phi_{n}1_3"][0]).reshape(CMP_BLOCK, 64, 64).transpose(1, 0, 2).reshape(64, -1)
        a[f"phi_{n}1"] = np.ascontiguousarray(np.concatenate([phi, phi], 0))
        a[f"phi_{n}2"] = np.ascontiguousarray(i[f"nsa_phi_{n}2_3"][0])
    a["phi_k2"] = np.concatenate([a["phi_k2"], a["phi_k2"]], 1)
    a["params"] = np.ascontiguousarray(np.concatenate(par, 1))
    a.update(constants())
    return {k: np.ascontiguousarray(v) for k, v in a.items()}, at


def constants():
    c = {}
    p, j = np.arange(P)[:, None], np.arange(T)[None, :]
    eye = np.eye(P)
    turn = np.zeros((P, P))
    for m in range(P):
        d = m % RET_QK
        if d < 32:
            turn[m + 32, m] = -1.0
        else:
            turn[m - 32, m] = 1.0
    causal = (p <= np.arange(P)[None, :]).astype(float)
    eps = np.tile(np.array([[1e-5, 1e-6]]), (P, 1))
    pick = np.zeros((P, 2 * HEADS - 1))
    pick[:, HEADS - 1] = 1.0
    c["base"] = np.concatenate([eye, turn, causal, np.ones((P, P)), eps, pick], 1)
    freqs = (1.0 / (np.float32(10000.0) ** np.linspace(0.0, 1.0, 32, dtype=np.float32))).astype(np.float32)
    ang = (np.arange(T, dtype=np.float32)[None, :] * freqs[:, None]).astype(np.float32)
    ang = np.tile(ang.astype(np.float64), (4, 1))
    c["rope"] = np.concatenate([np.cos(ang), np.sin(ang)], 1)
    gamma = np.log1p(-np.exp2(-5.0 - np.arange(RET_HEADS)))
    dist = j - p
    c["decay"] = np.concatenate(
        [np.where(dist >= 0, np.exp(np.maximum(dist, 0) * g), 0.0) * RET_QK ** -0.5 for g in gamma], 1)
    alibi = j - p - 384.0
    c["alibi"] = np.where(alibi > 0, NEG, alibi)
    t = np.arange(T)
    n = np.arange(N_CMP)
    ok = (n * CMP_STRIDE + CMP_BLOCK - 1)[None, :] <= t[:, None]
    center = n * CMP_STRIDE + (CMP_BLOCK - 1) * 0.5
    cd = np.where(ok, center[None, :] - t[:, None], NEG)
    for name, v in (("cmp_dist", cd), ("cmp_ok", ok.astype(float))):
        c[name] = v.reshape(TT, P, N_CMP).transpose(1, 0, 2).reshape(P, -1)
    sel = np.zeros((24, 12, P))
    for b in range(3):
        for tile in range(4):
            for q in range(P):
                sel[(2 * tile + q // 64) * 3 + b, b * 4 + tile, q] = 1.0
    c["gate_sel"] = sel.reshape(24, -1)
    c["iota"] = np.tile(np.arange(float(PEER_K))[None, :], (P, 1))
    return {k: np.ascontiguousarray(v, dtype=np.float32) for k, v in c.items()}


class Names:
    pass


class Counter:

    def __init__(self, nc, name):
        self.sem, self.base = nc.alloc_semaphore(name), 0

    def at(self, n):
        return self.base + n

    def passed(self, n):
        self.base += n


class Chain:

    def __init__(self, eng, counter):
        self.eng, self.counter, self.turn = eng, counter, 0

    def __call__(self, ins):
        self.counter.base += 1
        ins.then_inc(self.counter.sem, 1)
        self.eng.wait_ge(self.counter.sem, self.counter.base + self.turn)

    @contextmanager
    def loop(self, count, steps):
        start, outer = self.counter.base, self.turn
        with self.eng.Fori(0, count) as i:
            self.turn = outer + i * steps
            yield i
        assert self.counter.base == start + steps, (self.counter.base - start, steps)
        self.turn = outer
        self.counter.base = start + steps * count


PLAN = [
    ("w_z", 8, 256), ("w_xbc", 8, 256), ("w_dt", 8, 16), ("w_qk", 8, 256), ("w_g", 8, 256), ("w_v", 8, 256),
    ("w_mix", 16, 128), ("w_xk", 8, 256), ("w_xv", 8, 256), ("w_xq", 8, 256), ("w_xo", 8, 256),
    ("w_up", 8, 256), ("w_down", 22, 128),
    ("w2_ax", 8, 256), ("w2_ac", 8, 256), ("w2_ab", 8, 256), ("w2_rx", 8, 256), ("w2_ry", 8, 256),
    ("w2_rg", 1, 1280), ("w2_ig", 1, 1280), ("w2_ga", 8, 256), ("w2_gb", 8, 256), ("w2_out_a", 8, 256),
    ("w2_out_b", 10, 256), ("w2_o", 8, 256), ("w2_q", 8, 256),
    ("w3_gu", 8, 256), ("w3_gv", 8, 256), ("w3_mqk", 8, 256), ("w3_mv", 8, 256),
    ("w3_mo", 8, 256), ("w3_mi", 8, 4), ("w3_mf", 8, 4), ("w3_nq", 8, 256), ("w3_kvc", 8, 256),
    ("w3_ksw", 8, 256), ("w3_vsw", 8, 256), ("w3_ng", 8, 24),
    ("w3_ga", 8, 256), ("w3_gb", 8, 256), ("w3_gc", 8, 256),
    ("w3_up_a", 4, 512), ("w3_up_b", 4, 512), ("w3_up_c", 4, 512), ("w3_out", 8, 256),
    ("w3_mlp1a", 8, 256), ("w3_mlp2a", 16, 128), ("w3_mlp1b", 8, 256), ("w3_mlp2b", 16, 128),
]
RING = 2
UNITS = 2
UNIT_K = 8


class Split:

    def __init__(self, src, tiles, hi, lo):
        self.src, self.tiles, self.hi, self.lo, self.made = src, tiles, hi, lo, False


def part(name, act, evac, tile=P, n=T, tokens=0, by="act", steps=0, block_diag=False, side=None, side_steps=0, side_after=None, written_out=False, pe_before=None):
    p = Names()
    p.written_out, p.pe_before = written_out, pe_before
    p.side, p.side_steps, p.side_after = side, side_steps, side_after
    p.name, p.act, p.evac, p.tile, p.n, p.tokens, p.by, p.steps, p.block_diag = name, act, evac, tile, n, tokens, by, steps, block_diag
    p.split = act if isinstance(act, Split) else None
    return p


def linears(s, parts, act_start=None, act_end=None, dve_end=None, sync_last=None):
    nc = s.nc
    ahead, s.ahead = s.ahead, 0
    assert not ahead or parts[0].split
    fresh = []
    for p in parts:
        p.index = [w[0] for w in PLAN].index(p.name)
        assert p.index == s.next_part, p.name
        s.next_part += 1
        _, p.kt, p.width = PLAN[p.index]
        p.first = s.first_slab[p.index]
        p.slabs = s.first_slab[p.index + 1] - p.first
        p.per_slab = p.tokens or p.width // p.tile
        deep = UNIT_K * P // p.width if p.tokens else UNIT_K
        p.chunks = [(k, min(k + deep, p.kt)) for k in range(0, p.kt, deep)] if p.split else [(0, p.kt)]
        p.upt = len(p.chunks)
        p.shared = bool(p.split and p.tokens)
        p.slab_units = p.upt if p.shared else p.per_slab * p.upt
        p.tile0, p.unit0, p.split0 = s.tiles, s.units, s.split_units
        s.tiles += p.slabs * p.per_slab
        s.units += p.slabs * p.slab_units
        p.body = 4 if p.per_slab == 1 else 2
        p.bodies = p.slabs // p.body if p.slabs >= 2 * p.body and not p.tokens and not p.written_out and p.tile0 else 0
        p.tiles = p.body * p.per_slab
        for k in range(p.slabs):
            done = (k + 1) * p.slab_units
            s.slab_end.append((s.lo_made, p.split0 + done) if p.split else (s.units_done, p.unit0 + done))
        if p.split:
            s.split_units += p.slabs * p.slab_units
            if not p.split.made:
                p.split.made = True
                fresh.append((p, p.split, sum(f[1].tiles for f in fresh)))
        p.peel = 1 if p is parts[0] and p.bodies else 0

    def bodies(eng, p, slab):
        for i in range(p.peel):
            for j in range(p.body):
                slab(i, j)
        if p.bodies > p.peel:
            with eng.Fori(p.peel, p.bodies) as i:
                for j in range(p.body):
                    slab(i, j)
        for j in range(p.bodies * p.body, p.slabs):
            slab(0, j)

    def load(sync, ring_free, index, k, slot):
        if ring_free is not None:
            sync.wait_ge(ring_free[0].sem, ring_free[1])
        _, kt, width = PLAN[index]
        sync.dma_start(s.ring[:, slot, 0:kt * width], s.I[PLAN[index][0]][k]).then_inc(s.slab_ready[slot], 16)

    def load_static(sync, slab):
        if slab < s.first_slab[-1]:
            index = max(j for j in range(len(PLAN)) if s.first_slab[j] <= slab)
            load(sync, s.slab_end[slab - RING] if slab >= RING else None, index, slab - s.first_slab[index], slab % RING)

    def raw_and_split(p, i, j, u, c):
        unit = j * p.slab_units + u * p.upt + c
        k0, k1 = p.chunks[c]
        n0, n = (0, p.width) if p.shared else (u * P, P)
        raw = s.ring[:, (p.first + j) % RING, 0:p.kt * p.width].rearrange("p (k n) -> p k n", k=p.kt)[:, k0:k1, n0:n0 + n]
        hi, lo = (x[(p.split0 + unit) % UNITS][:, 0:(k1 - k0) * n].rearrange("p (k n) -> p k n", n=n) for x in (s.w_hi, s.w_lo))
        return unit, i * (p.tiles * p.upt), raw, hi, lo

    def wait_for_slab(eng, p, i, j):
        slab = p.first + j
        eng.wait_ge(s.slab_ready[slab % RING], (slab // RING + 1) * 16 + i * (p.body // RING) * 16)

    def high_parts(eng, p, i, j, u, c):
        unit, before, raw, hi, lo = raw_and_split(p, i, j, u, c)
        if p is parts[0] and isinstance(i, int) and i == 0 and unit < ahead:
            return
        if u == 0 and c == 0:
            wait_for_slab(eng, p, i, j)
        if not isinstance(i, int) or p.unit0 + unit + before >= UNITS:
            eng.wait_ge(s.units_done.sem, p.unit0 + unit + 1 - UNITS + before)
        ins = eng.activation(hi, raw, ACT.Copy) if p.by == "dve" else eng.tensor_copy(hi, raw)
        ins.then_inc(s.hi_made.sem, 1)

    def low_parts(eng, p, i, j, u, c):
        unit, before, raw, hi, lo = raw_and_split(p, i, j, u, c)
        if p is parts[0] and isinstance(i, int) and i == 0 and unit < ahead:
            return
        eng.wait_ge(s.hi_made.sem, p.split0 + unit + 1 + before)
        eng.tensor_tensor(lo, raw, hi.bitcast(F32), ALU.subtract).then_inc(s.lo_made.sem, 1)

    def split_units(eng, p, steps, others, chain=None):
        for q in parts:
            if p.side and q.name == p.side_after:
                eng.wait_ge(s.evac_done.sem, q.tile0 + q.slabs * q.per_slab)

        def slab(i, j):
            for u in range(1 if p.shared else p.per_slab):
                for c in range(p.upt):
                    for step in steps:
                        step(eng, p, i, j, u, c)
                    unit = j * p.slab_units + u * p.upt + c
                    if isinstance(i, int) and i == 0 and unit < 4:
                        others(unit)
                    if p.side and chain and (p.shared or c == p.upt - 1):
                        at = unit if p.shared else j * p.per_slab + u
                        p.side(eng, chain, p, i * p.tiles + at, at)

        if p.side and chain and p.bodies and p.by == "act":
            with chain.loop(p.bodies, p.side_steps) as i:
                for j in range(p.body):
                    slab(i, j)
            for j in range(p.bodies * p.body, p.slabs):
                slab(0, j)
        else:
            bodies(eng, p, slab)

    groups = [(split, at, range(k, min(k + UNIT_K, split.tiles))) for _, split, at in fresh for k in range(0, split.tiles, UNIT_K)]

    def activations(split_tiles):
        return lambda unit: [split_tiles(*g) for g in groups[unit:unit + 1 if unit < 3 else None]]

    def high_tiles(act):
        def tiles(split, at, ks):
            for k in ks:
                act.activation(split.hi(k), split.src(k), ACT.Copy).then_inc(s.act_hi.sem, 1)
        return tiles

    def low_tiles(dve):
        def tiles(split, at, ks):
            for k in ks:
                dve.wait_ge(s.act_hi.sem, s.act_hi.at(at + k + 1))
                dve.tensor_tensor(split.lo(k), split.src(k), split.hi(k).bitcast(F32), ALU.subtract).then_inc(s.act_lo.sem, 1)
        return tiles

    with nc.Block() as block:
        @block.sync
        def _(sync):
            for p in parts:
                if p.first == 0:
                    for slab in range(RING):
                        load_static(sync, slab)
                inside = max(p.slabs - RING, 0)
                pairs = inside // RING if inside >= 2 * RING else 0
                if pairs:
                    end = s.slab_end[p.first]
                    step = p.slab_units
                    with sync.Fori(0, pairs) as i:
                        for j in range(RING):
                            load(sync, (end[0], end[1] + (i * RING + j) * step), p.index, i * RING + j + RING, (p.first + j) % RING)
                if sync_last and p is parts[-1]:
                    sync_last(sync)
                for k in range(pairs * RING, p.slabs):
                    load_static(sync, p.first + k + RING)

        @block.tensor
        def _(pe):
            def token_products(p, j):
                tiles = [j * p.tokens + u for u in range(p.tokens)]
                bank = lambda t: s.ps[(p.tile0 + t) % BANKS]
                for t in tiles:
                    pe.wait_ge(s.evac_done.sem, p.tile0 + t - BANKS + 1)
                for c, (k0, k1) in enumerate(p.chunks):
                    unit, _, _, hi, lo = raw_and_split(p, 0, j, 0, c)
                    pe.wait_ge(s.lo_made.sem, p.split0 + unit + 1)
                    for u, t in enumerate(tiles):
                        out, x = bank(t)[:, 0:p.width], p.split
                        for k in range(k0, k1):
                            first, last = k == 0, k == p.kt - 1
                            x_hi, x_lo = (y(k)[:, u * P:(u + 1) * P] for y in (x.hi, x.lo))
                            pe.matmul(out, x_hi, hi[:, k - k0, :], start=first, stop=False)
                            pe.matmul(out, x_hi, lo[:, k - k0, :], start=False, stop=False)
                            mm = pe.matmul(out, x_lo, hi[:, k - k0, :], start=False, stop=last)
                    mm.then_inc(s.units_done.sem, 1)

            def products(p, i, j):
                if p.pe_before:
                    p.pe_before(pe, j)
                if not p.split:
                    wait_for_slab(pe, p, i, j)
                if p.shared:
                    token_products(p, j)
                    return
                w = s.ring[:, (p.first + j) % RING, 0:p.kt * p.width].rearrange("p (k n) -> p k n", k=p.kt)
                for u in range(p.per_slab):
                    t = j * p.per_slab + u
                    bank = s.ps[(p.tile0 + t) % BANKS]
                    if not isinstance(i, int) or p.tile0 + i * p.tiles + t >= BANKS:
                        pe.wait_ge(s.evac_done.sem, p.tile0 + t - BANKS + 1 + i * p.tiles)
                    for c, (k0, k1) in enumerate(p.chunks):
                        unit, before, _, hi, lo = raw_and_split(p, i, j, u, c) if p.split else (None, None, None, None, None)
                        if p.split:
                            pe.wait_ge(s.lo_made.sem, p.split0 + unit + 1 + before)
                        for k in range(k0, k1):
                            first, last = k == 0, k == p.kt - 1
                            if p.split:
                                if fresh and p is parts[0] and fresh[0][0] is p and isinstance(i, int) and i == 0 and t == 0:
                                    pe.wait_ge(s.act_lo.sem, s.act_lo.at(k + 1))
                                out, x = bank[:, 0:p.n], p.split
                                pe.matmul(out, hi[:, k - k0, :], x.hi(k), start=first, stop=False)
                                pe.matmul(out, hi[:, k - k0, :], x.lo(k), start=False, stop=False)
                                mm = pe.matmul(out, lo[:, k - k0, :], x.hi(k), start=False, stop=last)
                            elif p.tokens:
                                mm = pe.matmul(bank[:, 0:p.width], p.act(k)[:, u * P:(u + 1) * P], w[:, k, :], start=first, stop=last)
                            else:
                                mm = pe.matmul(bank[0:p.tile, 0:p.n], w[:, k, u * p.tile:(u + 1) * p.tile],
                                               p.act(u if p.block_diag else k), start=first, stop=last)
                        mm.then_inc(s.units_done.sem, 1)

            for n, p in enumerate(parts):
                if n and parts[n - 1].by != p.by:
                    pe.wait_ge(s.evac_done.sem, p.tile0)
                for q, split, at in fresh:
                    if q is p and n:
                        pe.wait_ge(s.act_lo.sem, s.act_lo.at(at + split.tiles))
                bodies(pe, p, lambda i, j: products(p, i, j))

        def evacuate(eng, chain, p):
            def one(t, bank):
                eng.wait_ge(s.units_done.sem, p.unit0 + ((t // p.tokens + 1) if p.shared else t + 1) * p.upt)
                if not isinstance(t, int) and p.by == "act":
                    eng.sem_inc(s.held, 1)
                ps = s.ps[bank]
                ps = ps[0:p.tile, 0:p.width if p.tokens else p.n]
                p.evac(eng, chain, t, ps).then_inc(s.evac_done.sem, 1)

            if p.bodies:
                with chain.loop(p.bodies, int(p.steps * p.tiles)) as i:
                    for u in range(p.tiles):
                        one(i * p.tiles + u, (p.tile0 + u) % BANKS)
            for t in range(p.bodies * p.tiles, p.slabs * p.per_slab):
                one(t, (p.tile0 + t) % BANKS)

        @block.scalar
        def _(act):
            chain = Chain(act, s.act_chain)
            if act_start:
                act_start(act)
            others = activations(high_tiles(act))
            for p in parts:
                mine = others if p is parts[0] else lambda unit: None
                if p.by == "dve" and p.split:
                    split_units(act, p, [high_parts], mine, chain)
                else:
                    for unit in range(4):
                        mine(unit)
                if p.by == "act":
                    evacuate(act, chain, p)
            if act_end:
                act_end(act)

        @block.vector
        def _(dve):
            chain = Chain(dve, s.dve_chain)
            others = activations(low_tiles(dve))
            for p in parts:
                mine = others if p is parts[0] else lambda unit: None
                if p.by == "act" and p.split:
                    split_units(dve, p, [high_parts, low_parts], mine, chain)
                else:
                    if p is parts[0] and p.split:
                        low_parts(dve, p, 0, 0, 0, 0)
                    for unit in range(4):
                        mine(unit)
                if p.by == "dve":
                    evacuate(dve, chain, p)
            if dve_end:
                dve_end(dve)

        @block.gpsimd
        def _(pool):
            def low_but_first(eng, p, i, j, u, c):
                if p is parts[0] and isinstance(i, int) and i == j == u == c == 0:
                    eng.wait_ge(s.lo_made.sem, p.split0 + 1)
                else:
                    low_parts(eng, p, i, j, u, c)

            for p in parts:
                if p.by == "dve" and p.split:
                    split_units(pool, p, [low_but_first], lambda unit: None)
    for p, split, at in fresh:
        s.act_hi.passed(split.tiles)
        s.act_lo.passed(split.tiles)


def split_ahead(s):
    _, kt, width = PLAN[s.next_part]
    slab, units = s.first_slab[s.next_part], s.split_units
    w = s.ring[:, slab % RING, 0:kt * width].rearrange("p (k n) -> p k n", k=kt)
    tiles = [(u, k) for u in range(width // P) for k in range(0, kt, UNIT_K)][:UNITS]
    raw = [w[:, k:k + UNIT_K, u * P:(u + 1) * P] for u, k in tiles]
    place = lambda x, n: x[(units + n) % UNITS].rearrange("p (k n) -> p k n", n=P)
    s.ahead = UNITS

    def high(act):
        act.wait_ge(s.slab_ready[slab % RING], (slab // RING + 1) * 16)
        for n in range(UNITS):
            act.activation(place(s.w_hi, n), raw[n], ACT.Copy).then_inc(s.hi_made.sem, 1)

    def low(pool):
        for n in range(UNITS):
            pool.wait_ge(s.hi_made.sem, units + n + 1)
            pool.tensor_tensor(place(s.w_lo, n), raw[n], place(s.w_hi, n).bitcast(F32), ALU.subtract).then_inc(s.lo_made.sem, 1)

    return high, low


def residual(s, scale=1.0):
    def evac(dve, step, t, ps):
        return dve.scalar_tensor_tensor(s.x[:, t, :], s.x[:, t, :], scale, ps, ALU.mult, ALU.add)
    return evac


def store(dst, func=ACT.Copy, bias=None, scale=1.0):
    def evac(act, step, t, ps):
        if bias is None:
            return act.activation(dst(t), ps, func, scale=scale)
        return act.activation(dst(t), ps, func, bias=bias(t), scale=scale)
    return evac


def store_by_token(dst, tiles, width=256):
    def evac(act, step, t, ps):
        return act.activation(dst[:, t % tiles, (t // tiles) * width:(t // tiles + 1) * width], ps, ACT.Copy)
    return evac


def norm(s, src, tiles, group, dst, scratch, center, eps, gain, bias=None, ahead=False):
    n, groups = group * P, tiles // group
    squares = group
    high, low = split_ahead(s) if ahead else (None, None)
    sq, std = scratch[:, 0:squares, :], scratch[:, squares:squares + 2, :]
    mean_ready, cen_ready, sq_ready, var_ready, std_ready, out_ready = s.norm_sems
    scaled, _ = s.pair_sems
    with s.nc.Block() as block:
        @block.tensor
        def _(pe):
            def mean(g):
                if g >= 2:
                    pe.wait_ge(cen_ready.sem, cen_ready.at((g - 1) * group))
                for u in range(group):
                    mm = pe.matmul(s.ps[4 + g % 2][:], s.ones, src[:, g * group + u, :], start=u == 0, stop=u == group - 1)
                mm.then_inc(mean_ready.sem, 1)

            if center:
                mean(0)
            for g in range(groups):
                if center and g + 1 < groups:
                    mean(g + 1)
                if g >= 2:
                    pe.wait_ge(std_ready.sem, std_ready.at(g - 1))
                for u in range(group):
                    t = g * group + u
                    pe.wait_ge(sq_ready.sem, sq_ready.at(t + 1))
                    mm = pe.matmul(s.ps[6 + g % 2][:], s.ones, sq[:, t % squares, :], start=u == 0, stop=u == group - 1)
                mm.then_inc(var_ready.sem, 1)

        @block.scalar
        def _(act):
            def root(g):
                act.wait_ge(var_ready.sem, var_ready.at(g + 1))
                if g >= 2:
                    act.wait_ge(out_ready.sem, out_ready.at(g - 1))
                act.activation(std[:, g % 2, :], s.ps[6 + g % 2][:], ACT.Sqrt, bias=s.eps[eps], scale=1.0 / n).then_inc(std_ready.sem, 1)

            for g in range(groups):
                for t in range(g * group, (g + 1) * group):
                    if center:
                        act.wait_ge(cen_ready.sem, cen_ready.at(t + 1))
                    if t >= squares:
                        act.wait_ge(var_ready.sem, var_ready.at((t - squares) // group + 1))
                    act.activation(sq[:, t % squares, :], src[:, t, :], ACT.Square).then_inc(sq_ready.sem, 1)
                if g:
                    root(g - 1)
            root(groups - 1)
            if ahead:
                high(act)
            if bias is not None:
                for t in range(tiles):
                    act.wait_ge(scaled.sem, scaled.at(t + 1))
                    act.activation(dst[:, t, :], dst[:, t, :], ACT.Identity, bias=bias[:, t:t + 1])

        @block.vector
        def _(dve):
            step = Chain(dve, s.dve_chain)

            def centre(g):
                dve.wait_ge(mean_ready.sem, mean_ready.at(g + 1))
                for u in range(group):
                    t = src[:, g * group + u, :]
                    dve.scalar_tensor_tensor(t, s.ps[4 + g % 2][:], -1.0 / n, t, ALU.mult, ALU.add).then_inc(cen_ready.sem, 1)

            if center:
                centre(0)
            for g in range(groups):
                if center and g + 1 < groups:
                    centre(g + 1)
                dve.wait_ge(std_ready.sem, std_ready.at(g + 1))
                if center:
                    dve.wait_ge(cen_ready.sem, cen_ready.at((g + 1) * group))
                r = std[:, g % 2, :]
                step(dve.reciprocal(r, r))
                both = range(g * group, (g + 1) * group)
                for t in both:
                    ins = dve.scalar_tensor_tensor(dst[:, t, :], src[:, t, :], gain[:, t:t + 1], r, ALU.mult, ALU.mult)
                    if bias is not None:
                        ins.then_inc(scaled.sem, 1)
                if bias is None:
                    ins.then_inc(out_ready.sem, 1)

        @block.gpsimd
        def _(pool):
            if ahead:
                low(pool)
    sq_ready.passed(tiles)
    for c in (var_ready, std_ready):
        c.passed(groups)
    if bias is not None:
        assert groups == 1
        scaled.passed(tiles)
    else:
        out_ready.passed(groups)
    if center:
        mean_ready.passed(groups)
        cen_ready.passed(tiles)


def norm_heads(s, src, tiles, dst, scratch, eps, gain, bias, post, ahead=False):
    sq, std = scratch[:, 0:2, :], scratch[0:tiles, 2, :]
    mean_ready, cen_ready, sq_ready, var_ready, std_ready, out_ready = s.norm_sems
    spread, _ = s.pair_sems
    high, low = split_ahead(s) if ahead else (None, None)
    with s.nc.Block() as block:
        @block.tensor
        def _(pe):
            def mean(g):
                if g >= 2:
                    pe.wait_ge(cen_ready.sem, cen_ready.at(g - 1))
                pe.matmul(s.ps[4 + g % 2][:], s.ones, src[:, g, :], start=True, stop=True).then_inc(mean_ready.sem, 1)

            mean(0)
            for g in range(tiles):
                if g + 1 < tiles:
                    mean(g + 1)
                pe.wait_ge(sq_ready.sem, sq_ready.at(g + 1))
                into = s.pick[:, HEADS - 1 - g:HEADS - 1 - g + tiles]
                pe.matmul(s.ps[6][0:tiles, :], into, sq[:, g % 2, :], start=g == 0, stop=g == tiles - 1).then_inc(var_ready.sem, 1)
            pe.wait_ge(std_ready.sem, std_ready.at(2))
            for g in range(tiles):
                if g >= BANKS:
                    pe.wait_ge(out_ready.sem, out_ready.at(g - BANKS + 1))
                pe.matmul(s.ps[g % BANKS][:], s.eye[0:tiles, g:g + 1].broadcast_to([tiles, P]), std, start=True, stop=True).then_inc(spread.sem, 1)

        @block.scalar
        def _(act):
            for g in range(tiles):
                act.wait_ge(cen_ready.sem, cen_ready.at(g + 1))
                if g >= 2:
                    act.wait_ge(var_ready.sem, var_ready.at(g - 1))
                act.activation(sq[:, g % 2, :], src[:, g, :], ACT.Square).then_inc(sq_ready.sem, 1)
            act.wait_ge(var_ready.sem, var_ready.at(tiles))
            act.activation(std, s.ps[6][0:tiles, :], ACT.Sqrt, bias=s.eps[eps][0:tiles, :], scale=1.0 / P).then_inc(std_ready.sem, 1)
            if ahead:
                high(act)

        @block.vector
        def _(dve):
            step = Chain(dve, s.dve_chain)
            for g in range(tiles):
                dve.wait_ge(mean_ready.sem, mean_ready.at(g + 1))
                dve.scalar_tensor_tensor(src[:, g, :], s.ps[4 + g % 2][:], -1.0 / P, src[:, g, :], ALU.mult, ALU.add).then_inc(cen_ready.sem, 1)
            dve.wait_ge(std_ready.sem, std_ready.at(1))
            dve.reciprocal(std, std).then_inc(std_ready.sem, 1)
            dve.wait_ge(cen_ready.sem, cen_ready.at(tiles))
            for g in range(tiles):
                dve.wait_ge(spread.sem, spread.at(g + 1))
                step(dve.scalar_tensor_tensor(dst[:, g, :], src[:, g, :], gain[:, g:g + 1], s.ps[g % BANKS][:], ALU.mult, ALU.mult))
                if bias is None:
                    ins = dve.tensor_tensor(dst[:, g, :], dst[:, g, :], post[:, g, :], ALU.mult)
                else:
                    ins = dve.scalar_tensor_tensor(dst[:, g, :], dst[:, g, :], bias[:, g:g + 1], post[:, g, :], ALU.add, ALU.mult)
                ins.then_inc(out_ready.sem, 1)

        @block.gpsimd
        def _(pool):
            if ahead:
                low(pool)
    for c in (mean_ready, cen_ready, sq_ready, var_ready, out_ready, spread):
        c.passed(tiles)
    std_ready.passed(2)


def softplus_rows(s, jobs):
    ready, taken = s.pair_sems
    with s.nc.Block() as block:
        @block.scalar
        def _(act):
            step = Chain(act, s.act_chain)
            for n, (x, out, e, w, d, sigmoid) in enumerate(jobs):
                step(act.activation(e, x, ACT.Abs))
                act.activation(e, e, ACT.Exp, scale=-1.0).then_inc(ready.sem, 1)
                act.wait_ge(taken.sem, taken.at(n + 1))
                act.activation(out, w, ACT.Ln).then_inc(ready.sem, 1)

        @block.vector
        def _(dve):
            step = Chain(dve, s.dve_chain)
            for n, (x, out, e, w, d, sigmoid) in enumerate(jobs):
                dve.wait_ge(ready.sem, ready.at(2 * n + 1))
                dve.tensor_scalar(w, e, 1.0, None, ALU.add).then_inc(taken.sem, 1)
                dve.wait_ge(taken.sem, taken.at(n + 1))
                step(dve.tensor_scalar(d, w, 1.0, None, ALU.subtract))
                step(dve.tensor_tensor(d, e, d, ALU.subtract))
                dve.wait_ge(ready.sem, ready.at(2 * n + 2))
                step(dve.reciprocal(w, w))
                step(dve.tensor_tensor(d, d, w, ALU.mult))
                step(dve.tensor_tensor(d, d, out, ALU.add))
                step(dve.tensor_scalar(e, x, 0.0, None, ALU.min if sigmoid else ALU.max))
                step(dve.tensor_tensor(out, e, d, ALU.subtract if sigmoid else ALU.add))
    ready.passed(2 * len(jobs))
    taken.passed(len(jobs))


def load_start(s):
    with s.nc.Block() as block:
        @block.sync
        def _(sync):
            for dst, src in ((s.base[:], s.I["base"]), (s.par[:], s.I["params"]), (s.xflat, s.I["x"])):
                sync.dma_start(dst, src).then_inc(s.loaded.sem, 16)
            sync.wait_ge(s.loaded.sem, s.loaded.at(48))
    s.loaded.passed(48)


def causal_conv(s, dve, step, dst, src, taps, t):
    n = len(taps)
    step(dve.tensor_scalar(dst, src(0), taps[0][:, t], None, ALU.mult))
    for k in range(1, n):
        ins = dve.scalar_tensor_tensor(dst, src(k), taps[k][:, t], dst, ALU.mult, ALU.add)
        if k < n - 1:
            step(ins)
    return ins


def first_projection(s):
    v = s.view
    s.sz, s.qk, s.sg = v(0, 8), v(21, 8), v(29, 8)
    s.xbc = s.arena[:, 8 * T:8 * T + 12 * (T + 3)].rearrange("p (a t) -> p a t", a=12)
    s.vt = v(37, 8).rearrange("p a t -> p (a t)").rearrange("p (t c) -> p t c", t=TT)
    s.dt_raw = s.arena[0:SSD_HEADS, 45 * T:46 * T]
    with s.nc.Block() as block:
        @block.gpsimd
        def _(pool):
            pool.memset(s.xbc[:, :, 0:3], 0.0)
    whole = lambda k: s.x[:, k, :]
    x = Split(whole, DT, s.rounded(58), s.rounded(66))
    s.xs = v(46, 12)

    def conv(dve, step, t):
        ins = causal_conv(s, dve, step, s.xs[:, t, :], lambda k: s.xbc[:, t, k:k + T], taps, bass.ds(t, 1))
        ins.then_inc(s.convolved.sem, 1)

    def store_v(act, step, t, ps):
        if t < 12:
            act.wait_ge(s.convolved.sem, s.convolved.at(t + 1))
            act.activation(s.xs[:, t, :], s.xs[:, t, :], ACT.Silu, bias=s.col("ssd_conv_b")[:, t:t + 1])
        return store_by_token(s.vt, TT)(act, step, t, ps)

    def first_convs(dve, step, p, t, u):
        conv(dve, step, t)

    def last_convs(dve, step, p, t, u):
        if u % 2 == 0:
            conv(dve, step, 8 + t // 2)

    taps = [s.col(f"ssd_conv{k}") for k in range(SSD_CONV)]

    rope, tmp = v(8, 2), v(10, 2)
    turned_ready, rotated = s.pair_sems

    def load_rope(sync):
        sync.wait_ge(s.convolved.sem, s.convolved.at(12))
        sync.dma_start(rope.rearrange("p a t -> p (a t)"), s.I["rope"]).then_inc(s.loaded.sem, 16)

    def partners(pe, j):
        for t in (2 * j, 2 * j + 1):
            if j == 0:
                pe.wait_ge(s.evac_done.sem, 8 + 12 + 1 + 8)
            if t >= 4:
                pe.wait_ge(rotated.sem, rotated.at(t - 3))
            pe.matmul(s.ps[4 + t % 4][:], s.turn, s.qk[:, t, :], start=True, stop=True).then_inc(turned_ready.sem, 1)

    def rotate(dve, step, p, t, u):
        if t == 0:
            dve.wait_ge(s.convolved.sem, s.convolved.at(12))
            dve.wait_ge(s.loaded.sem, s.loaded.at(16))
        dve.wait_ge(turned_ready.sem, turned_ready.at(t + 1))
        step(dve.tensor_tensor(tmp[:, t % 2, :], s.ps[4 + t % 4][:], rope[:, 1, :], ALU.mult))
        step(dve.tensor_tensor(s.qk[:, t, :], s.qk[:, t, :], rope[:, 0, :], ALU.mult))
        dve.tensor_tensor(s.qk[:, t, :], s.qk[:, t, :], tmp[:, t % 2, :], ALU.add).then_inc(rotated.sem, 1)

    linears(s, [
        part("w_z", x, store(lambda t: s.sz[:, t, :], ACT.Silu)),
        part("w_xbc", x, store(lambda t: s.xbc[:, t, 3:3 + T])),
        part("w_dt", whole, store(lambda t: s.dt_raw, ACT.Identity, lambda t: s.col("dt_bias")[0:SSD_HEADS, :]), tile=SSD_HEADS),
        part("w_qk", x, store(lambda t: s.qk[:, t, :]), side=first_convs, side_steps=12, side_after="w_xbc"),
        part("w_g", x, store(lambda t: s.sg[:, t, :], ACT.Silu), side=last_convs, side_steps=6),
        part("w_v", x, store_v, tokens=TT, pe_before=partners, side=rotate),
    ], sync_last=load_rope)
    s.loaded.passed(16)
    turned_ready.passed(8)
    rotated.passed(8)
    s.convolved.passed(12)


def ssd_prepare(s):
    row = lambda k: s.arena[0:SSD_HEADS, k * T:(k + 1) * T]
    s.dt, s.acs, e, w, d = row(61), row(45), row(58), row(59), row(60)
    softplus_rows(s, [(s.dt_raw, s.dt, e, w, d, False)])
    with s.nc.Block() as block:
        @block.scalar
        def _(act):
            act.activation(s.small[0:SSD_HEADS, 0:1], s.col("a_log")[0:SSD_HEADS, :], ACT.Exp).then_inc(s.pair_sems[0].sem, 1)

        @block.vector
        def _(dve):
            step = Chain(dve, s.dve_chain)
            step(dve.memset(w, 1.0))
            dve.wait_ge(s.pair_sems[0].sem, s.pair_sems[0].at(1))
            step(dve.tensor_scalar(d, s.dt, s.small[0:SSD_HEADS, 0:1], -1.0, ALU.mult, ALU.mult))
            step(dve.tensor_tensor_scan(s.acs, w, d, 0.0, ALU.mult, ALU.add))
    s.pair_sems[0].passed(1)


def ssd_turn(s):
    v = s.view
    s.dt_col, s.acs_col = (s.small[:, 64 + 64 * k:128 + 64 * k].rearrange("p (a h) -> p a h", a=TT) for k in range(2))
    s.xdt = v(63, 8).rearrange("p a t -> p (a t)").rearrange("p (t c) -> p t c", t=TT)
    s.cb = s.arena[:, 16 * T:16 * T + 2 * SEG_LEN].rearrange("p (g n) -> p g n", g=2)
    rows_ready, cols_ready, x_ready, x_done, cb_ready, cb_done = s.norm_sems
    with s.nc.Block() as block:
        @block.tensor
        def _(pe):
            for k, src in enumerate((s.dt, s.acs)):
                for a in range(TT):
                    mm = pe.transpose(s.ps[k][:, a * SSD_HEADS:(a + 1) * SSD_HEADS], src[:, a * P:(a + 1) * P], s.eye[0:SSD_HEADS, 0:SSD_HEADS])
            mm.then_inc(rows_ready.sem, 1)
            for a in range(TT):
                for half in range(2):
                    n = 2 * a + half
                    if n >= 2:
                        pe.wait_ge(x_done.sem, x_done.at(n - 1))
                    for u in range(4):
                        mm = pe.transpose(s.ps[2 + half][:, u * P:(u + 1) * P], s.xs[:, half * 4 + u, a * P:(a + 1) * P], s.eye)
                    mm.then_inc(x_ready.sem, 1)
            for g in range(2):
                for a in range(TT):
                    n = 4 * g + a
                    if n >= 4:
                        pe.wait_ge(cb_done.sem, cb_done.at(n - 3))
                    pe.matmul(s.ps[4 + a][:, 0:seg_width(a)], s.xs[:, 8 + g, a * P:(a + 1) * P], s.xs[:, 10 + g, a * P:T],
                              start=True, stop=True).then_inc(cb_ready.sem, 1)

        @block.vector
        def _(dve):
            dve.wait_ge(rows_ready.sem, rows_ready.at(1))
            dve.tensor_copy(s.acs_col.rearrange("p a h -> p (a h)"), s.ps[1][:, 0:64])
            dve.tensor_copy(s.dt_col.rearrange("p a h -> p (a h)"), s.ps[0][:, 0:64]).then_inc(cols_ready.sem, 1)
            dve.wait_ge(cols_ready.sem, cols_ready.at(1))
            for a in range(TT):
                for half in range(2):
                    dve.wait_ge(x_ready.sem, x_ready.at(2 * a + half + 1))
                    out = s.xdt[:, a, half * 512:half * 512 + 512].rearrange("p (h d) -> p h d", h=8)
                    dve.tensor_tensor(out, s.ps[2 + half][:].rearrange("p (h d) -> p h d", h=8),
                                      s.dt_col[:, a, half * 8:half * 8 + 8].unsqueeze(2).broadcast_to([P, 8, SSD_HD]),
                                      ALU.mult).then_inc(x_done.sem, 1)
            for g in range(2):
                for a in range(TT):
                    dve.wait_ge(cb_ready.sem, cb_ready.at(4 * g + a + 1))
                    seg = s.cb[:, g, SEG[a]:SEG[a] + seg_width(a)]
                    if a < TT - 1:
                        dve.tensor_copy(seg[:, P:], s.ps[4 + a][:, P:seg_width(a)])
                    dve.tensor_tensor(seg[:, 0:P], s.ps[4 + a][:, 0:P], s.causal, ALU.mult).then_inc(cb_done.sem, 1)
    for c, n in ((rows_ready, 1), (cols_ready, 1), (x_ready, 8), (x_done, 8), (cb_ready, 8), (cb_done, 8)):
        c.passed(n)


def ssd_heads(s):
    s.u = s.view(8, 8)
    s.att = [s.arena[:, o:o + SEG_LEN] for o in (58 * T, 58 * T + SEG_LEN, 71 * T)]
    bc_ready, diff_ready, exp_ready, att_ready, y_ready, y_done = s.norm_sems
    with s.nc.Block() as block:
        @block.tensor
        def _(pe):
            def sums(h):
                if h >= 2:
                    pe.wait_ge(diff_ready.sem, diff_ready.at(h - 1))
                pe.matmul(s.ps[h % 2][:], s.eye[0:SSD_HEADS, h:h + 1].broadcast_to([SSD_HEADS, P]), s.acs, start=True, stop=True).then_inc(bc_ready.sem, 1)

            sums(0)
            sums(1)
            for h in range(SSD_HEADS):
                if h + 2 < SSD_HEADS:
                    sums(h + 2)
                j, lo = h // 2, (h % 2) * SSD_HD
                if h % 2 == 0 and j >= 2:
                    pe.wait_ge(y_done.sem, y_done.at(j - 1))
                pe.wait_ge(att_ready.sem, att_ready.at(h + 1))
                for a in range(TT):
                    mm = pe.matmul(s.ps[2 + j % 2][lo:lo + SSD_HD, a * P:T], s.xdt[:, a, h * SSD_HD:(h + 1) * SSD_HD],
                                   s.att[h % 3][:, SEG[a]:SEG[a] + seg_width(a)], start=a == 0, stop=a == TT - 1, skip_group_check=True)
                mm.then_inc(y_ready.sem, 1)

        @block.scalar
        def _(act):
            for h in range(SSD_HEADS):
                act.wait_ge(diff_ready.sem, diff_ready.at(h + 1))
                act.activation(s.att[h % 3], s.att[h % 3], ACT.Exp).then_inc(exp_ready.sem, 1)

        @block.vector
        def _(dve):
            step = Chain(dve, s.dve_chain)

            def differences(h):
                dve.wait_ge(bc_ready.sem, bc_ready.at(h + 1))
                if h >= 3:
                    dve.wait_ge(y_ready.sem, y_ready.at(h - 2))
                for a in range(TT):
                    ins = dve.tensor_scalar(s.att[h % 3][:, SEG[a]:SEG[a] + seg_width(a)], s.ps[h % 2][:, a * P:T],
                                            s.acs_col[:, a, h:h + 1], 0.0, ALU.subtract, ALU.min)
                ins.then_inc(diff_ready.sem, 1)

            def gated(j):
                dve.wait_ge(y_ready.sem, y_ready.at(2 * j + 2))
                ins = dve.scalar_tensor_tensor(s.u[:, j, :], s.xs[:, j, :], s.col("ssd_d")[:, j:j + 1], s.ps[2 + j % 2][:], ALU.mult, ALU.add)
                ins.then_inc(y_done.sem, 1)
                dve.wait_ge(y_done.sem, y_done.at(j + 1))
                step(dve.tensor_tensor(s.u[:, j, :], s.u[:, j, :], s.sz[:, j, :], ALU.mult))

            differences(0)
            for h in range(SSD_HEADS):
                if h + 1 < SSD_HEADS:
                    differences(h + 1)
                dve.wait_ge(exp_ready.sem, exp_ready.at(h + 1))
                dve.tensor_tensor(s.att[h % 3], s.att[h % 3], s.cb[:, h // 8, :], ALU.mult).then_inc(att_ready.sem, 1)
                if h % 2 == 0 and h:
                    gated(h // 2 - 1)
            gated(SSD_HEADS // 2 - 1)
    for c, n in ((bc_ready, 16), (diff_ready, 16), (exp_ready, 16), (att_ready, 16), (y_ready, 16), (y_done, 8)):
        c.passed(n)


def retention(s):
    decay = s.view(46, 8)
    s.yr = s.view(63, 8)
    s_ready, s_done, y_ready, y_done, _, _ = s.norm_sems
    with s.nc.Block() as block:
        @block.sync
        def _(sync):
            sync.dma_start(decay.rearrange("p a t -> p (a t)"), s.I["decay"]).then_inc(s.loaded.sem, 16)

        @block.tensor
        def _(pe):
            def scores(h):
                j, lo = h // 2, (h % 2) * RET_QK
                for a in range(TT):
                    if h >= 1:
                        pe.wait_ge(s_done.sem, s_done.at(4 * (h - 1) + a + 1))
                    pe.matmul(s.ps[a][:, 0:seg_width(a)], s.qk[lo:lo + RET_QK, 4 + j, a * P:(a + 1) * P],
                              s.qk[lo:lo + RET_QK, j, a * P:T], start=True, stop=True).then_inc(s_ready.sem, 1)

            scores(0)
            for h in range(RET_HEADS):
                if h >= 2:
                    pe.wait_ge(y_done.sem, y_done.at(h - 1))
                for a in range(TT):
                    pe.wait_ge(s_done.sem, s_done.at(4 * h + a + 1))
                    mm = pe.matmul(s.ps[4 + h % 2][:, a * P:T], s.vt[:, a, h * RET_DV:(h + 1) * RET_DV],
                                   s.att[h % 2][:, SEG[a]:SEG[a] + seg_width(a)], start=a == 0, stop=a == TT - 1, skip_group_check=True)
                mm.then_inc(y_ready.sem, 1)
                if h + 1 < RET_HEADS:
                    scores(h + 1)

        @block.vector
        def _(dve):
            dve.wait_ge(s.loaded.sem, s.loaded.at(16))
            for h in range(RET_HEADS):
                if h >= 2:
                    dve.wait_ge(y_ready.sem, y_ready.at(h - 1))
                for a in range(TT):
                    dve.wait_ge(s_ready.sem, s_ready.at(4 * h + a + 1))
                    dve.tensor_tensor(s.att[h % 2][:, SEG[a]:SEG[a] + seg_width(a)], s.ps[a][:, 0:seg_width(a)],
                                      decay[:, h, 0:seg_width(a)], ALU.mult).then_inc(s_done.sem, 1)

        @block.scalar
        def _(act):
            for h in range(RET_HEADS):
                act.wait_ge(y_ready.sem, y_ready.at(h + 1))
                act.activation(s.yr[:, h, :], s.ps[4 + h % 2][:], ACT.Copy).then_inc(y_done.sem, 1)
    s.loaded.passed(16)
    for c, n in ((s_ready, 32), (s_done, 32), (y_ready, 8), (y_done, 8)):
        c.passed(n)


def first_mixer(s):
    first_projection(s)
    ssd_prepare(s)
    ssd_turn(s)
    ssd_heads(s)
    norm(s, s.u, 8, 4, s.u, s.view(46, 6), False, 0, s.col("ssd_norm"))
    retention(s)
    norm_heads(s, s.yr, 8, s.yr, s.view(46, 3), 0, s.col("gn_w"), s.col("gn_b"), s.sg, ahead=True)
    both = Split(lambda k: s.u[:, k, :] if k < 8 else s.yr[:, k - 8, :], 16, s.rounded(46),
                 lambda k: s.rounded(8)(k) if k < 8 else s.rounded(63 - 8)(k))
    linears(s, [part("w_mix", both, residual(s, ALPHA), by="dve")])
    norm(s, s.x, 8, 8, s.x, s.view(0, 10), True, 0, s.col("ln1_g"), s.col("ln1_b"), ahead=True)


def attention_unit(q, k, keys, table, slope, ok, scale, v, pieces, channels, row, causal, out):
    u = Names()
    u.q, u.k, u.keys, u.table, u.slope, u.ok, u.scale = q, k, keys, table, slope, ok, scale
    u.v, u.pieces, u.channels, u.row, u.causal, u.out = v, pieces, channels, row, causal, out
    return u


AHEAD = 2
PROBS = 4


def attention(s, units):
    nc = s.nc
    sc_ready, shifted, exp_ready, p_ready, pt_ready, pt_done = s.norm_sems
    o_ready, o_done = s.pair_sems
    steps = [(n, u, a) for n, (u, a) in enumerate((u, a) for u in range(len(units)) for a in range(TT))]
    outs = [(u, m) for u in range(len(units)) for m in range(units[u].pieces)]
    with nc.Block() as block:
        @block.tensor
        def _(pe):
            def scores(n, u, a):
                if n >= 3:
                    pe.wait_ge(shifted.sem, shifted.at(n - 2))
                q, k = units[u].q(a), units[u].k
                w = units[u].keys(a)
                for m in range(len(q)):
                    mm = pe.matmul(s.ps[n % 3][:, 0:w], q[m], k[m][:, 0:w], start=m == 0, stop=m == len(q) - 1)
                mm.then_inc(sc_ready.sem, 1)

            def turned(n, u, a):
                if n >= 3:
                    pe.wait_ge(pt_done.sem, pt_done.at(n - 2))
                pe.wait_ge(p_ready.sem, p_ready.at(n + 1))
                w = units[u].keys(a)
                for st in range(-(-w // P)):
                    ww = min(P, w - st * P)
                    mm = pe.transpose(s.ps[3 + n % 3][0:ww, st * P:(st + 1) * P], s.prob[n % PROBS][:, st * P:st * P + ww], s.eye)
                mm.then_inc(pt_ready.sem, 1)

            def values(u):
                pe.wait_ge(pt_done.sem, pt_done.at(TT * (u + 1)))
                w = units[u].keys(TT - 1)
                n_st = -(-w // P)
                for m in range(units[u].pieces):
                    o = outs.index((u, m))
                    if o >= 2:
                        pe.wait_ge(o_done.sem, o_done.at(o - 1))
                    for st in range(n_st):
                        ww = min(P, w - st * P)
                        lo = st * P if units[u].causal else 0
                        ch = units[u].channels
                        row = units[u].row
                        mm = pe.matmul(s.ps[6 + o % 2][row:row + ch, lo:T], units[u].v(st, m), s.pt[u % 2][0:ww, st, lo:T],
                                       start=st == 0, stop=st == n_st - 1, skip_group_check=True)
                    mm.then_inc(o_ready.sem, 1)

            for m in steps[:AHEAD + 1]:
                scores(*m)
            for n, u, a in steps:
                if n + AHEAD + 1 < len(steps):
                    scores(*steps[n + AHEAD + 1])
                turned(n, u, a)
                if a == 0 and u:
                    values(u - 1)
            values(len(units) - 1)

        @block.vector
        def _(dve):
            step = Chain(dve, s.dve_chain)

            def shift(n, u, a):
                dve.wait_ge(sc_ready.sem, sc_ready.at(n + 1))
                w, un = units[u].keys(a), units[u]
                sc, neg = s.prob[n % PROBS][:, 0:w], s.small[:, 8 + n % PROBS:9 + n % PROBS]
                if n >= PROBS:
                    dve.wait_ge(pt_ready.sem, pt_ready.at(n - PROBS + 1))
                if un.table is not None:
                    step(dve.scalar_tensor_tensor(sc, un.table(a), un.slope, s.ps[n % 3][:, 0:w], ALU.mult, ALU.add))
                else:
                    step(dve.tensor_scalar(sc, s.ps[n % 3][:, 0:w], un.scale, None, ALU.mult))
                dve.tensor_reduce(neg, sc, AX.X, ALU.max, negate=True).then_inc(shifted.sem, 1)

            for m in steps[:AHEAD]:
                shift(*m)
            for n, u, a in steps:
                if n + AHEAD < len(steps):
                    shift(*steps[n + AHEAD])
                dve.wait_ge(exp_ready.sem, exp_ready.at(n + 1))
                w, un = units[u].keys(a), units[u]
                total = s.small[:, 12 + n % PROBS:13 + n % PROBS]
                step(dve.reciprocal(total, total))
                pr = s.prob[n % PROBS][:, 0:w]
                if un.ok is not None:
                    ins = dve.scalar_tensor_tensor(pr, pr, total, un.ok(a), ALU.mult, ALU.mult)
                else:
                    ins = dve.tensor_scalar(pr, pr, total, None, ALU.mult)
                ins.then_inc(p_ready.sem, 1)

        @block.scalar
        def _(act):
            def exps(n, u, a):
                act.wait_ge(shifted.sem, shifted.at(n + 1))
                if n >= PROBS:
                    act.wait_ge(p_ready.sem, p_ready.at(n - PROBS + 1))
                pr = s.prob[n % PROBS][:, 0:units[u].keys(a)]
                act.activation(pr, pr, ACT.Exp, bias=s.small[:, 8 + n % PROBS:9 + n % PROBS],
                               accum_out=s.small[:, 12 + n % PROBS:13 + n % PROBS]).then_inc(exp_ready.sem, 1)

            def take(u):
                for m in range(units[u].pieces):
                    o = outs.index((u, m))
                    act.wait_ge(o_ready.sem, o_ready.at(o + 1))
                    row = units[u].row
                    act.activation(units[u].out(m), s.ps[6 + o % 2][row:row + units[u].channels, :], ACT.Copy).then_inc(o_done.sem, 1)

            for m in steps[:AHEAD]:
                exps(*m)
            for n, u, a in steps:
                if n + AHEAD < len(steps):
                    exps(*steps[n + AHEAD])
                act.wait_ge(pt_ready.sem, pt_ready.at(n + 1))
                w = units[u].keys(a)
                if a == 0 and u >= 2:
                    act.wait_ge(o_ready.sem, o_ready.at(outs.index((u - 1, 0))))
                n_st, ww = -(-w // P), min(P, w)
                act.activation(s.pt[u % 2][0:ww, 0:n_st, a * P:(a + 1) * P],
                               s.ps[3 + n % 3][0:ww, 0:n_st * P].rearrange("p (s q) -> p s q", s=n_st), ACT.Copy).then_inc(pt_done.sem, 1)
                if a == 1 and u:
                    take(u - 1)
            take(len(units) - 1)
    for c in s.norm_sems:
        c.passed(len(steps))
    for c in s.pair_sems:
        c.passed(len(outs))


def cross_attention(s):
    v = s.view
    mem = v(0, 4).rearrange("p a t -> p (a t)").rearrange("p (k m) -> p k m", k=DT)
    xk = v(4, 4).rearrange("p a t -> p (a t)").rearrange("p (k m) -> p k m", k=DT)
    xv = v(8, 4).rearrange("p a t -> p (a t)").rearrange("p (t c) -> p t c", t=2)
    xq, o = v(12, 8), v(20, 8)
    s.prob = [s.arena[:, (28 + k) * T:(29 + k) * T] for k in range(PROBS)]
    s.pt = [v(32 + 4 * k, 4) for k in range(2)]
    with s.nc.Block() as block:
        @block.sync
        def _(sync):
            sync.dma_start(mem.rearrange("p k m -> p (k m)"), s.I["mem"]).then_inc(s.loaded.sem, 16)
            sync.wait_ge(s.loaded.sem, s.loaded.at(16))
    s.loaded.passed(16)

    half = lambda at: lambda k: s.rounded(at)(k // 2)[:, (k % 2) * MEM:(k % 2 + 1) * MEM]
    mem_split = Split(lambda k: mem[:, k, :], DT, half(40), half(44))
    x_split = Split(lambda k: s.x[:, k, :], DT, s.rounded(48), s.rounded(56))
    linears(s, [
        part("w_xk", mem_split, store(lambda t: xk[:, t, :]), n=MEM),
        part("w_xv", mem_split, store_by_token(xv, 2), tokens=2),
        part("w_xq", x_split, store(lambda t: xq[:, t, :])),
    ])

    def unit(h):
        return attention_unit(
            q=lambda a: [xq[:, 2 * h + m, a * P:(a + 1) * P] for m in range(2)], k=[xk[:, 2 * h + m, :] for m in range(2)],
            keys=lambda a: MEM, table=None, slope=None, ok=None, scale=XHD ** -0.5,
            v=lambda st, m: xv[:, st, h * XHD + m * P:h * XHD + (m + 1) * P], pieces=2, channels=P, row=0, causal=False,
            out=lambda m: o[:, 2 * h + m, :])

    attention(s, [unit(h) for h in range(XH)])
    linears(s, [part("w_xo", Split(lambda k: o[:, k, :], DT, s.rounded(40), s.rounded(20)), residual(s, ALPHA), by="dve")])
    norm(s, s.x, 8, 8, s.x, v(0, 10), True, 0, s.col("ln2_g"), s.col("ln2_b"), ahead=True)


def conv_glu(s):
    v = s.view
    gated = v(0, FF_TILES)
    up = s.arena[:, 22 * T:22 * T + 2 * (T + 2)].rearrange("p (n t) -> p n t", n=2)
    acc = v(27, 2)
    silu_ready = s.norm_sems[0]
    nc = s.nc
    with nc.Block() as block:
        @block.gpsimd
        def _(pool):
            pool.memset(up[:, :, 0:2], 0.0)

    one = lambda name, t: s.col(name)[:, bass.ds(t, 1)]

    def evac(dve, step, t, ps):
        odd = evac.turn % 2
        evac.turn += 1
        src, dst = up[:, odd, :], acc[:, odd, :]
        step(dve.tensor_scalar(src[:, 2:2 + T], ps, one("b_up", t), None, ALU.add))
        step(dve.tensor_scalar(dst, src[:, 0:T], one("ffn_conv0", t), None, ALU.mult))
        step(dve.scalar_tensor_tensor(dst, src[:, 1:1 + T], one("ffn_conv1", t), dst, ALU.mult, ALU.add))
        ins = dve.scalar_tensor_tensor(dst, src[:, 2:2 + T], one("ffn_conv2", t), dst, ALU.mult, ALU.add)
        if not odd:
            return ins
        step(ins)
        dve.wait_ge(silu_ready.sem, silu_ready.at(t // 2 + 1))
        return dve.scalar_tensor_tensor(gated[:, t // 2, :], dst, one("ffn_conv_b", t), gated[:, t // 2, :], ALU.add, ALU.mult)

    def silu(act, tile0, t):
        act.wait_ge(s.evac_done.sem, tile0 + t + 1)
        if not isinstance(t, int):
            act.sem_inc(s.held, 1)
        act.activation(gated[:, t // 2, :], acc[:, 0, :], ACT.Silu, bias=one("ffn_conv_b", t)).then_inc(silu_ready.sem, 1)

    def side(act, step, p, t, u):
        if u % 2 == 0 and not (isinstance(t, int) and t < 2):
            silu(act, p.tile0, t - 2)

    def last_silu(act):
        silu(act, s.tiles - 2 * FF_TILES, 2 * FF_TILES - 2)

    evac.turn = 0
    linears(s, [part("w_up", Split(lambda k: s.x[:, k, :], DT, s.rounded(53), s.rounded(61)), evac, by="dve", steps=3.5, side=side)], act_end=last_silu)
    silu_ready.passed(FF_TILES)
    linears(s, [part("w_down", Split(lambda k: gated[:, k, :], FF_TILES, s.rounded(22), s.rounded(0)), residual(s, ALPHA), by="dve")])
    norm(s, s.x, 8, 8, s.x, v(0, 10), True, 0, s.col("ln3_g"), s.col("ln3_b"))


def store_out(s, out):
    with s.nc.Block() as block:
        @block.sync
        def _(sync):
            sync.dma_start(out, s.xflat).then_inc(s.loaded.sem, 16)
            sync.wait_ge(s.loaded.sem, s.loaded.at(16))
    s.loaded.passed(16)


def rounded_tile(s, t, arena_at):
    if t not in s.rounded_tiles:
        s.rounded_tiles[t] = s.nc.alloc_sbuf_tensor_at(f"rounded{t}", [P, T], F32R, offset=arena_at + 4 * T * t)[:]
    return s.rounded_tiles[t]


def build(nc, I, at, out, upto=99):
    s = Names()
    s.nc, s.I, s.next_part, s.tiles, s.units, s.split_units, s.ahead, s.slab_end, s.first_slab = nc, I, 0, 0, 0, 0, 0, [], [0]
    for name, _, _ in PLAN:
        s.first_slab.append(s.first_slab[-1] + I[name].shape[0])
    s.x = nc.alloc_sbuf_tensor("x_res", [P, DT, T], F32)[:]
    s.xflat = s.x.rearrange("p k t -> p (k t)")
    s.ring = nc.alloc_sbuf_tensor("weight_ring", [P, RING, SLAB], F32)[:]
    s.base = nc.alloc_sbuf_tensor("base_tables", [P, 4 * P + 2 + 2 * HEADS - 1], F32)
    s.par = nc.alloc_sbuf_tensor("params_sb", [P, I["params"].shape[1]], F32)
    s.small = nc.alloc_sbuf_tensor("small", [P, 256], F32)
    arena_at = nc.sbuf_base
    s.arena = nc.alloc_sbuf_tensor("arena", [P, 74 * T], F32)
    s.rounded_tiles = {}
    s.rounded = lambda at: lambda k: rounded_tile(s, at + k, arena_at)
    units_at = nc.sbuf_base
    s.w_hi, s.w_lo = ([nc.alloc_sbuf_tensor(f"weights_{name}{k}", [P, UNIT_K * P], F32R)[:] for k in range(UNITS)] for name in ("hi", "lo"))
    s.expert_sums = nc.alloc_sbuf_tensor_at("expert_sums", [P, 2 * UNITS * UNIT_K * P], F32, offset=units_at)[:]
    s.ps = [nc.alloc_psum_tensor(f"bank{b}", [P, T], F32) for b in range(8)]
    s.eye, s.turn, s.causal, s.ones = (s.base[:, k * P:(k + 1) * P] for k in range(4))
    s.pick = s.base[:, 4 * P + 2:]
    s.eps = [s.base[:, 4 * P + k:4 * P + k + 1] for k in range(2)]
    s.col = lambda name: s.par[:, at[name][0]:at[name][0] + at[name][1]]
    s.view = lambda o, n: s.arena[:, o * T:(o + n) * T].rearrange("p (a t) -> p a t", t=T)
    s.slab_ready = [nc.alloc_semaphore(f"slab_ready{k}") for k in range(RING)]
    names = ("loaded", "units_done", "evac_done", "hi_made", "lo_made", "act_hi", "act_lo", "act_chain", "dve_chain")
    (s.loaded, s.units_done, s.evac_done, s.hi_made, s.lo_made, s.act_hi, s.act_lo, s.act_chain, s.dve_chain) = (Counter(nc, n) for n in names)
    s.norm_sems = [Counter(nc, f"step{k}_ready") for k in range(6)]
    s.pair_sems = [Counter(nc, f"pair{k}_ready") for k in range(2)]
    s.gathered = [Counter(nc, f"gathered{k}") for k in range(2 * GATHER)]
    s.held = nc.alloc_semaphore("held")
    s.mod_sems = [Counter(nc, n) for n in ("silu_ready", "row_turned", "ada_done", "ada_taken")]
    s.ada_ready = [Counter(nc, f"ada_ready{k}") for k in range(BANKS)]
    s.convolved = Counter(nc, "convolved")
    s.cond_loaded, s.cols_ready = Counter(nc, "cond_loaded"), Counter(nc, "cols_ready")
    stages = STAGES[:upto]
    load_start(s)
    for stage in stages:
        stage(s)
    store_out(s, out)


def second_inputs_projected(s):
    v = s.view
    s.n = v(0, 8)
    norm(s, s.x, 8, 8, s.n, v(8, 10), False, 1, s.col("norm_mix"), ahead=True)
    s.ab, s.ry, s.ax = v(16, 8), v(35, RT), v(45, 8)
    s.rx = s.arena[:, 24 * T:24 * T + RT * (T + 3)].rearrange("p (a t) -> p a t", a=RT)
    s.cx = s.arena[:, 53 * T:53 * T + 8 * (T + 2)].rearrange("p (a t) -> p a t", a=8)
    with s.nc.Block() as block:
        @block.gpsimd
        def _(pool):
            pool.memset(s.cx[:, :, 0:2], 0.0)
            pool.memset(s.rx[:, :, 0:3], 0.0)
    n = s.n_split = Split(lambda k: s.n[:, k, :], DT, s.rounded(8), s.rounded(0))

    s.rc = s.view(45, RT)

    def conv_a(dve, step, p, t, u):
        if not (isinstance(t, int) and t >= 8):
            taps = [s.col(f"conv_a{k}") for k in range(3)]
            step(causal_conv(s, dve, step, s.ax[:, t, :], lambda k: s.cx[:, t, k:k + T], taps, bass.ds(t, 1)))
            step(dve.tensor_tensor(s.ab[:, t, :], s.ab[:, t, :], s.ax[:, t, :], ALU.mult))

    def conv_r(dve, step, p, t, u):
        taps = [s.col(f"rnn_conv{k}") for k in range(4)]
        step(causal_conv(s, dve, step, s.rc[:, t, :], lambda k: s.rx[:, t, k:k + T], taps, bass.ds(t, 1)))
        step(dve.tensor_scalar(s.rc[:, t, :], s.rc[:, t, :], s.col("rnn_conv_b")[:, bass.ds(t, 1)], None, ALU.add))

    linears(s, [part("w2_ax", n, store(lambda t: s.ax[:, t, :]))])
    linears(s, [
        part("w2_ac", n, lambda dve, step, t, ps: dve.tensor_tensor(s.cx[:, t, 2:2 + T], ps, s.ax[:, t, :], ALU.mult), by="dve"),
        part("w2_ab", n, store(lambda t: s.ab[:, t, :])),
        part("w2_rx", n, store(lambda t: s.rx[:, t, 3:3 + T]), side=conv_a, side_steps=16, side_after="w2_ab"),
        part("w2_ry", n, store(lambda t: s.ry[:, t, :], ACT.Gelu_apprx_tanh), side=conv_r, side_steps=20, side_after="w2_rx"),
    ])


def rates(s):
    cols = [s.small[:, 16 + 16 * k:16 + 16 * k + RT] for k in range(6)]
    neg_lam, s.rate, e, w, d, s.neg_rate = cols
    with s.nc.Block() as block:
        @block.vector
        def _(dve):
            step = Chain(dve, s.dve_chain)
            step(dve.tensor_scalar(neg_lam, s.col("lru_lambda"), -1.0, None, ALU.mult))
    softplus_rows(s, [(neg_lam, s.rate, e, w, d, False)])
    with s.nc.Block() as block:
        @block.vector
        def _(dve):
            step = Chain(dve, s.dve_chain)
            step(dve.tensor_scalar(s.neg_rate, s.rate, -8.0, None, ALU.mult))
            step(dve.tensor_scalar(s.rate, s.rate, 8.0, None, ALU.mult))


def recurrence(s):
    v = s.view
    r, gate, a = v(24, RT), v(55, RT), v(55, RT)
    square = [s.arena[:, o * T:(o + 1) * T] for o in (34, 65)]
    ga, gb = v(66, 8), v(55, 8)
    rc = lambda k: s.rc[:, k, :]
    _, a_ready, tanh_ready, room_ready, root_ready, scanned = s.norm_sems

    def gate_inputs(dve):
        for t in range(RT):
            dve.wait_ge(s.evac_done.sem, s.tiles - RT + t + 1)
            dve.tensor_tensor(rc(t), rc(t), gate[:, t, :], ALU.mult)

    linears(s, [
        part("w2_rg", rc, store(lambda t: r[:, t, :], ACT.Sigmoid, lambda t: s.col("b_rg")[:, t:t + 1]), block_diag=True),
        part("w2_ig", rc, store(lambda t: gate[:, t, :], ACT.Sigmoid, lambda t: s.col("b_ig")[:, t:t + 1]), block_diag=True),
    ], dve_end=gate_inputs)

    def decays(act):
        for t in range(RT):
            act.activation(a[:, t, :], r[:, t, :], ACT.Exp, scale=s.neg_rate[:, t:t + 1]).then_inc(a_ready.sem, 1)
        for t in range(RT):
            act.wait_ge(a_ready.sem, a_ready.at(t + 1))
            act.activation(r[:, t, :], r[:, t, :], ACT.Tanh, scale=s.rate[:, t:t + 1]).then_inc(tanh_ready.sem, 1)

    def factor(dve, step, t):
        sq = square[t % 2]
        dve.wait_ge(a_ready.sem, a_ready.at(t + 1))
        step(dve.tensor_tensor(sq, a[:, t, :], a[:, t, :], ALU.mult))
        dve.wait_ge(tanh_ready.sem, tanh_ready.at(t + 1))
        step(dve.scalar_tensor_tensor(r[:, t, :], sq, 1.0, r[:, t, :], ALU.add, ALU.mult))
        dve.tensor_scalar(r[:, t, :], r[:, t, :], 0.0, None, ALU.max).then_inc(room_ready.sem, 1)

    def root(act, t):
        act.wait_ge(room_ready.sem, room_ready.at(t + 1))
        act.activation(r[:, t, :], r[:, t, :], ACT.Sqrt).then_inc(root_ready.sem, 1)

    def scan(dve, step, t):
        dve.wait_ge(root_ready.sem, root_ready.at(t + 1))
        step(dve.tensor_tensor(rc(t), rc(t), r[:, t, :], ALU.mult))
        step(dve.tensor_tensor_scan(r[:, t, :], a[:, t, :], rc(t), 0.0, ALU.mult, ALU.add))
        dve.tensor_tensor(s.ry[:, t, :], s.ry[:, t, :], r[:, t, :], ALU.mult).then_inc(scanned.sem, 1)

    last = DT - 1

    def beside_ga(dve, step, p, t, u):
        factor(dve, step, t)
        if t == last:
            for k in range(DT, RT):
                factor(dve, step, k)
        if t >= 2:
            scan(dve, step, t - 2)

    def beside_gb(dve, step, p, t, u):
        if t < 2:
            for k in (last - 1 + 2 * t, last + 2 * t):
                scan(dve, step, k)

    def store_ga(act, step, t, ps):
        for k in (range(2) if t == 0 else range(t + 1, t + 2) if t < last else range(DT, RT)):
            root(act, k)
        return act.activation(ga[:, t, :], ps, ACT.Sigmoid)

    def store_gb(act, step, t, ps):
        if t == 0:
            act.wait_ge(scanned.sem, scanned.at(RT))
        return act.activation(gb[:, t, :], ps, ACT.Sigmoid)

    linears(s, [
        part("w2_ga", s.n_split, store_ga, side=beside_ga, written_out=True),
        part("w2_gb", s.n_split, store_gb, side=beside_gb, written_out=True),
    ], act_start=decays)
    for c in (a_ready, tanh_ready, room_ready, root_ready, scanned):
        c.passed(RT)
    return ga, gb


def second_mixer(s):
    v = s.view
    second_inputs_projected(s)
    rates(s)
    ga, gb = recurrence(s)
    merged = v(45, 8)

    def add_b(dve, step, t, ps):
        step(dve.tensor_tensor(gb[:, t, :], ps, gb[:, t, :], ALU.mult))
        return dve.tensor_tensor(merged[:, t, :], merged[:, t, :], gb[:, t, :], ALU.add)

    linears(s, [
        part("w2_out_a", Split(lambda k: s.ab[:, k, :], DT, s.rounded(24), s.rounded(16)), lambda dve, step, t, ps: dve.tensor_tensor(merged[:, t, :], ps, ga[:, t, :], ALU.mult), by="dve"),
        part("w2_out_b", Split(lambda k: s.ry[:, k, :], RT, s.rounded(0), s.rounded(35)), add_b, by="dve", steps=1),
    ])
    linears(s, [part("w2_o", Split(lambda k: merged[:, k, :], DT, s.rounded(0), s.rounded(45)), residual(s), by="dve")])


def turn_tiles(s, src, dst):
    ready, taken = s.pair_sems
    with s.nc.Block() as block:
        @block.tensor
        def _(pe):
            for n in range(2 * TT):
                a, half = n // 2, n % 2
                if n >= 2:
                    pe.wait_ge(taken.sem, taken.at(n - 1))
                for u in range(4):
                    mm = pe.transpose(s.ps[n % 2][:, u * P:(u + 1) * P], src[:, half * 4 + u, a * P:(a + 1) * P], s.eye)
                mm.then_inc(ready.sem, 1)

        @block.vector
        def _(dve):
            for n in range(2 * TT):
                dve.wait_ge(ready.sem, ready.at(n + 1))
                dve.tensor_copy(dst[:, n // 2, (n % 2) * 512:(n % 2) * 512 + 512], s.ps[n % 2][:]).then_inc(taken.sem, 1)
    ready.passed(2 * TT)
    taken.passed(2 * TT)


PHASES = [(table, a) for a in range(TT) for table in "uv"]
CHOICE = ({0: 0, 1: 1, 3: 2, 4: 3, 6: 4}, {0: 5, 2: 6, 4: 7, 6: None})
ROUND = 1.5 * 2.0 ** 23
ROWS = 2 * GATHER
TURNS = SLOTS // ROWS


def experts(s, q, n_tok, y, keys, scratch):
    score = lambda a, c: s.ps[4 * ((a + 1) % 2) + c // 4][:, (c % 4) * P:(c % 4 + 1) * P]
    flat = lambda x: x.rearrange("p h k -> p (h k)")
    f = lambda o, n: scratch[:, o:o + n]
    g = lambda o: s.arena[:, 68 * T + o:68 * T + o + 256].rearrange("p (c k) -> p c k", k=PEER_K)
    val, ind, indf = g(0), g(256).bitcast(U32), g(512)
    rest, cand = f(0, 256), f(256, 256)
    top = [f(512 + SLOTS * k, SLOTS).rearrange("p (h k) -> p h k", k=PEER_K) for k in range(2)]
    pos = f(768, SLOTS).bitcast(U32)
    posf, row, column, number, second_number = [f(896 + SLOTS * k, SLOTS) for k in range(5)]
    biggest, total, iota = f(1536, PEER_H), f(1544, PEER_H), f(1552, PEER_K)
    match = f(1568, SLOTS * PEER_K).rearrange("p (h k i) -> p h k i", h=PEER_H, k=PEER_K)
    act_ = s.arena[:, 72 * T:73 * T]
    place = s.small[:, 192:192 + ROWS].bitcast(U32)
    of_tile = lambda x, a: x[:, a * SLOTS:(a + 1) * SLOTS]
    sc_ready, sorted_, shifted, exp_ready, chosen, gelu_ready = s.norm_sems
    numbers_ready, used = s.pair_sems
    def scores(pe, a):
        for c in range(2 * PEER_H):
            mm = pe.matmul(score(a, c), q[:, c, a * P:(a + 1) * P], keys[:, c, :], start=True, stop=True)
        mm.then_inc(sc_ready.sem, 1)

    def best(dve, step, values, numbers, src, spare):
        step(dve.max(values[:, 0:8], src))
        dve.max_index(numbers[:, 0:8], values[:, 0:8], src)
        step(dve.match_replace(spare, values[:, 0:8], src, -3.0e38))
        step(dve.max(values[:, 8:16], spare))
        step(dve.max_index(numbers[:, 8:16], values[:, 8:16], spare))

    def choose_head(dve, step, a, h):
        for c in (2 * h, 2 * h + 1):
            best(dve, step, val[:, c, :], ind[:, c, :], score(a, c), rest[:, 0:NKEYS])
        step(dve.tensor_tensor(cand.rearrange("p (i j) -> p i j", i=PEER_K),
                               val[:, 2 * h, :].unsqueeze(2).broadcast_to([P, PEER_K, PEER_K]),
                               val[:, 2 * h + 1, :].unsqueeze(1).broadcast_to([P, PEER_K, PEER_K]), ALU.add))
        best(dve, step, top[a % 2][:, h, :], pos[:, h * PEER_K:(h + 1) * PEER_K], cand, rest)

    def numbers(dve, step, a):
        t = top[a % 2]
        dve.tensor_copy(biggest, t[:, :, 0]).then_inc(sorted_.sem, 1)
        step(dve.tensor_copy(indf, ind))
        step(dve.tensor_copy(posf, pos))
        step(dve.tensor_scalar(row, posf, 1.0 / PEER_K, -7.5 / PEER_K, ALU.mult, ALU.add))
        step(dve.tensor_scalar(row, row, ROUND, ROUND, ALU.add, ALU.subtract))
        step(dve.scalar_tensor_tensor(column, row, -float(PEER_K), posf, ALU.mult, ALU.add))
        for half, (digit, found) in enumerate(((row, number), (column, second_number))):
            step(dve.tensor_tensor(match.rearrange("p h k i -> p (h k) i"),
                                   iota.unsqueeze(1).broadcast_to([P, SLOTS, PEER_K]),
                                   digit.unsqueeze(2).broadcast_to([P, SLOTS, PEER_K]), ALU.is_equal))
            keys_of = indf.rearrange("p (h two) k -> p h two k", two=2)[:, :, half, :]
            step(dve.tensor_tensor(match, match, keys_of.unsqueeze(2).broadcast_to([P, PEER_H, PEER_K, PEER_K]), ALU.mult))
            step(dve.tensor_reduce(found, match.rearrange("p h k i -> p (h k) i"), AX.X, ALU.add))
        step(dve.scalar_tensor_tensor(number, number, float(NKEYS), second_number, ALU.mult, ALU.add))
        dve.tensor_copy(of_tile(s.expert, a), number).then_inc(chosen.sem, 1)
        dve.wait_ge(sorted_.sem, sorted_.at(a + 1))
        dve.tensor_tensor(t, t, biggest.unsqueeze(2).broadcast_to([P, PEER_H, PEER_K]), ALU.subtract).then_inc(shifted.sem, 1)

    def load_keys(sync):
        sync.dma_start(keys.rearrange("p c n -> p (c n)"), s.I["keys"]).then_inc(s.loaded.sem, 16)
        sync.dma_start(iota, s.I["iota"]).then_inc(s.loaded.sem, 16)

    def first_scores(pe):
        pe.wait_ge(s.loaded.sem, s.loaded.at(32))
        scores(pe, 0)

    def first_choice(dve):
        step = Chain(dve, s.dve_chain)
        dve.wait_ge(s.loaded.sem, s.loaded.at(32))
        dve.wait_ge(sc_ready.sem, sc_ready.at(1))
        for h in range(PEER_H):
            choose_head(dve, step, 0, h)
        numbers(dve, step, 0)

    slots = s.arena[:, 36 * T:52 * T].rearrange("p (j n) -> p j n", j=BANKS)
    modulation(s, slots, s.arena[0:1, 52 * T:52 * T + 6 * D], load_keys, first_scores, first_choice)
    with s.nc.Block() as block:
        @block.tensor
        def _(pe):
            for a in range(1, TT):
                if a >= 2:
                    pe.wait_ge(sorted_.sem, sorted_.at(a - 1))
                scores(pe, a)

        @block.scalar
        def _(act):
            def place_numbers(phase, turn, half):
                a = PHASES[phase][1]
                act.activation(place[:, half * GATHER:(half + 1) * GATHER],
                               s.expert[:, bass.ds(a * SLOTS + turn * ROWS + half * GATHER, GATHER)], ACT.Copy).then_inc(numbers_ready.sem, 1)

            def places_free(phase, turn, half):
                for j in range(half * GATHER, (half + 1) * GATHER):
                    act.wait_ge(s.gathered[j].sem, s.gathered[j].at(16 * (phase * TURNS + turn)))
                act.sem_inc(s.held, 1)

            def exp_top(a):
                act.wait_ge(shifted.sem, shifted.at(a + 1))
                act.activation(flat(top[a % 2]), flat(top[a % 2]), ACT.Exp).then_inc(exp_ready.sem, 1)

            for phase, (table, a) in enumerate(PHASES):
                act.wait_ge(chosen.sem, chosen.at(a + 1))
                for half in range(2):
                    if phase:
                        places_free(phase, 0, half)
                    place_numbers(phase, 0, half)
                if phase == 0:
                    exp_top(0)
                elif table == "u":
                    exp_top(a)
                if phase and PHASES[phase - 1][0] == "u":
                    b = PHASES[phase - 1][1]
                    act.wait_ge(used.sem, used.at(phase * SLOTS))
                    act.activation(of_tile(act_, b), of_tile(act_, b), ACT.Gelu_apprx_tanh).then_inc(gelu_ready.sem, 1)
                with act.Fori(1, TURNS) as turn:
                    for half in range(2):
                        places_free(phase, turn, half)
                        place_numbers(phase, turn, half)

        @block.gpsimd
        def _(pool):
            def gather(phase, turn, j):
                if j % GATHER == 0:
                    pool.wait_ge(numbers_ready.sem, numbers_ready.at(2 * (phase * TURNS + turn) + j // GATHER + 1))
                if phase or not isinstance(turn, int):
                    pool.wait_ge(used.sem, used.at(ROWS * (phase * TURNS + turn) - ROWS + j + 1))
                    pool.sem_inc(s.held, 1)
                pool.indirect_dma_start(out=s.rows[:, j, :], out_offset=None, in_=s.I["expert_" + PHASES[phase][0]],
                                        in_offset=bass.IndirectOffsetOnAxis(ap=place[:, j:j + 1], axis=0)).then_inc(s.gathered[j].sem, 16)

            for phase in range(len(PHASES)):
                for j in range(ROWS):
                    gather(phase, 0, j)
                with pool.Fori(1, TURNS) as turn:
                    for j in range(ROWS):
                        gather(phase, turn, j)

        @block.vector
        def _(dve):
            step = Chain(dve, s.dve_chain)

            def weights(a):
                dve.wait_ge(exp_ready.sem, exp_ready.at(a + 1))
                t = top[a % 2]
                step(dve.tensor_reduce(total, t, AX.X, ALU.add))
                step(dve.reciprocal(total, total))
                step(dve.tensor_tensor(of_tile(s.gate, a).rearrange("p (h k) -> p h k", k=PEER_K), t,
                                       total.unsqueeze(2).broadcast_to([P, PEER_H, PEER_K]), ALU.mult))

            def use(phase, turn):
                table, a = PHASES[phase]
                for j in range(ROWS):
                    slot, n = turn * ROWS + j, phase * TURNS + turn
                    row = s.rows[:, j, :]
                    dve.wait_ge(s.gathered[j].sem, s.gathered[j].at((n + 1) * 16))
                    if table == "u":
                        ins = dve.scalar_tensor_tensor(row, row, 1.0, n_tok[:, a, :], ALU.mult, ALU.mult,
                                                       accum_out=act_[:, bass.ds(a * SLOTS + slot, 1)])
                    else:
                        dve.wait_ge(used.sem, used.at(n * ROWS + j - 1))
                        total = (y, n_tok)[j % 2][:, a, :]
                        ins = dve.scalar_tensor_tensor(total, row, s.gate[:, bass.ds(a * SLOTS + slot, 1)], total, ALU.mult, ALU.add)
                    ins.then_inc(used.sem, 1)

            for phase, (table, a) in enumerate(PHASES):
                if (phase == 1) if a == 0 else (table == "u"):
                    weights(a)
                if table == "v":
                    dve.wait_ge(gelu_ready.sem, gelu_ready.at(a + 1))
                    step(dve.tensor_tensor(of_tile(s.gate, a), of_tile(s.gate, a), of_tile(act_, a), ALU.mult))
                    step(dve.memset(y[:, a, :], 0.0))
                    step(dve.memset(n_tok[:, a, :], 0.0))
                between = CHOICE[table == "v"] if a + 1 < TT else {}
                if between and table == "u":
                    dve.wait_ge(sc_ready.sem, sc_ready.at(a + 2))
                starts = sorted({0, *between})
                for start, end in zip(starts, starts[1:] + [TURNS]):
                    if start in between and between[start] is not None:
                        choose_head(dve, step, a + 1, between[start])
                    elif start in between:
                        numbers(dve, step, a + 1)
                    with dve.Fori(start, end) as turn:
                        use(phase, turn)
                if table == "v":
                    dve.wait_ge(used.sem, used.at((phase + 1) * SLOTS))
                    step(dve.tensor_tensor(y[:, a, :], y[:, a, :], n_tok[:, a, :], ALU.add))
    s.loaded.passed(32)
    for c in s.norm_sems:
        c.passed(TT)
    numbers_ready.passed(2 * TURNS * len(PHASES))
    used.passed(SLOTS * len(PHASES))
    for c in s.gathered:
        c.passed(16 * TURNS * len(PHASES))


def peer(s):
    v = s.view
    n, q = v(0, 8), v(8, 16)
    tokens = lambda o: v(o, 8).rearrange("p a t -> p (a t)").rearrange("p (a c) -> p a c", a=TT)
    n_tok, y = tokens(28), s.expert_sums.rearrange("p (a c) -> p a c", a=TT)
    s.rows = v(36, 32).rearrange("p a t -> p (a t)").rearrange("p (j d) -> p j d", d=D)
    s.expert, s.gate = s.arena[:, 70 * T:71 * T].bitcast(U32), s.arena[:, 71 * T:72 * T]
    keys = s.arena[:, 24 * T:28 * T].rearrange("p (c n) -> p c n", n=NKEYS)
    norm(s, s.x, 8, 8, n, v(8, 10), False, 1, s.col("norm_ffn"), ahead=True)
    linears(s, [part("w2_q", Split(lambda k: n[:, k, :], DT, s.rounded(24), s.rounded(32)), store(lambda t: q[:, t, :]))])
    turn_tiles(s, n, n_tok)
    experts(s, q, n_tok, y, keys, s.arena[:, 0:8 * T])

    ready, taken = s.pair_sems
    with s.nc.Block() as block:
        @block.tensor
        def _(pe):
            for k in range(DT):
                if k >= 2:
                    pe.wait_ge(taken.sem, taken.at(k - 1))
                for a in range(TT):
                    mm = pe.transpose(s.ps[k % 2][:, a * P:(a + 1) * P], y[:, a, k * P:(k + 1) * P], s.eye)
                mm.then_inc(ready.sem, 1)

        @block.vector
        def _(dve):
            for k in range(DT):
                dve.wait_ge(ready.sem, ready.at(k + 1))
                dve.tensor_tensor(s.x[:, k, :], s.x[:, k, :], s.ps[k % 2][:], ALU.add).then_inc(taken.sem, 1)
    ready.passed(DT)
    taken.passed(DT)
    norm(s, s.x, 8, 8, s.x, v(10, 10), False, 1, s.col("norm_final"))


def modulation(s, slots, row, first_loads, first_scores, first_choice):
    mod = s.small[:, 64:64 + 6 * DT]
    cond = s.small[:, 120:120 + DT]
    silu_ready, turned, done, taken = s.mod_sems
    weights = s.I["w3_ada"]
    slabs, width = weights.shape[0], 6 * D // weights.shape[0]
    turns, tiles = slabs // BANKS, 6 * DT
    s.shift1, s.gain1, s.gate1, s.shift2, s.gain2, s.gate2 = (mod[:, k * DT:(k + 1) * DT] for k in range(6))

    def each_turn(eng, body):
        for j in range(BANKS):
            body(0, j)
        with eng.Fori(1, turns) as turn:
            for j in range(BANKS):
                body(turn, j)

    with s.nc.Block() as block:
        @block.sync
        def _(sync):
            def load(turn, j):
                if not isinstance(turn, int):
                    sync.wait_ge(done.sem, done.at(turn * BANKS - BANKS + j + 1))
                sync.dma_start(slots[:, j, :], weights[turn * BANKS + j]).then_inc(s.ada_ready[j].sem, 16)

            first_loads(sync)
            sync.dma_start(cond, s.I["c"]).then_inc(s.cond_loaded.sem, 16)
            each_turn(sync, load)

        @block.scalar
        def _(act):
            def take(turn, j):
                act.wait_ge(done.sem, done.at(turn * BANKS + j + 1))
                if not isinstance(turn, int):
                    act.sem_inc(s.held, 1)
                act.activation(row[:, bass.ds((turn * BANKS + j) * width, width)], s.ps[j][0:1, 0:width], ACT.Copy).then_inc(taken.sem, 1)

            act.wait_ge(s.cond_loaded.sem, s.cond_loaded.at(16))
            act.activation(cond, cond, ACT.Silu).then_inc(silu_ready.sem, 1)
            each_turn(act, take)

        @block.tensor
        def _(pe):
            def piece(turn, j):
                if not isinstance(turn, int):
                    pe.wait_ge(taken.sem, taken.at(turn * BANKS - BANKS + j + 1))
                pe.wait_ge(s.ada_ready[j].sem, s.ada_ready[j].at(16 * (turn + 1)))
                for k in range(DT):
                    mm = pe.matmul(s.ps[j][0:1, 0:width], cond[:, k:k + 1], slots[:, j, k * width:(k + 1) * width], start=k == 0, stop=k == DT - 1)
                mm.then_inc(done.sem, 1)

            first_scores(pe)
            pe.wait_ge(silu_ready.sem, silu_ready.at(1))
            each_turn(pe, piece)
            pe.wait_ge(taken.sem, taken.at(slabs))
            for t in range(tiles):
                mm = pe.matmul(s.ps[0][:, t:t + 1], row[:, t * P:(t + 1) * P], s.ones[0:1, 0:1], start=True, stop=True)
            mm.then_inc(turned.sem, 1)

        @block.vector
        def _(dve):
            first_choice(dve)
            step = Chain(dve, s.dve_chain)
            dve.wait_ge(turned.sem, turned.at(1))
            step(dve.tensor_tensor(mod, s.ps[0][:, 0:tiles], s.col("b_ada"), ALU.add))
            dve.scalar_tensor_tensor(s.gain1, s.gain1, 1.0, s.col("g_norm1"), ALU.add, ALU.mult)
            dve.scalar_tensor_tensor(s.gain2, s.gain2, 1.0, s.col("g_norm2"), ALU.add, ALU.mult)
    s.cond_loaded.passed(16)
    for c in s.ada_ready:
        c.passed(16 * turns)
    for c, n in zip(s.mod_sems, (1, 1, slabs, slabs)):
        c.passed(n)


def third_projection(s):
    v = s.view
    s.h = v(0, 8)
    norm(s, s.x, 8, 8, s.h, v(8, 10), False, 1, s.gain1, s.shift1, ahead=True)
    s.gu, s.gv, s.mv, s.mo, s.nq, s.kvc, s.ksw = v(8, 4), v(12, 4), v(25, 4), v(29, 4), v(35, 4), v(39, 2), v(41, 4)
    s.mqk = s.arena[:, 16 * T:16 * T + 8 * (T + 3)].rearrange("p (a t) -> p a t", a=8)

    s.vsw = s.arena[:, 45 * T:47 * T].rearrange("p (a c) -> p a c", a=TT)
    s.mi, s.mf, s.ng = s.arena[0:4, 33 * T:34 * T], s.arena[0:4, 34 * T:35 * T], s.arena[0:24, 47 * T:48 * T]
    with s.nc.Block() as block:
        @block.gpsimd
        def _(pool):
            pool.memset(s.mqk[:, :, 0:3], 0.0)
    whole = lambda k: s.h[:, k, :]
    h = Split(whole, DT, s.rounded(56), s.rounded(64))
    s.conv_qk = v(48, 8)
    taps = [s.col(f"ml_conv{k}") for k in range(4)]

    def conv(first):
        def side(dve, step, p, t, u):
            t += first
            ins = causal_conv(s, dve, step, s.conv_qk[:, t, :], lambda k: s.mqk[:, t, k:k + T], taps, bass.ds(t, 1))
            ins.then_inc(s.convolved.sem, 1)
        return side

    def store_values(act, step, t, ps):
        for k in (2 * t, 2 * t + 1):
            act.wait_ge(s.convolved.sem, s.convolved.at(k + 1))
            act.activation(s.conv_qk[:, k, :], s.conv_qk[:, k, :], ACT.Silu, bias=s.col("ml_conv_b")[:, k:k + 1])
        return act.activation(s.vsw[:, t, :], ps, ACT.Copy)


    linears(s, [
        part("w3_gu", h, store(lambda t: s.gu[:, t, :], ACT.Gelu_apprx_tanh)),
        part("w3_gv", h, store(lambda t: s.gv[:, t, :], ACT.Gelu_apprx_tanh)),
        part("w3_mqk", h, store(lambda t: s.mqk[:, t, 3:3 + T])),
        part("w3_mv", h, store_by_token(s.mv, TT), tokens=TT),
        part("w3_mo", h, store(lambda t: s.mo[:, t, :], ACT.Sigmoid), side=conv(0), side_after="w3_mqk"),
        part("w3_mi", whole, store(lambda t: s.mi, ACT.Identity, lambda t: s.col("ml_bi")[0:4, :]), tile=4),
        part("w3_mf", whole, store(lambda t: s.mf, ACT.Identity, lambda t: s.col("ml_bf")[0:4, :]), tile=4),
        part("w3_nq", h, store(lambda t: s.nq[:, t, :], scale=NSA_DH ** -0.5), side=conv(4)),
        part("w3_kvc", h, store(lambda t: s.kvc[:, t, :])),
        part("w3_ksw", h, store(lambda t: s.ksw[:, t, :])),
        part("w3_vsw", h, store_values, tokens=TT),
        part("w3_ng", whole, store(lambda t: s.ng, ACT.Sigmoid), tile=24),
    ])
    s.convolved.passed(8)


def spatial_gating(s):
    v = s.view
    norm(s, s.gv, 4, 4, s.gv, v(56, 6), True, 1, s.col("gm_ln_g"), s.col("gm_ln_b"))
    by_token = v(56, 4)
    w = s.arena[:, 60 * T:61 * T].rearrange("p (g t) -> p g t", g=4)
    b = s.arena[:, 61 * T:62 * T].rearrange("p (g t) -> p g t", g=4)
    tmp = v(62, 4)
    turned, taken, masked, mixed, _, _ = s.norm_sems
    with s.nc.Block() as block:
        @block.sync
        def _(sync):
            sync.dma_start(w.rearrange("p g t -> p (g t)"), s.I["gm_w"]).then_inc(s.loaded.sem, 16)
            sync.dma_start(b.rearrange("p g t -> p (g t)"), s.I["gm_b"]).then_inc(s.loaded.sem, 16)

        @block.tensor
        def _(pe):
            for a in range(TT):
                for g in range(4):
                    mm = pe.transpose(s.ps[a][:, g * P:(g + 1) * P], s.gv[:, g, a * P:(a + 1) * P], s.eye)
                mm.then_inc(turned.sem, 1)
            pe.wait_ge(taken.sem, taken.at(TT))
            pe.wait_ge(masked.sem, masked.at(1))
            for g in range(4):
                for a in range(TT):
                    mm = pe.matmul(s.ps[4 + g][:, a * P:(a + 1) * P], by_token[:, a, g * P:(g + 1) * P], w[:, g, :], start=True, stop=True)
                mm.then_inc(mixed.sem, 1)

        @block.vector
        def _(dve):
            step = Chain(dve, s.dve_chain)
            dve.wait_ge(s.loaded.sem, s.loaded.at(32))
            dve.tensor_tensor(w, w, s.causal.unsqueeze(1).broadcast_to([P, 4, P]), ALU.mult).then_inc(masked.sem, 1)
            for a in range(TT):
                dve.wait_ge(turned.sem, turned.at(a + 1))
                dve.tensor_copy(by_token[:, a, :], s.ps[a][:]).then_inc(taken.sem, 1)
            for g in range(4):
                dve.wait_ge(mixed.sem, mixed.at(g + 1))
                step(dve.tensor_tensor(tmp[:, g, :].rearrange("p (a t) -> p a t", a=TT), s.ps[4 + g][:].rearrange("p (a t) -> p a t", a=TT),
                                       b[:, g, :].unsqueeze(1).broadcast_to([P, TT, P]), ALU.add))
                dve.tensor_tensor(s.gu[:, g, :], s.gu[:, g, :], tmp[:, g, :], ALU.mult)
    s.loaded.passed(32)
    for c, n in ((turned, TT), (taken, TT), (masked, 1), (mixed, 4)):
        c.passed(n)


def mlstm(s):
    v = s.view
    qk = s.conv_qk
    s.yb = v(12, 4)
    row = lambda k: s.arena[0:4, k * T:(k + 1) * T]
    lf, e, w, d, F, g, M, m = (row(56 + k) for k in range(8))
    g_col = s.small[:, 128:144].rearrange("p (a h) -> p a h", a=TT)
    att = [s.arena[:, o * T:o * T + SEG_LEN] for o in (64, 69)]
    floor, rec = ([s.arena[:, o * T:(o + 1) * T] for o in pair] for pair in ((67, 72), (68, 73)))
    softplus_rows(s, [(s.mf, lf, e, w, d, True)])
    with s.nc.Block() as block:
        @block.vector
        def _(dve):
            step = Chain(dve, s.dve_chain)
            step(dve.memset(w, 1.0))
            step(dve.tensor_tensor_scan(F, w, lf, 0.0, ALU.mult, ALU.add))
            step(dve.tensor_tensor(g, s.mi, F, ALU.subtract))
            step(dve.tensor_tensor_scan(M, w, g, 0.0, ALU.mult, ALU.max))
            step(dve.tensor_tensor(m, F, M, ALU.add))
    cols_ready = s.cols_ready
    m_ready, s_ready, exp_ready, att_ready, sums_ready, done = s.norm_sems
    diff_ready, abs_ready = s.pair_sems
    heads = 4
    with s.nc.Block() as block:
        @block.tensor
        def _(pe):
            for a in range(TT):
                mm = pe.transpose(s.ps[7][:, a * heads:(a + 1) * heads], g[:, a * P:(a + 1) * P], s.eye[0:heads, 0:heads])
            mm.then_inc(cols_ready.sem, 1)
            def scores(h):
                if h:
                    pe.wait_ge(exp_ready.sem, exp_ready.at(h))
                pick = s.eye[0:heads, h:h + 1].broadcast_to([heads, P])
                pe.matmul(s.ps[0][:], pick, M, start=True, stop=True)
                pe.matmul(s.ps[1][:], pick, m, start=True, stop=True).then_inc(m_ready.sem, 1)
                if h:
                    pe.wait_ge(att_ready.sem, att_ready.at(h))
                for a in range(TT):
                    mm = pe.matmul(s.ps[2 + a][:, 0:seg_width(a)], qk[:, heads + h, a * P:(a + 1) * P], qk[:, h, a * P:T], start=True, stop=True)
                mm.then_inc(s_ready.sem, 1)

            scores(0)
            for h in range(heads):
                if h + 1 < heads:
                    scores(h + 1)
                pe.wait_ge(att_ready.sem, att_ready.at(h + 1))
                if h:
                    pe.wait_ge(done.sem, done.at(h))
                for a in range(TT):
                    seg = att[h % 2][:, SEG[a]:SEG[a] + seg_width(a)]
                    pe.matmul(s.ps[6][:, a * P:T], s.mv[:, a, h * P:(h + 1) * P], seg, start=a == 0, stop=a == TT - 1, skip_group_check=True)
                    mm = pe.matmul(s.ps[7][:, a * P:T], s.ones, seg, start=a == 0, stop=a == TT - 1, skip_group_check=True)
                mm.then_inc(sums_ready.sem, 1)

        @block.scalar
        def _(act):
            def exps(h):
                act.wait_ge(m_ready.sem, m_ready.at(h + 1))
                if h >= 2:
                    act.wait_ge(done.sem, done.at(h - 1))
                act.activation(floor[h % 2], s.ps[1][:], ACT.Exp, scale=-1.0)
                act.wait_ge(diff_ready.sem, diff_ready.at(h + 1))
                act.activation(att[h % 2], att[h % 2], ACT.Exp, scale=-1.0).then_inc(exp_ready.sem, 1)

            exps(0)
            for h in range(heads):
                if h + 1 < heads:
                    exps(h + 1)
                act.wait_ge(sums_ready.sem, sums_ready.at(h + 1))
                if h >= 2:
                    act.wait_ge(done.sem, done.at(h - 1))
                act.activation(rec[h % 2], s.ps[7][:], ACT.Abs).then_inc(abs_ready.sem, 1)

        @block.vector
        def _(dve):
            step = Chain(dve, s.dve_chain)

            def differences(h):
                dve.wait_ge(m_ready.sem, m_ready.at(h + 1))
                if h >= 2:
                    dve.wait_ge(sums_ready.sem, sums_ready.at(h - 1))
                for a in range(TT):
                    ins = dve.tensor_scalar(att[h % 2][:, SEG[a]:SEG[a] + seg_width(a)], s.ps[0][:, a * P:T], g_col[:, a, h:h + 1], 0.0, ALU.subtract, ALU.max)
                ins.then_inc(diff_ready.sem, 1)

            dve.wait_ge(cols_ready.sem, cols_ready.at(1))
            step(dve.tensor_copy(g_col.rearrange("p a h -> p (a h)"), s.ps[7][:, 0:TT * heads]))
            def scored(h):
                dve.wait_ge(exp_ready.sem, exp_ready.at(h + 1))
                dve.wait_ge(s_ready.sem, s_ready.at(h + 1))
                for a in range(TT):
                    seg = att[h % 2][:, SEG[a]:SEG[a] + seg_width(a)]
                    ins = dve.scalar_tensor_tensor(seg, s.ps[2 + a][:, 0:seg_width(a)], P ** -0.5, seg, ALU.mult, ALU.mult)
                step(ins)
                for a in range(TT):
                    seg = att[h % 2][:, SEG[a]:SEG[a] + P]
                    ins = dve.tensor_tensor(seg, seg, s.causal, ALU.mult)
                ins.then_inc(att_ready.sem, 1)

            differences(0)
            scored(0)
            for h in range(heads):
                if h + 1 < heads:
                    differences(h + 1)
                    scored(h + 1)
                dve.wait_ge(abs_ready.sem, abs_ready.at(h + 1))
                step(dve.tensor_tensor(rec[h % 2], rec[h % 2], floor[h % 2], ALU.max))
                step(dve.reciprocal(rec[h % 2], rec[h % 2]))
                dve.tensor_tensor(s.yb[:, h, :], s.ps[6][:], rec[h % 2], ALU.mult).then_inc(done.sem, 1)
    cols_ready.passed(1)
    for c in s.norm_sems + s.pair_sems:
        c.passed(heads)
    norm_heads(s, s.yb, 4, s.yb, v(56, 3), 1, s.col("ml_norm"), None, s.mo)


def compress(s):
    blocks = [s.arena[:, (48 + 2 * k) * T:(48 + 2 * k) * T + CMP_BLOCK * N_CMP].rearrange("p (i n) -> p i n", i=CMP_BLOCK) for k in range(2)]
    phi1 = [s.arena[:, (52 + 4 * k) * T:(56 + 4 * k) * T].rearrange("p (i e) -> p i e", i=CMP_BLOCK) for k in range(2)]
    phi_k2, phi_v2 = s.arena[0:64, 60 * T:60 * T + 128], s.arena[0:64, 60 * T + 128:60 * T + 192]
    hidden = s.arena[0:64, 61 * T:61 * T + 4 * N_CMP].rearrange("p (c n) -> p c n", c=4)
    s.k_cmp = s.arena[:, 62 * T:62 * T + 2 * N_CMP].rearrange("p (g n) -> p g n", g=2)
    s.v_cmp = s.arena[0:N_CMP, 63 * T:63 * T + 128].rearrange("p (g e) -> p g e", g=2)
    blocks_ready, summed, hidden_ready, second_ready, _, _ = s.norm_sems
    with s.nc.Block() as block:
        @block.sync
        def _(sync):
            for dst, src in ((phi1[0].rearrange("p i e -> p (i e)"), "phi_k1"), (phi1[1].rearrange("p i e -> p (i e)"), "phi_v1"),
                             (phi_k2, "phi_k2"), (phi_v2, "phi_v2")):
                sync.dma_start(dst, s.I[src]).then_inc(s.loaded.sem, 16)

        @block.vector
        def _(dve):
            for k, pe_name in enumerate(("pe_k", "pe_v")):
                tokens = s.kvc[:, k, :].rearrange("p (m l) -> p l m", l=CMP_STRIDE)
                for hi in range(2):
                    part_ = slice(hi * CMP_STRIDE, (hi + 1) * CMP_STRIDE)
                    ins = dve.tensor_tensor(blocks[k][:, part_, :], tokens[:, :, hi:hi + N_CMP],
                                            s.col(pe_name)[:, part_].unsqueeze(2).broadcast_to([P, CMP_STRIDE, N_CMP]), ALU.add)
            ins.then_inc(blocks_ready.sem, 1)
            dve.wait_ge(second_ready.sem, second_ready.at(1))
            for g in range(2):
                dve.tensor_copy(s.k_cmp[:, g, :], s.ps[4 + g][:, 0:N_CMP])
                dve.tensor_copy(s.v_cmp[:, g, :], s.ps[6 + g][0:N_CMP, 0:64])

        @block.tensor
        def _(pe):
            pe.wait_ge(s.loaded.sem, s.loaded.at(64))
            pe.wait_ge(blocks_ready.sem, blocks_ready.at(1))
            for k in range(2):
                for g in range(2):
                    lo = g * 64
                    for i in range(CMP_BLOCK):
                        mm = pe.matmul(s.ps[2 * k + g][0:64, 0:N_CMP], phi1[k][lo:lo + 64, i, :], blocks[k][lo:lo + 64, i, :],
                                       start=i == 0, stop=i == CMP_BLOCK - 1)
            mm.then_inc(summed.sem, 1)
            pe.wait_ge(hidden_ready.sem, hidden_ready.at(1))
            for g in range(2):
                pe.matmul(s.ps[4 + g][:, 0:N_CMP], phi_k2, hidden[:, g, :], start=True, stop=True)
                mm = pe.matmul(s.ps[6 + g][0:N_CMP, 0:64], hidden[:, 2 + g, :], phi_v2, start=True, stop=True)
            mm.then_inc(second_ready.sem, 1)

        @block.scalar
        def _(act):
            act.wait_ge(summed.sem, summed.at(1))
            for c in range(4):
                ins = act.activation(hidden[:, c, :], s.ps[c][0:64, 0:N_CMP], ACT.Gelu_apprx_tanh)
            ins.then_inc(hidden_ready.sem, 1)
    s.loaded.passed(64)
    for c in (blocks_ready, summed, hidden_ready, second_ready):
        c.passed(1)


def sparse_attention(s):
    v = s.view
    compress(s)
    o = v(16, 12)
    s.prob = [s.arena[:, (64 + k) * T:(65 + k) * T] for k in range(PROBS)]
    s.pt = [v(48 + 4 * k, 4) for k in range(2)]
    alibi = s.arena[:, 56 * T:57 * T]
    dist, ok = (s.arena[:, (57 + k) * T:(57 + k) * T + TT * N_CMP].rearrange("p (a n) -> p a n", a=TT) for k in range(2))
    sel = s.arena[0:24, 59 * T:62 * T].rearrange("p (c q) -> p c q", q=P)
    with s.nc.Block() as block:
        @block.sync
        def _(sync):
            for dst, src in ((alibi, "alibi"), (dist.rearrange("p a n -> p (a n)"), "cmp_dist"), (ok.rearrange("p a n -> p (a n)"), "cmp_ok"),
                             (sel.rearrange("p c q -> p (c q)"), "gate_sel")):
                sync.dma_start(dst, s.I[src]).then_inc(s.loaded.sem, 16)
            sync.wait_ge(s.loaded.sem, s.loaded.at(64))
    s.loaded.passed(64)

    def unit(h, branch):
        lo, g = (h % 2) * 64, h // 4
        common = dict(q=lambda a: [s.nq[lo:lo + 64, h // 2, a * P:(a + 1) * P]], slope=2.0 ** -(h + 1.0), scale=1.0, pieces=1, channels=64,
                      row=lo, out=lambda m: o[lo:lo + 64, branch * 4 + h // 2, :])
        if branch == 0:
            return attention_unit(k=[s.k_cmp[lo:lo + 64, g, :]], keys=lambda a: N_CMP, table=lambda a: dist[:, a, :], ok=lambda a: ok[:, a, :],
                                   v=lambda st, m: s.v_cmp[:, g, :], causal=False, **common)
        return attention_unit(k=[s.ksw[lo:lo + 64, 2 * (branch - 1) + g, :]], keys=lambda a: (a + 1) * P,
                               table=lambda a: alibi[:, (TT - 1 - a) * P:T], ok=None,
                               v=lambda st, m: s.vsw[:, st, (branch - 1) * P + g * 64:(branch - 1) * P + g * 64 + 64], causal=True, **common)

    attention(s, [unit(h, b) for h in range(NSA_H) for b in range(3)])
    gate_ready, used = s.pair_sems
    s.yc = v(16, 4)
    with s.nc.Block() as block:
        @block.tensor
        def _(pe):
            for c in range(12):
                if c >= 4:
                    pe.wait_ge(used.sem, used.at(c - 3))
                pe.matmul(s.ps[c % 4][:], sel[:, c, :], s.ng, start=True, stop=True).then_inc(gate_ready.sem, 1)

        @block.vector
        def _(dve):
            for c in range(12):
                dve.wait_ge(gate_ready.sem, gate_ready.at(c + 1))
                dve.tensor_tensor(o[:, c, :], o[:, c, :], s.ps[c % 4][:], ALU.mult).then_inc(used.sem, 1)
            step = Chain(dve, s.dve_chain)
            dve.wait_ge(used.sem, used.at(12))
            step(dve.tensor_tensor(s.yc, s.yc, o[:, 4:8, :], ALU.add))
            step(dve.tensor_tensor(s.yc, s.yc, o[:, 8:12, :], ALU.add))
    gate_ready.passed(12)
    used.passed(12)


def gated_residual(s, gate):
    def evac(dve, step, t, ps):
        return dve.scalar_tensor_tensor(s.x[:, t, :], ps, gate[:, bass.ds(t, 1)], s.x[:, t, :], ALU.mult, ALU.add)
    return evac


def third_mixer(s):
    v = s.view
    third_projection(s)
    spatial_gating(s)
    mlstm(s)
    sparse_attention(s)
    ga, gb, gc, merged = v(28, 8), v(36, 8), v(44, 8), v(52, 8)
    h = Split(lambda k: s.h[:, k, :], DT, s.rounded(60), s.rounded(0))
    linears(s, [part("w3_" + name, h, store(lambda t, dst=dst: dst[:, t, :], ACT.Sigmoid)) for name, dst in (("ga", ga), ("gb", gb), ("gc", gc))])

    def add(gate):
        def evac(dve, step, t, ps):
            step(dve.tensor_tensor(gate[:, t, :], ps, gate[:, t, :], ALU.mult))
            return dve.tensor_tensor(merged[:, t, :], merged[:, t, :], gate[:, t, :], ALU.add)
        return evac

    linears(s, [
        part("w3_up_a", Split(lambda k: s.gu[:, k, :], 4, s.rounded(60), s.rounded(8)), lambda dve, step, t, ps: dve.tensor_tensor(merged[:, t, :], ps, ga[:, t, :], ALU.mult), by="dve"),
        part("w3_up_b", Split(lambda k: s.yb[:, k, :], 4, s.rounded(64), s.rounded(12)), add(gb), by="dve", steps=1),
        part("w3_up_c", Split(lambda k: s.yc[:, k, :], 4, s.rounded(68), s.rounded(16)), add(gc), by="dve", steps=1),
    ])
    linears(s, [part("w3_out", Split(lambda k: merged[:, k, :], DT, s.rounded(0), s.rounded(52)), gated_residual(s, s.gate1), by="dve")])


def squared_relu_mlp(s):
    v = s.view
    half = FF3_TILES // 2
    h, wide = v(0, 8), v(16, half)
    norm(s, s.x, 8, 8, h, v(8, 10), False, 1, s.gain2, s.shift2, ahead=True)
    h_split = Split(lambda k: h[:, k, :], DT, s.rounded(8), s.rounded(0))

    def evac(dve, step, t, ps):
        step(dve.tensor_scalar(wide[:, t, :], ps, 0.0, None, ALU.max))
        return dve.tensor_tensor(wide[:, t, :], wide[:, t, :], wide[:, t, :], ALU.mult)

    for name in "ab":
        linears(s, [part("w3_mlp1" + name, h_split, evac, by="dve", steps=1)])
        wide_split = Split(lambda k: wide[:, k, :], half, s.rounded(32), s.rounded(16))
        linears(s, [part("w3_mlp2" + name, wide_split, gated_residual(s, s.gate2), by="dve")])
    norm(s, s.x, 8, 8, s.x, v(0, 10), False, 1, s.col("g_final"))
STAGES = [first_mixer, cross_attention, conv_glu, second_mixer, peer, third_mixer, squared_relu_mlp]


def kernel(**inputs):
    from concourse import bacc
    from concourse.bass_utils import run_bass_kernel_spmd

    nc = bacc.Bacc("TRN2", target_bir_lowering=False, num_devices=1)
    arrays, at = lay_out({k: np.asarray(v) for k, v in inputs.items()})
    aps = {k: nc.dram_tensor("in_" + k, v.shape, F32, kind="ExternalInput").ap() for k, v in arrays.items()}
    out = nc.dram_tensor("out", (P, DT * T), F32, kind="ExternalOutput").ap()
    build(nc, aps, at, out)
    r = run_bass_kernel_spmd(nc, [{"in_" + k: v for k, v in arrays.items()}], core_ids=[0])
    got = r.results[0]["out"]
    return got.reshape(P, DT, T).transpose(2, 1, 0).reshape(1, T, D)
```
